# Optimizing a Trainium2 kernel written in Bass

```python
import math
import jax, jax.numpy as jnp
from jax import lax
import numpy as np

D_MODEL = 1024
BATCH = 1
SEQ = 512
DEPTH = 2

GRID_W = 64
CTX_LEN = 256

MLA_HEADS = 8
MLA_NOPE = 64
MLA_ROPE = 32
MLA_QK = MLA_NOPE + MLA_ROPE
MLA_V = 64
MLA_Q_RANK = 768
MLA_KV_RANK = 256
MLA_WIDTH = MLA_HEADS * MLA_V
MLA_SCALE = 1.0 / math.sqrt(MLA_QK)
NA_HEADS = 4
NA_HEAD_DIM = 64
NA_WIDTH = NA_HEADS * NA_HEAD_DIM
NA_WIN_R = 8
NA_WIN_C = 16
NA_SCALE = 1.0 / math.sqrt(NA_HEAD_DIM)
POOL_WINDOWS = (2, 4, 8, 16)
POOL_GROUPS = 4
POOL_GROUP_DIM = 64
POOL_WIDTH = POOL_GROUPS * POOL_GROUP_DIM
MIX_WIDTH = MLA_WIDTH + NA_WIDTH + POOL_WIDTH
IN_COLS = MLA_Q_RANK + MLA_KV_RANK + MLA_ROPE + 3 * NA_WIDTH + POOL_WIDTH
D_FF = 2816
N_MOD = 9
ROPE_BASE = 10000.0
Q_BLOCK = 128
EPS = 1e-6

kernel_name = "hybrid_mla_natten_pool_macaron_dit"

def rms_norm(x, gain=None):
    xf = x.astype(jnp.float32)
    y = xf * lax.rsqrt(jnp.mean(xf * xf, axis=-1, keepdims=True) + EPS)
    if gain is not None:
        y = y * gain.astype(jnp.float32)
    return y.astype(x.dtype)

def modulate(h, shift, scale):
    return h * (1.0 + scale) + shift

def swiglu(h, w_gate, w_up, w_down):
    return (jax.nn.silu(h @ w_gate) * (h @ w_up)) @ w_down

def split_cols(z):
    sizes = (MLA_Q_RANK, MLA_KV_RANK, MLA_ROPE, NA_WIDTH, NA_WIDTH, NA_WIDTH, POOL_WIDTH)
    idx, acc = [], 0
    for s in sizes[:-1]:
        acc += s
        idx.append(acc)
    return jnp.split(z, idx, axis=-1)

def axial_rope_tables(n_tok):
    t = jnp.arange(n_tok, dtype=jnp.int32)
    row = (t // GRID_W).astype(jnp.float32)
    col = (t % GRID_W).astype(jnp.float32)
    axis_dim = MLA_ROPE // 2
    inv_freq = ROPE_BASE ** (-jnp.arange(0, axis_dim, 2, dtype=jnp.float32) / axis_dim)
    ar = row[:, None, None] * inv_freq
    ac = col[:, None, None] * inv_freq
    return (jnp.cos(ar), jnp.sin(ar), jnp.cos(ac), jnp.sin(ac))

def rotate(x, cos, sin):
    h = x.shape[-1] // 2
    x1, x2 = x[..., :h], x[..., h:]
    cos = cos.astype(x.dtype)
    sin = sin.astype(x.dtype)
    return jnp.concatenate([x1 * cos - x2 * sin, x1 * sin + x2 * cos], axis=-1)

def axial_rope(x, cos_r, sin_r, cos_c, sin_c):
    a = MLA_ROPE // 2
    return jnp.concatenate([rotate(x[..., :a], cos_r, sin_r), rotate(x[..., a:], cos_c, sin_c)], axis=-1)

def attend(q, k, v, scale):
    s = jnp.einsum('bqhd,bkhd->bhqk', q, k).astype(jnp.float32) * scale
    p = jax.nn.softmax(s, axis=-1).astype(v.dtype)
    return jnp.einsum('bhqk,bkhd->bqhd', p, v)

def blocked_attention(q, k, v, scale):
    B, N, H, Dk = q.shape
    nb = N // Q_BLOCK
    qb = q.reshape(B, nb, Q_BLOCK, H, Dk).transpose(1, 0, 2, 3, 4)
    out = lax.map(lambda qi: attend(qi, k, v, scale), qb)
    return out.transpose(1, 0, 2, 3, 4).reshape(B, N, H, v.shape[-1])

def mla_qkv(cq_in, ckv_in, kr_in, g_cq, w_q_up, g_ckv, w_kv_up, g_q, g_k, rope):
    B, N, _ = cq_in.shape
    q = (rms_norm(cq_in, g_cq) @ w_q_up).reshape(B, N, MLA_HEADS, MLA_QK)
    kv = (rms_norm(ckv_in, g_ckv) @ w_kv_up).reshape(B, N, MLA_HEADS, MLA_NOPE + MLA_V)
    k_nope, v = kv[..., :MLA_NOPE], kv[..., MLA_NOPE:]
    k_rope = jnp.broadcast_to(kr_in[:, :, None, :], (B, N, MLA_HEADS, MLA_ROPE))
    k = jnp.concatenate([k_nope, k_rope], axis=-1)
    q = rms_norm(q, g_q)
    k = rms_norm(k, g_k)
    if rope is not None:
        q = jnp.concatenate([q[..., :MLA_NOPE], axial_rope(q[..., MLA_NOPE:], *rope)], axis=-1)
        k = jnp.concatenate([k[..., :MLA_NOPE], axial_rope(k[..., MLA_NOPE:], *rope)], axis=-1)
    return q, k, v

def na_qkv(q_in, k_in, v_in, g_q, g_k):
    B, N, _ = q_in.shape
    shp = (B, N, NA_HEADS, NA_HEAD_DIM)
    return (rms_norm(q_in.reshape(shp), g_q), rms_norm(k_in.reshape(shp), g_k), v_in.reshape(shp))

def neighborhood_attention(q, k, v, k_ctx, v_ctx, rpb, rows):
    B, S, H, D = q.shape
    kr = min(NA_WIN_R, rows)
    kc = NA_WIN_C
    qg = q.reshape(B, rows, GRID_W, H, D)
    kg = k.reshape(B, rows, GRID_W, H, D)
    vg = v.reshape(B, rows, GRID_W, H, D)
    col = jnp.arange(GRID_W)
    col_start = jnp.clip(col - kc // 2, 0, GRID_W - kc)
    col_idx = col_start[:, None] + jnp.arange(kc)
    col_off = col_idx - col[:, None] + (NA_WIN_C - 1)

    def one_row(r):
        r0 = jnp.clip(r - kr // 2, 0, rows - kr)
        kblk = lax.dynamic_slice_in_dim(kg, r0, kr, axis=1)
        vblk = lax.dynamic_slice_in_dim(vg, r0, kr, axis=1)
        kn = kblk[:, :, col_idx]
        vn = vblk[:, :, col_idx]
        qr = lax.dynamic_index_in_dim(qg, r, axis=1, keepdims=False)
        row_off = r0 + jnp.arange(kr) - r + (NA_WIN_R - 1)
        bias = rpb[:, row_off[None, :, None], col_off[:, None, :]]
        s_loc = jnp.einsum('bwhd,brwkhd->bhwrk', qr, kn).astype(jnp.float32) * NA_SCALE
        s_loc = (s_loc + bias.astype(jnp.float32)).reshape(B, H, GRID_W, kr * kc)
        s_ctx = jnp.einsum('bwhd,bchd->bhwc', qr, k_ctx).astype(jnp.float32) * NA_SCALE
        p = jax.nn.softmax(jnp.concatenate([s_loc, s_ctx], axis=-1), axis=-1).astype(v.dtype)
        p_loc = p[..., :kr * kc].reshape(B, H, GRID_W, kr, kc)
        p_ctx = p[..., kr * kc:]
        return (jnp.einsum('bhwrk,brwkhd->bwhd', p_loc, vn)
                + jnp.einsum('bhwc,bchd->bwhd', p_ctx, v_ctx))

    out = lax.map(one_row, jnp.arange(rows))
    return out.transpose(1, 0, 2, 3, 4).reshape(B, S, H, D)

def multiscale_pool(u, w_pool, pool_scale):
    B, N, _ = u.shape
    uf = u.astype(jnp.float32)
    cs = jnp.concatenate([jnp.zeros((B, 1, POOL_WIDTH), jnp.float32), jnp.cumsum(uf, axis=1)], axis=1)
    t = jnp.arange(N)
    outs = []
    for g, w in enumerate(POOL_WINDOWS):
        lo = jnp.clip(t - w // 2, 0, N)
        hi = jnp.clip(t + w // 2, 0, N)
        seg = cs[:, :, g * POOL_GROUP_DIM:(g + 1) * POOL_GROUP_DIM]
        cnt = (hi - lo).astype(jnp.float32)[None, :, None]
        outs.append((seg[:, hi] - seg[:, lo]) / cnt - uf[..., g * POOL_GROUP_DIM:(g + 1) * POOL_GROUP_DIM])
    pooled = jnp.stack(outs, axis=2).astype(u.dtype)
    y = jnp.einsum('bngc,gcd->bngd', pooled, w_pool)
    return y.reshape(B, N, POOL_WIDTH) * pool_scale

def token_mixing(hx, hc, w_in, g_cq, w_q_up, g_ckv, w_kv_up, g_mla_q, g_mla_k,
                 g_na_q, g_na_k, na_rpb, w_pool, pool_scale, w_out, rope, rows, need_ctx):
    B, S, _ = hx.shape
    C = hc.shape[1]
    zx = split_cols(hx @ w_in)
    zc = split_cols(hc @ w_in)
    qa_x, ka_x, va_x = mla_qkv(zx[0], zx[1], zx[2], g_cq, w_q_up, g_ckv, w_kv_up, g_mla_q, g_mla_k, rope)
    qa_c, ka_c, va_c = mla_qkv(zc[0], zc[1], zc[2], g_cq, w_q_up, g_ckv, w_kv_up, g_mla_q, g_mla_k, None)
    ya_x = blocked_attention(qa_x, jnp.concatenate([ka_c, ka_x], axis=1),
                             jnp.concatenate([va_c, va_x], axis=1), MLA_SCALE).reshape(B, S, MLA_WIDTH)
    qb_x, kb_x, vb_x = na_qkv(zx[3], zx[4], zx[5], g_na_q, g_na_k)
    qb_c, kb_c, vb_c = na_qkv(zc[3], zc[4], zc[5], g_na_q, g_na_k)
    yb_x = neighborhood_attention(qb_x, kb_x, vb_x, kb_c, vb_c, na_rpb, rows).reshape(B, S, NA_WIDTH)
    yc_x = multiscale_pool(zx[6], w_pool, pool_scale)
    out_x = jnp.concatenate([ya_x, yb_x, yc_x], axis=-1) @ w_out
    if not need_ctx:
        return out_x, None
    ya_c = attend(qa_c, ka_c, va_c, MLA_SCALE).reshape(B, C, MLA_WIDTH)
    yb_c = attend(qb_c, kb_c, vb_c, NA_SCALE).reshape(B, C, NA_WIDTH)
    yc_c = multiscale_pool(zc[6], w_pool, pool_scale)
    out_c = jnp.concatenate([ya_c, yb_c, yc_c], axis=-1) @ w_out
    return out_x, out_c

def setup_inputs(seed: int = 0) -> dict:
    key = jax.random.key(seed)
    ks = jax.random.split(key, 24)
    f32 = jnp.float32
    L = DEPTH

    def nrm(k, shape, s):
        return jax.random.normal(k, shape, f32) * s

    return {
        "x": nrm(ks[0], (BATCH, SEQ, D_MODEL), 1.0),
        "c": nrm(ks[1], (BATCH, D_MODEL), 1.0),
        "ctx": nrm(ks[2], (BATCH, CTX_LEN, D_MODEL), 1.0),
        "c_ctx": nrm(ks[3], (D_MODEL,), 1.0),
        "w_mod": nrm(ks[4], (L, D_MODEL, N_MOD * D_MODEL), 0.5 * D_MODEL ** -0.5),
        "b_mod": nrm(ks[5], (L, N_MOD * D_MODEL), 0.02),
        "w_ffn_gate": nrm(ks[6], (L, 2, D_MODEL, D_FF), D_MODEL ** -0.5),
        "w_ffn_up": nrm(ks[7], (L, 2, D_MODEL, D_FF), D_MODEL ** -0.5),
        "w_ffn_down": nrm(ks[8], (L, 2, D_FF, D_MODEL), D_FF ** -0.5),
        "w_in": nrm(ks[9], (L, D_MODEL, IN_COLS), D_MODEL ** -0.5),
        "g_cq": 1.0 + nrm(ks[10], (L, MLA_Q_RANK), 0.05),
        "w_q_up": nrm(ks[11], (L, MLA_Q_RANK, MLA_HEADS * MLA_QK), MLA_Q_RANK ** -0.5),
        "g_ckv": 1.0 + nrm(ks[12], (L, MLA_KV_RANK), 0.05),
        "w_kv_up": nrm(ks[13], (L, MLA_KV_RANK, MLA_HEADS * (MLA_NOPE + MLA_V)), MLA_KV_RANK ** -0.5),
        "g_mla_q": 1.0 + nrm(ks[14], (L, MLA_QK), 0.05),
        "g_mla_k": 1.0 + nrm(ks[15], (L, MLA_QK), 0.05),
        "g_na_q": 1.0 + nrm(ks[16], (L, NA_HEAD_DIM), 0.05),
        "g_na_k": 1.0 + nrm(ks[17], (L, NA_HEAD_DIM), 0.05),
        "na_rpb": nrm(ks[18], (L, NA_HEADS, 2 * NA_WIN_R - 1, 2 * NA_WIN_C - 1), 0.1),
        "w_pool": nrm(ks[19], (L, POOL_GROUPS, POOL_GROUP_DIM, POOL_GROUP_DIM), POOL_GROUP_DIM ** -0.5),
        "pool_scale": 1.0 + nrm(ks[20], (L, POOL_WIDTH), 0.05),
        "w_out": nrm(ks[21], (L, MIX_WIDTH, D_MODEL), MIX_WIDTH ** -0.5),
    }

def reference(x, c, ctx, c_ctx, w_mod, b_mod, w_ffn_gate, w_ffn_up, w_ffn_down, w_in,
              g_cq, w_q_up, g_ckv, w_kv_up, g_mla_q, g_mla_k, g_na_q, g_na_k, na_rpb,
              w_pool, pool_scale, w_out):
    B, S, D = x.shape
    rows = S // GRID_W
    rope = axial_rope_tables(S)
    xc = ctx
    for l in range(DEPTH):
        last = l == DEPTH - 1
        mx = (jax.nn.silu(c) @ w_mod[l] + b_mod[l]).reshape(B, N_MOD, 1, D)
        mc = (jax.nn.silu(c_ctx) @ w_mod[l] + b_mod[l]).reshape(1, N_MOD, 1, D)
        x = x + 0.5 * mx[:, 2] * swiglu(modulate(rms_norm(x), mx[:, 0], mx[:, 1]),
                                        w_ffn_gate[l, 0], w_ffn_up[l, 0], w_ffn_down[l, 0])
        xc = xc + 0.5 * mc[:, 2] * swiglu(modulate(rms_norm(xc), mc[:, 0], mc[:, 1]),
                                          w_ffn_gate[l, 0], w_ffn_up[l, 0], w_ffn_down[l, 0])
        yx, yc = token_mixing(modulate(rms_norm(x), mx[:, 3], mx[:, 4]),
                              modulate(rms_norm(xc), mc[:, 3], mc[:, 4]),
                              w_in[l], g_cq[l], w_q_up[l], g_ckv[l], w_kv_up[l], g_mla_q[l], g_mla_k[l],
                              g_na_q[l], g_na_k[l], na_rpb[l], w_pool[l], pool_scale[l], w_out[l],
                              rope, rows, not last)
        x = x + mx[:, 5] * yx
        x = x + 0.5 * mx[:, 8] * swiglu(modulate(rms_norm(x), mx[:, 6], mx[:, 7]),
                                        w_ffn_gate[l, 1], w_ffn_up[l, 1], w_ffn_down[l, 1])
        if not last:
            xc = xc + mc[:, 5] * yc
            xc = xc + 0.5 * mc[:, 8] * swiglu(modulate(rms_norm(xc), mc[:, 6], mc[:, 7]),
                                              w_ffn_gate[l, 1], w_ffn_up[l, 1], w_ffn_down[l, 1])
    return x


_drawn_inputs = setup_inputs


def setup_inputs(seed=0):
    import zlib

    import numpy as np

    out = dict(_drawn_inputs(seed))
    spreads = {}
    factors = {'ctx': 3.042,
     'g_cq': 8.0,
     'g_ckv': 8.0,
     'g_mla_q': 8.0,
     'g_mla_k': 8.0,
     'g_na_q': 8.0,
     'g_na_k': 8.0,
     'na_rpb': 25.055,
     'pool_scale': 5.949}
    for name, (base, spread) in spreads.items():
        noise = np.random.default_rng([zlib.crc32(name.encode()), seed]).standard_normal(out[name].shape)
        drawn = base * np.exp(spread * noise) if base else spread * noise
        out[name] = __import__('jax').numpy.asarray(drawn.astype(out[name].dtype))
    for name, factor in factors.items():
        out[name] = (out[name] * factor).astype(out[name].dtype)
    return out
```

```python
from contextlib import ExitStack

import numpy as np

import concourse.bass as bass
from concourse import mybir

STOP = None
F32 = mybir.dt.float32
F32R = mybir.dt.float32r
ALU = mybir.AluOpType
ACT = mybir.ActivationFunctionType
AX_X = mybir.AxisListType.X

P = 128
D_MODEL = 1024
KD = D_MODEL // P
SEQ, CTX = 512, 256
TOK = SEQ + CTX
PARTS = ((0, SEQ), (SEQ, TOK))
DEPTH = 2
GRID_W = 64
MLA_HEADS, NOPE, ROPE, V_DIM = 8, 64, 32, 64
QK = NOPE + ROPE
Q_RANK, KV_RANK = 768, 256
MLA_SCALE = QK ** -0.5
NA_HEADS, NA_DIM, WIN_R, WIN_C = 4, 64, 8, 16
NA_WIDTH = NA_HEADS * NA_DIM
NA_SCALE = NA_DIM ** -0.5
POOL_G = 4
D_FF = 2816
HALF = D_FF // P // 2
N_MOD = 9
MOD_TILES = N_MOD * KD
EPS = 1e-6
NEG = -1.0e30
C_Q, C_KV, C_KR = 0, Q_RANK, Q_RANK + KV_RANK
C_QN = C_KR + ROPE
C_KN, C_VN, C_POOL = C_QN + NA_WIDTH, C_QN + 2 * NA_WIDTH, C_QN + 3 * NA_WIDTH
RPB_R, RPB_C = 2 * WIN_R - 1, 2 * WIN_C - 1
N_RPB = DEPTH * NA_HEADS * RPB_R * RPB_C
BIAS_SLOTS = RPB_R - 1
V_BMOD, V_GCQ, V_GCKV, V_PSC, V_GQ, V_GK, V_GNQ, V_GNK, V_C = 0, 72, 78, 80, 82, 83, 84, 85, 86
PAD = 8
POOLW = PAD + CTX + PAD + SEQ + PAD

MIX_ORDER = [("pool", 0), ("cq", 0), ("cq", 1), ("wpool", 0), ("pool", 1), ("cq", 2), ("cq", 3), ("wpool", 1),
             ("cq", 4), ("cq", 5), ("ckv", 0), ("ckv", 1), ("kr", 0), ("qn", 0), ("qn", 1), ("kn", 0), ("kn", 1),
             ("vn", 0), ("vn", 1)]
MIX_COL = {"pool": C_POOL, "cq": C_Q, "ckv": C_KV, "kr": C_KR, "qn": C_QN, "kn": C_KN, "vn": C_VN}
MIX_OUT, _n = {}, 0
for _kind, _c in MIX_ORDER:
    if _kind == "wpool":
        MIX_OUT["y", 2 * _c], MIX_OUT["y", 2 * _c + 1] = _n, _n + 1
        _n += 2
    else:
        MIX_OUT[_kind, _c] = _n
        _n += 1
MIX_OUT["q", 0] = _n
MIX_OUT["kv", 0], MIX_OUT["kv", 1], MIX_OUT["wo", 0] = _n + 8, _n + 14, _n + 20
T_Q = len(MIX_ORDER)
T_KV, T_WO = T_Q + MLA_HEADS, T_Q + MLA_HEADS + 2

FF_TILES = 2 * (2 * HALF + KD)
MIX_TILES = 37
MIX_OUTS = 49
WIDTHS = []
FF_T0, FF_O0, MIX_T0, MIX_O0 = [], [], [], []
N_START = SEQ // P + CTX // P + 2
_o = N_START
for _l in range(DEPTH):
    for _fi in range(2):
        FF_T0.append(len(WIDTHS))
        FF_O0.append(_o)
        WIDTHS += ([KD * P] * (2 * HALF) + [HALF * P] * KD) * 2
        _o += FF_TILES
        if _fi == 0:
            MIX_T0.append(len(WIDTHS))
            MIX_O0.append(_o)
            WIDTHS += [P if kind == "wpool" else KD * P for kind, _ in MIX_ORDER]
            WIDTHS += [Q_RANK // P * QK] * MLA_HEADS + [KV_RANK // P * 4 * P] * 2 + [KD * P] * KD
            _o += MIX_OUTS
N_TILES, O_END = {"ff0": 60, "mix0": MIX_T0[0] + MIX_TILES}.get(STOP, len(WIDTHS)), _o


class Nth:

    def __init__(self, i, stride, const):
        if isinstance(i, int):
            i, stride, const = 0, 0, i * stride + const
        self.i, self.stride, self.const = i, stride, const

    def __add__(self, k):
        return Nth(self.i, self.stride, self.const + k)

    def _at(self, stride, const):
        return self.i * stride + const if stride else const

    def n(self, plus=0):
        return self._at(self.stride, self.const + plus)

    def half(self, plus=0, times=1):
        assert self.stride % 2 == 0
        return self._at(self.stride // 2 * times, (self.const // 2 + plus) * times)

    @property
    def odd(self):
        assert self.stride % 2 == 0
        return self.const % 2


def steps(eng, a, b):
    if b - a == 1:
        yield a
    else:
        with eng.Fori(a, b) as i:
            yield i


def width(t0, stride, a, b):
    w = {WIDTHS[t0 + stride * i] if t0 + stride * i < N_TILES else 0 for i in range(a, b)}
    assert len(w) == 1
    return w.pop()


START_MOD = 2 * KD
FF_SEGS = [
    [[(0, 1, 0, START_MOD, 4), (1, 10, 0, START_MOD, 4), (10, 11, 0, START_MOD, 4)],
     [(0, 3, 0, 60, 4), (3, 10, 1, 60, 4), (10, 11, 1, 60, 4)]],
    [[(0, 1, 1, 104, 2), (1, 10, 1, 104, 2), (10, 11, 1, 104, 2)],
     [(0, 9, 1, 126, 2), (9, 10, 1, 0, 0), (10, 11, 1, 0, 0)]],
    [[(0, 1, 1, 0, 0), (1, 10, 1, 0, 0), (10, 11, 1, 0, 0)], [(0, 10, 1, 0, 0), (10, 11, 1, 0, 0)]],
    [[(0, 1, 1, 0, 0), (1, 10, 1, 0, 0), (10, 11, 1, 0, 0)], [(0, 10, 1, 0, 0), (10, 11, 1, 0, 0)]],
]


def program(nc, x, c, ctx_in, c_ctx, w_mod, b_mod, w_gate, w_up, w_down, w_in, g_cq, w_q_up, g_ckv, w_kv_up,
            g_mla_q, g_mla_k, g_na_q, g_na_k, na_rpb, w_pool, pool_scale, w_out,
            k_ident, k_perm, k_cos, k_sin, k_invcnt, out, rpb_pad, na_bias, stop):
    with ExitStack() as ctx:
        def sem(name):
            return ctx.enter_context(nc.semaphore(name))

        base = (nc.sbuf_base + 63) // 64 * 64
        place = {}

        def sb(name, shape, dt, at=None, off=0):
            nonlocal base
            size = int(np.prod(shape[1:])) * 4
            if at is None:
                start, base = base, base + (size + 31) // 32 * 32
            else:
                start = place[at][0] + off
                assert off + size <= place[at][1] + 0, (name, off, size, place[at])
            place[name] = (start, size)
            return nc.alloc_sbuf_tensor_at(name, shape, dt, offset=start)

        xT = sb("xT", [P, KD, TOK], F32)
        sb("wring", [P, 6 * HALF * P], F32)
        slot_bytes = 2 * HALF * P * 4
        w_raw = sb("w_raw", [P, 2, HALF * P], F32, "wring", 0)
        w_hi = sb("w_hi", [P, 2, HALF * P], F32R, "wring", slot_bytes)
        w_lo = sb("w_lo", [P, 2, HALF * P], F32R, "wring", 2 * slot_bytes)
        sb("harea", [P, 2 * KD * TOK], F32)
        h_hi = sb("h_hi", [P, KD, TOK], F32R, "harea", 0)
        h_lo = sb("h_lo", [P, KD, TOK], F32R, "harea", KD * TOK * 4)
        x_rows = sb("x_rows", [P, TOK // P, D_MODEL], F32, "harea", 0)
        out_rows = sb("out_rows", [P, 2, D_MODEL], F32, "harea", 0)
        sb("sarea", [P, 2 * HALF * TOK], F32)
        s_hi = sb("s_hi", [P, HALF, TOK], F32R, "sarea", 0)
        s_lo = sb("s_lo", [P, HALF, TOK], F32R, "sarea", HALF * TOK * 4)
        sb("scratch", [P, 4 * TOK], F32)
        sq = sb("sq", [P, 2, TOK], F32, "scratch", 0)
        hf = sb("hf", [P, 2, TOK], F32, "scratch", 2 * TOK * 4)
        sg = sb("sg", [P, TOK], F32, "scratch", 0)
        sf = sb("sf", [P, TOK], F32, "scratch", 2 * TOK * 4)
        q_f = sb("q_f", [P, MLA_HEADS, TOK], F32, "harea", 0)
        k_f = sb("k_f", [P, MLA_HEADS, TOK], F32, "harea", KD * TOK * 4)
        RQ, RK = Q_RANK // P, KV_RANK // P
        cq_hi = sb("cq_hi", [P, RQ, TOK], F32R, "sarea", 0)
        cq_f = sb("cq_f", [P, RQ, TOK], F32, "sarea", RQ * TOK * 4)
        cq_lo = sb("cq_lo", [P, RQ, TOK], F32R, "sarea", RQ * TOK * 4)
        ck_at = 2 * RQ * TOK * 4
        ck_hi = sb("ck_hi", [P, RK, TOK], F32R, "sarea", ck_at)
        ck_f = sb("ck_f", [P, RK, TOK], F32, "sarea", ck_at + RK * TOK * 4)
        ck_lo = sb("ck_lo", [P, RK, TOK], F32R, "sarea", ck_at + RK * TOK * 4)
        na_at = ck_at + 2 * RK * TOK * 4
        na_f = sb("na_f", [P, 4, TOK], F32, "sarea", na_at)
        vn_f = sb("vn_f", [P, TOK // P, NA_WIDTH], F32, "sarea", na_at + 4 * TOK * 4)
        y_f = sb("y_f", [P, 6, TOK], F32, "sarea", 0)
        v_f = sb("v_f", [P, TOK // P, MLA_HEADS * V_DIM], F32, "sarea", 6 * TOK * 4)
        pu = sb("pu", [P, POOLW], F32, "sarea", na_at)
        pool_lo = sb("pool_lo", [P, TOK], F32R, "sarea", na_at)
        ps = [sb(f"ps{i}", [P, POOLW], F32, "sarea", na_at + (i + 1) * POOLW * 4) for i in range(2)]
        inv_cnt = sb("inv_cnt", [P, POOLW], F32, "sarea", na_at + 3 * POOLW * 4)
        pool_hi = sb("pool_hi", [P, TOK], F32R, "sarea", na_at + 4 * POOLW * 4)
        qs_hi, qs_lo, ks_hi, ks_lo = (sb(n, [P, TOK], F32R, "wring", i * TOK * 4)
                                      for i, n in enumerate(("qs_hi", "qs_lo", "ks_hi", "ks_lo")))
        vs_hi, vs_lo = (sb(n, [P, TOK // P, P], F32R, "wring", (4 + i) * TOK * 4) for i, n in enumerate(("vs_hi", "vs_lo")))
        pt_hi, pt_lo = (sb(n, [P, TOK // P, 2 * P], F32R, "wring", (6 + 2 * i) * TOK * 4)
                        for i, n in enumerate(("pt_hi", "pt_lo")))
        na_tt = sb("na_tt", [P, 2, BIAS_SLOTS * GRID_W], F32, "scratch", 0)
        rp_row = sb("rp_row", [1, N_RPB + 2 * P], F32, "sarea", 0)
        bias_st = sb("bias_st", [P, DEPTH * NA_HEADS, BIAS_SLOTS, GRID_W], F32, "sarea", 38912)
        mod_raw = sb("mod_raw", [P, 2, KD, P], F32)
        yp_f = sb("yp_f", [P, 2, TOK], F32, "mod_raw", 0)
        sb("pbuf", [P, 2 * TOK], F32)
        acc = sb("acc", [P, TOK], F32, "pbuf", 0)
        rstd = sb("rstd", [P, TOK], F32, "pbuf", TOK * 4)
        prob = sb("prob", [P, 2, TOK], F32, "pbuf", 0)
        kr_f = sb("kr_f", [P, TOK], F32)
        rot_s = sb("rot_s", [P, SEQ], F32)
        cos = sb("cos", [P, SEQ], F32)
        sin = sb("sin", [P, SEQ], F32)
        perm = sb("perm", [P, QK], F32)
        perm_q = sb("perm_q", [P, QK], F32)
        perm_k = sb("perm_k", [P, QK], F32)
        blk = sb("blk", [P, P], F32)
        stat = sb("stat", [P, 2, 4], F32)
        ident = sb("ident", [P, P], F32)
        ones = sb("ones", [P, P], F32)
        eps = sb("eps", [P, 1], F32)
        vrows = sb("vrows", [P, DEPTH, P], F32)
        vecs = sb("vecs", [P, DEPTH, P], F32)
        vecs_half = sb("vecs_half", [P, DEPTH, P], F32)
        cs = sb("cs", [P, KD, 2], F32)
        mod = sb("mod", [P, DEPTH * MOD_TILES, 2], F32)
        mv = sb("mv", [P, 3, KD, 2], F32)

        pair = [ctx.enter_context(nc.psum_tensor(f"pair{i}", [P, 1024], F32)) for i in range(2)]
        pmid = ctx.enter_context(nc.psum_tensor("pmid", [P, 1024], F32))
        psum2 = ctx.enter_context(nc.psum_tensor("psum2", [P, 1024], F32))
        mod_ps = [pmid[:, 0:2], pmid[:, 512:514]]

        x_loaded, ctx_loaded, const_loaded = sem("x_loaded"), sem("ctx_loaded"), sem("const_loaded")
        vec_zero, vec_loaded = sem("vec_zero"), sem("vec_loaded")
        const_set, cs_ready, vec_half_ready = sem("const_set"), sem("cs_ready"), sem("vec_half_ready")
        w_loaded = [sem("w_loaded0"), sem("w_loaded1")]
        w_hi_done, w_lo_done = sem("w_hi_done"), sem("w_lo_done")
        acc_done = sem("acc_done")
        acc_free = [sem("acc_free0"), sem("acc_free1")]
        mod_loaded = [sem("mod_loaded0"), sem("mod_loaded1")]
        mod_done = sem("mod_done")
        mod_free = [sem("mod_free0"), sem("mod_free1")]
        mv_ready = sem("mv_ready")
        gate_ready = sem("gate_ready")
        n_sq, n_acc, n_sum, n_std, n_rstd = (sem(f"n_{k}") for k in ("sq", "acc", "sum", "std", "rstd"))
        n_t, n_full, n_hi, n_lo = (sem(f"n_{k}") for k in ("t", "full", "hi", "lo"))
        s_hi_done = sem("s_hi_done")
        bias_raw, bias_pad, bias_toep, bias_cut, bias_stored = (
            sem(f"bias_{k}") for k in ("raw", "pad", "toep", "cut", "stored"))
        table_loaded, blk_set, perm_ready = sem("table_loaded"), sem("blk_set"), sem("perm_ready")
        inv_loaded = sem("inv_loaded")
        pads_set, pool_step, pool_hi_done, pool_lo_done = (
            sem(n) for n in ("pads_set", "pool_step", "pool_hi_done", "pool_lo_done"))
        kr_spread, kr_sq = sem("kr_spread"), sem("kr_sq")
        h_sum, h_std, h_rstd, h_step, h_done = (sem(f"h_{k}") for k in ("sum", "std", "rstd", "step", "done"))
        w_loaded_pool = sem("w_loaded_pool")
        a_hi, a_lo = sem("a_hi"), sem("a_lo")
        a_s, a_max, a_exp, a_rsum, a_prob, a_t, a_pth, a_ptl, a_pv, a_out, a_dve = (
            sem(f"a_{k}") for k in ("s", "max", "exp", "rsum", "prob", "t", "pth", "ptl", "pv", "out", "dve"))
        tt_loaded = [sem("tt_loaded0"), sem("tt_loaded1")]
        y_hi_done, y_lo_done = sem("y_hi_done"), sem("y_lo_done")
        s_lo_done = sem("s_lo_done")
        out_staged, out_stored = sem("out_staged"), [sem("out_stored0"), sem("out_stored1")]

        def load(eng, t, src, dst):
            if not (t.stride == 0 and t.const < 2):
                eng.wait_ge(w_lo_done, t.n(-1))
            eng.dma_start(dst, src).then_inc(w_loaded[t.odd], 16)

        def split_hi(eng, t, w, done):
            if w == 0:
                return
            if done is not None:
                eng.wait_ge(acc_done, done.n(1))
            eng.wait_ge(w_loaded[t.odd], t.half(1, 16))
            eng.activation(w_hi[:, t.odd, 0:w], w_raw[:, t.odd, 0:w], ACT.Copy).then_inc(w_hi_done, 1)

        def split_lo(eng, t, w):
            if w == 0:
                return
            eng.wait_ge(w_hi_done, t.n(1))
            eng.tensor_tensor(w_lo[:, t.odd, 0:w], w_raw[:, t.odd, 0:w], w_hi[:, t.odd, 0:w].bitcast(F32),
                              ALU.subtract).then_inc(w_lo_done, 1)

        def read_out(o):
            return o.half(1)

        def product(eng, t, o, chunks, lhs, rhs, cols, before_chunk=None):
            if t is not None:
                eng.wait_ge(w_lo_done, t.n(1))
            eng.wait_ge(acc_free[o.odd], o.half())
            for k in range(chunks):
                if before_chunk:
                    before_chunk(k)
                (wh, wl), first, end = lhs(k), k == 0, k == chunks - 1
                for a, b in cols:
                    (rh, rl), dst = rhs(k, a, b), pair[o.odd][0:wh.shape[-1], a:b]
                    eng.matmul(dst, wh, rh, start=first, stop=False)
                    eng.matmul(dst, wh, rl, start=False, stop=False)
                for a, b in cols:
                    (rh, rl), dst = rhs(k, a, b), pair[o.odd][0:wh.shape[-1], a:b]
                    last = eng.matmul(dst, wl, rh, start=False, stop=end)
            last.then_inc(acc_done, 1)

        def wtile(t, per=P):
            return lambda k: (w_hi[:, t.odd, k * per:(k + 1) * per], w_lo[:, t.odd, k * per:(k + 1) * per])

        def h_moving(k, a, b):
            return h_hi[:, k, a:b], h_lo[:, k, a:b]

        norms = []

        def norm_bases(q):
            return sum(n["chunks"] for n in norms[:q]), sum(n["chunks"] - 1 for n in norms[:q])

        def norm_act(eng, q):
            n = norms[q]
            b0, a0 = norm_bases(q)
            w, ch = n["w"], n["chunks"]
            for k in range(ch):
                n["ready"](eng, k)
                if k >= 2:
                    eng.wait_ge(n_acc, a0 + max(1, k - 2))
                eng.activation(sq[:, k % 2, 0:w], n["src"](k), ACT.Square).then_inc(n_sq, 1)
            eng.wait_ge(n_sum, q + 1)
            eng.activation(sq[:, 0, 0:w], psum2[:, 0:w], ACT.Sqrt, bias=eps[:, 0:1],
                           scale=1.0 / (ch * P)).then_inc(n_std, 1)
            if n["mods"]:
                eng.wait_ge(mv_ready, n["mods"])
            for k in range(ch):
                eng.wait_ge(n_t, b0 + k + 1)
                if k >= 2:
                    eng.wait_ge(n_lo, b0 + k - 1)
                if n["shift"]:
                    for p, (a, b) in enumerate(PARTS):
                        if a < w:
                            last = eng.activation(hf[:, k % 2, a:b], sq[:, k % 2, a:b], ACT.Identity,
                                                  bias=n["shift"](k, p), scale=n["scale"](k, p))
                else:
                    last = eng.activation(hf[:, k % 2, 0:w], sq[:, k % 2, 0:w], ACT.Copy, scale=n["scale"](k, 0))
                last.then_inc(n_full, 1)
                eng.wait_ge(n_full, b0 + k + 1)
                eng.activation(n["hi"][:, k, 0:w], hf[:, k % 2, 0:w], ACT.Copy).then_inc(n_hi, 1)

        def norm_dve(eng, q):
            n = norms[q]
            b0, a0 = norm_bases(q)
            w, ch = n["w"], n["chunks"]
            for k in range(1, ch):
                eng.wait_ge(n_sq, b0 + k + 1)
                if k > 1:
                    eng.wait_ge(n_acc, a0 + k - 1)
                eng.tensor_tensor(acc[:, 0:w], sq[:, 0, 0:w] if k == 1 else acc[:, 0:w], sq[:, k % 2, 0:w],
                                  ALU.add).then_inc(n_acc, 1)
            eng.wait_ge(n_std, q + 1)
            eng.reciprocal(rstd[:, 0:w], sq[:, 0, 0:w]).then_inc(n_rstd, 1)
            eng.wait_ge(n_rstd, q + 1)
            for k in range(ch + 1):
                if k < ch:
                    if k >= 2:
                        eng.wait_ge(n_full, b0 + k - 1)
                    eng.tensor_tensor(sq[:, k % 2, 0:w], n["src"](k), rstd[:, 0:w], ALU.mult).then_inc(n_t, 1)
                if k >= 1:
                    eng.wait_ge(n_hi, b0 + k)
                    eng.tensor_tensor(n["lo"][:, k - 1, 0:w], hf[:, (k - 1) % 2, 0:w],
                                      n["hi"][:, k - 1, 0:w].bitcast(F32), ALU.subtract).then_inc(n_lo, 1)

        def norm_pe(eng, q):
            n = norms[q]
            _, a0 = norm_bases(q)
            eng.wait_ge(n_acc, a0 + n["chunks"] - 1)
            for a, b in PARTS:
                if a < n["w"]:
                    last = eng.matmul(psum2[:, a:b], ones[:, :], acc[:, a:b], start=True, stop=True)
            last.then_inc(n_sum, 1)

        def x_ready(o_first, eng_outs):
            def ready(eng, k):
                for o in eng_outs(k):
                    eng.wait_ge(acc_free[o % 2], o // 2 + 1)
            return ready

        def add_x_norm(block, w, outs, mods):
            norms.append(dict(chunks=KD, w=w, src=lambda k: xT[:, k, 0:w], ready=x_ready(0, outs), mods=mods,
                              scale=lambda k, p: mv[:, 0, k, p:p + 1], shift=lambda k, p: mv[:, 1, k, p:p + 1],
                              hi=h_hi, lo=h_lo))

        X_NORM, CQ_NORM, CK_NORM = {}, {}, {}
        mv_count = 0
        for l in range(DEPTH):
            for b in range(3):
                if (l, b) == (0, 0):
                    outs = lambda k: range(DEPTH, N_START) if k == 0 else ()
                else:
                    if b == 1:
                        o_end = FF_O0[2 * l] + FF_TILES
                    elif b == 2:
                        o_end = MIX_O0[l] + MIX_OUTS
                    else:
                        o_end = FF_O0[2 * l - 1] + FF_TILES
                    outs = (lambda o_end: lambda k: (o_end - KD + k,))(o_end)
                mv_count += 4
                X_NORM[l, b] = len(norms)
                add_x_norm((l, b), SEQ if (l, b) == (DEPTH - 1, 2) else TOK, outs, mv_count)
                if b == 1:
                    for kind, where, col, src, hi, lo, ch in (("cq", CQ_NORM, V_GCQ, cq_f, cq_hi, cq_lo, RQ),
                                                              ("ckv", CK_NORM, V_GCKV, ck_f, ck_hi, ck_lo, RK)):
                        where[l] = len(norms)
                        made = [MIX_O0[l] + MIX_OUT[kind, k] for k in range(ch)]
                        norms.append(dict(chunks=ch, w=TOK, src=lambda k, src=src: src[:, k, :], mods=0, shift=None,
                                          ready=x_ready(0, lambda k, made=made: (made[k],)),
                                          scale=lambda k, p, l=l, col=col: vecs[:, l, col + k:col + k + 1],
                                          hi=hi, lo=lo))

        def mod_vectors(eng, l, b):
            tiles = l * MOD_TILES + (3 * b + 2) * KD
            eng.wait_ge(mod_free[0], tiles // 2)
            eng.wait_ge(mod_free[1], tiles // 2)
            for which, group, add in ((0, 3 * b + 1, 1.0), (1, 3 * b, 0.0)):
                u = l * MOD_TILES + group * KD
                for j in range(2):
                    eng.scalar_tensor_tensor(mv[:, which, :, j], mod[:, u:u + KD, j], add,
                                             vecs[:, l, V_BMOD + group * KD:V_BMOD + (group + 1) * KD],
                                             ALU.add, ALU.add).then_inc(mv_ready, 1)

        def gate_vectors(eng, l, b):
            tiles = l * MOD_TILES + (3 * b + 3) * KD
            eng.wait_ge(mod_free[0], tiles // 2)
            eng.wait_ge(mod_free[1], tiles // 2)
            group, u = 3 * b + 2, l * MOD_TILES + (3 * b + 2) * KD
            bias = vecs if b == 1 else vecs_half
            for j in range(2):
                eng.scalar_tensor_tensor(mv[:, 2, :, j], mod[:, u:u + KD, j], 1.0 if b == 1 else 0.5,
                                         bias[:, l, V_BMOD + group * KD:V_BMOD + (group + 1) * KD],
                                         ALU.mult, ALU.add).then_inc(gate_ready, 1)
            eng.wait_ge(gate_ready, 2 * (3 * l + b + 1))

        def mod_load(eng, l, u):
            if not (u.stride == 0 and u.const < 2):
                eng.wait_ge(mod_done, u.n(-1))
            src = w_mod[l].rearrange("(k p) (t m) -> p k t m", p=P, m=P)[:, :, u.n(-l * MOD_TILES), :]
            eng.dma_start(mod_raw[:, u.odd, :, :], src).then_inc(mod_loaded[u.odd], 16)

        def mod_product(eng, u):
            eng.wait_ge(mod_loaded[u.odd], u.half(1, 16))
            if not (u.stride == 0 and u.const < 2):
                eng.wait_ge(mod_free[u.odd], u.half())
            for k in range(KD):
                last = eng.matmul(mod_ps[u.odd], mod_raw[:, u.odd, k, :], cs[:, k, :], start=k == 0,
                                  stop=k == KD - 1)
            last.then_inc(mod_done, 1)

        def mod_read(eng, u):
            eng.wait_ge(mod_done, u.n(1))
            eng.tensor_copy(mod[:, bass.ds(u.n(), 1), :], mod_ps[u.odd].rearrange("p (a b) -> p a b", a=1))\
               .then_inc(mod_free[u.odd], 1)

        def ff_cols(inst):
            return PARTS[:1] if inst == 3 else PARTS

        def ff_pe(eng, inst):
            cols = ff_cols(inst)
            lo0 = norm_bases(X_NORM[inst // 2, 2 * (inst % 2)])[0]
            for half in range(2):
                n0, o0 = FF_T0[inst] + 30 * half, FF_O0[inst] + 30 * half
                for a, b, _, u0, per in FF_SEGS[inst][half]:
                    for i in steps(eng, a, b):
                        for j in range(2):
                            t, o = Nth(i, 2, n0 + j), Nth(i, 2, o0 + j)
                            before = None
                            if half == 0 and (a, b) == (0, 1) and j == 0:
                                before = lambda k: eng.wait_ge(n_lo, lo0 + k + 1)
                            product(eng, t, o, KD, wtile(t), h_moving, cols, before)
                            for m in range(per // 2):
                                mod_product(eng, Nth(i, per, u0 + j * (per // 2) + m))
                for i in steps(eng, 0, KD // 2):
                    for j in range(2):
                        t, o = Nth(i, 2, n0 + 2 * HALF + j), Nth(i, 2, o0 + 2 * HALF + j)
                        if isinstance(i, int) or j == 0:
                            eng.wait_ge(s_lo_done, (2 * inst + half + 1) * HALF)
                        product(eng, t, o, HALF, wtile(t), lambda k, a, b: (s_hi[:, k, a:b], s_lo[:, k, a:b]), cols)

        def ff_up_load(eng, inst, half, i):
            l, fi = divmod(inst, 2)
            for j, w in enumerate((w_gate, w_up)):
                t = Nth(i, 2, FF_T0[inst] + 30 * half + j)
                src = w[l, fi].rearrange("(k p) (f m) -> p k f m", p=P, m=P)
                load(eng, t, src[:, :, i + half * HALF, :], w_raw[:, t.odd, 0:KD * P].rearrange("p (k m) -> p k m", m=P))

        def ff_down_load(eng, inst, half, i):
            l, fi = divmod(inst, 2)
            for j in range(2):
                t = Nth(i, 2, FF_T0[inst] + 30 * half + 2 * HALF + j)
                src = w_down[l, fi].rearrange("(f p) (d m) -> p f d m", p=P, m=P)
                load(eng, t, src[:, half * HALF:(half + 1) * HALF, i * 2 + j, :],
                     w_raw[:, t.odd, :].rearrange("p (k m) -> p k m", m=P))

        def first_loads(eng, b):
            if b is None:
                return
            if b[:2] == "ff":
                ff_up_load(eng, int(b[2]), 0, 0)
            else:
                for n in range(2):
                    mix_tile_load(eng, int(b[3]), n)

        def ff_sp(eng, inst, following):
            if inst == 1:
                eng.wait_ge(y_lo_done, KD)
            for half in range(2):
                for a, b, l, u0, per in FF_SEGS[inst][half]:
                    for i in steps(eng, a, b):
                        if b == HALF:
                            ff_down_load(eng, inst, half, 0)
                        else:
                            ff_up_load(eng, inst, half, i + 1)
                        for m in range(per):
                            mod_load(eng, l, Nth(i, per, u0 + m))
                for i in steps(eng, 1, KD // 2):
                    ff_down_load(eng, inst, half, i)
                if half == 0:
                    ff_up_load(eng, inst, 1, 0)
                else:
                    first_loads(eng, following)

        def ff_act(eng, inst):
            w = ff_cols(inst)[-1][1]
            eng.preload_act_table_set("silu_and_others")
            for half in range(2):
                n0, o0 = FF_T0[inst] + 30 * half, FF_O0[inst] + 30 * half
                s0 = (2 * inst + half) * HALF
                for a, b, _, _, _ in FF_SEGS[inst][half]:
                    for i in steps(eng, a, b):
                        t, o, s = Nth(i, 2, n0), Nth(i, 2, o0), Nth(i, 1, s0)
                        eng.wait_ge(acc_done, o.n(1))
                        eng.activation(sg[:, 0:w], pair[o.odd][:, 0:w], ACT.Silu).then_inc(acc_free[o.odd], 1)
                        split_hi(eng, t + 2, width(n0 + 2, 2, a, b), o)
                        eng.wait_ge(acc_free[(o + 1).odd], read_out(o + 1))
                        eng.activation(s_hi[:, bass.ds(i, 1), 0:w].rearrange("p a t -> p (a t)"), sf[:, 0:w],
                                       ACT.Copy).then_inc(s_hi_done, 1)
                        split_hi(eng, t + 3, width(n0 + 3, 2, a, b), o + 1)
                for a, b in ((0, 3), (3, 4)):
                    for i in steps(eng, a, b):
                        for j in range(2):
                            t, o = Nth(i, 2, n0 + 2 * HALF + j), Nth(i, 2, o0 + 2 * HALF + j)
                            split_hi(eng, t + 2, width(n0 + 2 * HALF + 2 + j, 2, a, b), o)

        def residual(eng, o, d, cols):
            eng.wait_ge(acc_done, o.n(1))
            for p, (a, b) in enumerate(cols):
                last = eng.scalar_tensor_tensor(
                    xT[:, bass.ds(d, 1), a:b].rearrange("p a t -> p (a t)"), pair[o.odd][:, a:b],
                    mv[:, 2, bass.ds(d, 1), p], xT[:, bass.ds(d, 1), a:b].rearrange("p a t -> p (a t)"),
                    ALU.mult, ALU.add)
            last.then_inc(acc_free[o.odd], 1)

        def ff_dve(eng, inst):
            cols = ff_cols(inst)
            w = cols[-1][1]
            l, fi = divmod(inst, 2)
            for half in range(2):
                n0, o0 = FF_T0[inst] + 30 * half, FF_O0[inst] + 30 * half
                s0 = (2 * inst + half) * HALF
                for a, b, _, u0, per in FF_SEGS[inst][half]:
                    for i in steps(eng, a, b):
                        t, o, s = Nth(i, 2, n0), Nth(i, 2, o0), Nth(i, 1, s0)
                        split_lo(eng, t + 2, width(n0 + 2, 2, a, b))
                        for m in range(per // 2):
                            mod_read(eng, Nth(i, per, u0 + m))
                        eng.wait_ge(acc_done, o.n(2))
                        eng.wait_ge(acc_free[o.odd], read_out(o))
                        eng.tensor_tensor(sf[:, 0:w], pair[(o + 1).odd][:, 0:w], sg[:, 0:w],
                                          ALU.mult).then_inc(acc_free[(o + 1).odd], 1)
                        for m in range(per // 2):
                            mod_read(eng, Nth(i, per, u0 + per // 2 + m))
                        eng.wait_ge(s_hi_done, s.n(1))
                        eng.tensor_tensor(s_lo[:, bass.ds(i, 1), 0:w].rearrange("p a t -> p (a t)"), sf[:, 0:w],
                                          s_hi[:, bass.ds(i, 1), 0:w].bitcast(F32).rearrange("p a t -> p (a t)"),
                                          ALU.subtract).then_inc(s_lo_done, 1)
                        split_lo(eng, t + 3, width(n0 + 3, 2, a, b))
                if half == 0:
                    gate_vectors(eng, l, 2 * fi)
                for a, b in ((0, 3), (3, 4)):
                    for i in steps(eng, a, b):
                        for j in range(2):
                            t, o = Nth(i, 2, n0 + 2 * HALF + j), Nth(i, 2, o0 + 2 * HALF + j)
                            residual(eng, o, Nth(i, 2, j).n(), cols)
                            split_lo(eng, t + 2, width(n0 + 2 * HALF + 2 + j, 2, a, b))

        def mo(l, kind, c=0):
            return Nth(0, 1, MIX_O0[l] + MIX_OUT[kind, c])

        def mix_outs(l, n):
            kind, c = MIX_ORDER[n]
            return [mo(l, "y", 2 * c), mo(l, "y", 2 * c + 1)] if kind == "wpool" else [mo(l, kind, c)]

        def mix_last_out(l, n):
            if n < T_Q:
                return mix_outs(l, n)[-1]
            if n < T_KV:
                return mo(l, "q") + (n - T_Q)
            return mo(l, "kv", n - T_KV) + 5

        H_STEPS = 4 + 2 * MLA_HEADS

        def head_step(l, what, h=0):
            return H_STEPS * l + {"na": 0, "q": 4, "k": 4 + MLA_HEADS}[what] + h

        def swapped_product(eng, t, o, chunks, stat, moving):
            eng.wait_ge(w_lo_done, t.n(1))
            eng.wait_ge(acc_free[o.odd], o.half())
            for tc in range(TOK // P):
                dst = pair[o.odd][:, tc * P:(tc + 1) * P]
                for k in range(chunks):
                    (ah, al), (wh, wl) = stat(k, tc), moving(k)
                    if len(wh.shape) == 3:
                        d = dst.rearrange("p (a b) -> p a b", a=wh.shape[1])
                    else:
                        d = dst
                    eng.matmul(d, ah, wh, start=k == 0, stop=False)
                    eng.matmul(d, ah, wl, start=False, stop=False)
                    last = eng.matmul(d, al, wh, start=False, stop=k == chunks - 1)
            last.then_inc(acc_done, 1)

        def head_sum(eng, s, squares_out, rows, ones_ap, rot=None):
            eng.wait_ge(acc_free[squares_out.odd], read_out(squares_out))
            if not (s.stride == 0 and s.const < 1):
                eng.wait_ge(h_std, s.n())
            for a, b in PARTS:
                last = eng.matmul(psum2[0:rows, a:b], ones_ap, sq[0:rows, 0, a:b], start=True, stop=True)
            if rot is not None:
                lhs, rhs = rot
                eng.wait_ge(h_done, s.n(-1))
                last = eng.matmul(pmid[0:QK, s.odd * 512:s.odd * 512 + SEQ], lhs, rhs, start=True, stop=True)
            last.then_inc(h_sum, 1)

        def head_std(eng, s, rows, dim):
            eng.wait_ge(h_sum, s.n(1))
            if not (s.stride == 0 and s.const < 1):
                eng.wait_ge(h_rstd, s.n())
            eng.activation(sq[0:rows, 1, :], psum2[0:rows, 0:TOK], ACT.Sqrt, bias=eps[0:rows, 0:1],
                           scale=1.0 / dim).then_inc(h_std, 1)

        def mix_pe(eng, l):
            t0 = MIX_T0[l]
            q = X_NORM[l, 1]
            norm_pe(eng, q)
            lo0 = norm_bases(q)[0]
            na_out = [mo(l, "qn", 0), mo(l, "qn", 1), mo(l, "kn", 0), mo(l, "kn", 1)]

            def na_sum(m):
                head_sum(eng, Nth(0, 1, head_step(l, "na", m)), na_out[m], P, blk[:, :])

            for n, (kind, c) in enumerate(MIX_ORDER):
                t, outs = Nth(0, 1, t0 + n), mix_outs(l, n)
                if kind == "wpool":
                    eng.wait_ge(pool_lo_done, 2 * l + c + 1)
                    for g in range(2):
                        r = slice(g * 64, g * 64 + 64)
                        product(eng, t, outs[g], 1, lambda k: (w_hi[r, t.odd, 0:P], w_lo[r, t.odd, 0:P]),
                                lambda k, a, b: (pool_hi[r, a:b], pool_lo[r, a:b]), PARTS)
                elif kind == "vn":
                    swapped_product(eng, t, outs[0], KD,
                                    lambda k, tc: (h_hi[:, k, tc * P:(tc + 1) * P], h_lo[:, k, tc * P:(tc + 1) * P]),
                                    wtile(t))
                else:
                    before = (lambda k: eng.wait_ge(n_lo, lo0 + k + 1)) if n == 0 else None
                    product(eng, t, outs[0], KD, wtile(t), h_moving, PARTS, before)
                if (kind, c) == ("ckv", 0):
                    norm_pe(eng, CQ_NORM[l])
                if (kind, c) == ("kr", 0):
                    norm_pe(eng, CK_NORM[l])
                if (kind, c) in (("qn", 1), ("kn", 0), ("kn", 1), ("vn", 0)):
                    na_sum({("qn", 1): 0, ("kn", 0): 1, ("kn", 1): 2, ("vn", 0): 3}[kind, c])
            for i in steps(eng, 0, MLA_HEADS // 2):
                for j in range(2):
                    t, o = Nth(i, 2, t0 + T_Q + j), Nth(i, 2, mo(l, "q").const + j)
                    product(eng, t, o, RQ, wtile(t, QK), lambda k, a, b: (cq_hi[:, k, a:b], cq_lo[:, k, a:b]), PARTS)
                for j in range(2):
                    head_sum(eng, Nth(i, 2, head_step(l, "q", j)), Nth(i, 2, mo(l, "q").const + j), QK,
                             ones[0:QK, 0:QK], (perm_q[0:QK, :], q_f[0:QK, bass.ds(i * 2 + j, 1), 0:SEQ]
                                                .rearrange("p a t -> p (a t)")))
            eng.wait_ge(kr_spread, MLA_HEADS * (l + 1))
            eng.wait_ge(kr_sq, l + 1)
            ck_moving = lambda k, a, b: (ck_hi[:, k, a:b], ck_lo[:, k, a:b])
            k_sum = lambda h: head_sum(eng, Nth(0, 1, head_step(l, "k", h)), mo(l, "kv", h // 4) + h % 4, QK,
                                       ones[0:QK, 0:QK], (perm_k[0:QK, :], k_f[0:QK, h, 0:SEQ]))
            for c in range(2):
                t = Nth(0, 1, t0 + T_KV + c)
                view = [w[:, t.odd, 0:RK * 4 * P].rearrange("p (k h m) -> p k h m", k=RK, m=P) for w in (w_hi, w_lo)]
                for h in range(4):
                    product(eng, t, mo(l, "kv", c) + h, RK, lambda k: (view[0][:, k, h, :], view[1][:, k, h, :]),
                            ck_moving, PARTS)
                    if h:
                        k_sum(4 * c + h - 1)
                for v in range(2):
                    swapped_product(eng, t, mo(l, "kv", c) + (4 + v), RK,
                                    lambda k, tc: (ck_hi[:, k, tc * P:(tc + 1) * P], ck_lo[:, k, tc * P:(tc + 1) * P]),
                                    lambda k: tuple(x[:, k, 2 * v:2 * v + 2, NOPE:] for x in view))
                    if v == 0:
                        k_sum(4 * c + 3)
            attention_pe(eng, l)
            cols = y_cols(l)
            for i0, i1 in ((0, 1), (1, KD // 2)):
                for i in steps(eng, i0, i1):
                    for j in range(2):
                        t, o = Nth(i, 2, t0 + T_WO + j), Nth(i, 2, mo(l, "wo").const + j)
                        before = (lambda k: eng.wait_ge(y_lo_done, KD * l + k + 1)) if i0 == 0 and j == 0 else None
                        product(eng, t, o, KD, wtile(t), h_moving, cols, before)

        def y_cols(l):
            return PARTS if l < DEPTH - 1 else PARTS[:1]

        def mix_tile_load(eng, l, n):
            if isinstance(n, Nth):
                t = n
                h = n.n(-(MIX_T0[l] + T_Q))
                src = w_q_up[l].rearrange("(k p) (h m) -> p k h m", p=P, m=QK)[:, :, h, :]
                load(eng, t, src, w_raw[:, t.odd, 0:RQ * QK].rearrange("p (k m) -> p k m", m=QK))
                return
            t = Nth(0, 1, MIX_T0[l] + n)
            if n >= T_KV:
                c = n - T_KV
                src = w_kv_up[l].rearrange("(k p) n -> p k n", p=P)[:, :, c * 4 * P:(c + 1) * 4 * P]
                load(eng, t, src, w_raw[:, t.odd, 0:RK * 4 * P].rearrange("p (k m) -> p k m", k=RK))
                return
            kind, c = MIX_ORDER[n]
            if kind == "wpool":
                eng.wait_ge(w_lo_done, t.n(-1))
                for half in range(2):
                    eng.dma_start(w_raw[:, t.odd, half * 64:half * 64 + 64],
                                  w_pool[l, 2 * c:2 * c + 2].rearrange("g c d -> (g c) d"))\
                       .then_inc(w_loaded_pool, 16)
                eng.wait_ge(w_loaded_pool, 32 * (2 * l + c + 1))
                eng.sem_inc(w_loaded[t.odd], 16)
                return
            col = MIX_COL[kind] + c * P
            src = w_in[l].rearrange("(k p) n -> p k n", p=P)[:, :, col:col + P]
            load(eng, t, src, w_raw[:, t.odd, 0:KD * P].rearrange("p (k m) -> p k m", m=P))

        def wo_load(eng, l, t):
            d = t.n(-(MIX_T0[l] + T_WO))
            src = w_out[l].rearrange("(k p) (d m) -> p k d m", p=P, m=P)[:, :, d, :]
            load(eng, t, src, w_raw[:, t.odd, 0:KD * P].rearrange("p (k m) -> p k m", m=P))

        def mix_sp(eng, l):
            for n in range(2, T_Q):
                if n == 2:
                    eng.wait_ge(acc_done, MIX_O0[l])
                    eng.dma_start(inv_cnt[:, :], k_invcnt[:, 0, :]).then_inc(inv_loaded, 16)
                mix_tile_load(eng, l, n)
                if MIX_ORDER[n] == ("cq", 3):
                    eng.wait_ge(pool_lo_done, 2 * l + 1)
                    eng.dma_start(inv_cnt[:, :], k_invcnt[:, 1, :]).then_inc(inv_loaded, 16)
            for i in steps(eng, 0, MLA_HEADS // 2):
                for j in range(2):
                    mix_tile_load(eng, l, Nth(i, 2, MIX_T0[l] + T_Q + j))
            for c in range(2):
                mix_tile_load(eng, l, T_KV + c)
            nb = att_chunks(l)
            eng.wait_ge(h_done, H_STEPS * (l + 1))
            eng.wait_ge(bias_stored, 16)
            for i in range(2):
                for j in range(2):
                    if i:
                        eng.wait_ge(a_max, ATT_C0[l] + 4 * nb + (nb // 2) * (j + 1))
                    eng.dma_start(na_tt[:, j, :], na_bias[l, 2 * i + j]).then_inc(tt_loaded[j], 16)
            eng.wait_ge(a_out, (ATT_C0[l] + 6 * nb) // 2)
            for i in steps(eng, 0, KD // 2):
                for j in range(2):
                    wo_load(eng, l, Nth(i, 2, MIX_T0[l] + T_WO + j))

        def evacuate(eng, o, dst, scale=None):
            eng.wait_ge(acc_done, o.n(1))
            src = pair[o.odd][:, 0:TOK]
            if len(dst.shape) == 3:
                src = src.rearrange("p (a b) -> p a b", a=dst.shape[1])
            eng.tensor_copy(dst, src).then_inc(acc_free[o.odd], 1)

        def mix_act(eng, l):
            t0 = MIX_T0[l]
            norm_act(eng, X_NORM[l, 1])
            eng.preload_act_table_set("sqrt_and_others")
            na_out = [mo(l, "qn", 0), mo(l, "qn", 1), mo(l, "kn", 0), mo(l, "kn", 1)]
            for n, (kind, c) in enumerate(MIX_ORDER):
                t, outs = Nth(0, 1, t0 + n), mix_outs(l, n)
                if kind == "wpool":
                    eng.wait_ge(pool_step, pool_steps(l, c + 1))
                    for a, b, at in ((0, SEQ, 2 * PAD + CTX), (SEQ, TOK, PAD)):
                        eng.activation(pool_hi[:, a:b], ps[0][:, at:at + b - a], ACT.Copy).then_inc(pool_hi_done, 1)
                if kind == "kr":
                    eng.wait_ge(acc_done, outs[0].n(1))
                    eng.activation(kr_f[NOPE:QK, :], pair[outs[0].odd][0:ROPE, 0:TOK], ACT.Copy)\
                       .then_inc(acc_free[outs[0].odd], 1)
                if kind in ("qn", "kn"):
                    m = c + 2 * (kind == "kn")
                    eng.wait_ge(acc_done, outs[0].n(1))
                    eng.activation(na_f[:, m, :], pair[outs[0].odd][:, 0:TOK], ACT.Copy)
                    if m:
                        head_std(eng, Nth(0, 1, head_step(l, "na", m - 1)), P, NA_DIM)
                    eng.activation(sq[:, 0, :], pair[outs[0].odd][:, 0:TOK], ACT.Square)\
                       .then_inc(acc_free[outs[0].odd], 1)
                split_hi(eng, t + 2, WIDTHS[t0 + n + 2], outs[-1])
                if (kind, c) == ("vn", 0):
                    head_std(eng, Nth(0, 1, head_step(l, "na", 3)), P, NA_DIM)
                if (kind, c) == ("cq", 5):
                    norm_act(eng, CQ_NORM[l])
                if (kind, c) == ("ckv", 1):
                    norm_act(eng, CK_NORM[l])
            for a, b in ((0, 3), (3, 4)):
                for i in steps(eng, a, b):
                    for j in range(2):
                        t, o = Nth(i, 2, t0 + T_Q + j), Nth(i, 2, mo(l, "q").const + j)
                        s = Nth(i, 2, head_step(l, "q", j))
                        eng.wait_ge(acc_done, o.n(1))
                        eng.activation(q_f[0:QK, bass.ds(i * 2 + j, 1), :].rearrange("p a t -> p (a t)"),
                                       pair[o.odd][0:QK, 0:TOK], ACT.Copy)
                        if j == 1:
                            head_std(eng, s + (-1), QK, QK)
                        eng.activation(sq[0:QK, 0, :], pair[o.odd][0:QK, 0:TOK], ACT.Square)\
                           .then_inc(acc_free[o.odd], 1)
                        split_hi(eng, t + 2, width(t0 + T_Q + j + 2, 2, a, b), o)
                    head_std(eng, s, QK, QK)
            eng.activation(sq[NOPE:QK, 0, :], kr_f[NOPE:QK, :], ACT.Square).then_inc(kr_sq, 1)
            for h in range(MLA_HEADS):
                o, s = mo(l, "kv", h // 4) + h % 4, Nth(0, 1, head_step(l, "k", h))
                eng.wait_ge(acc_done, o.n(1))
                eng.activation(k_f[0:NOPE, h, :], pair[o.odd][0:NOPE, 0:TOK], ACT.Copy)
                if h:
                    head_std(eng, s + (-1), QK, QK)
                eng.activation(sq[0:NOPE, 0, :], pair[o.odd][0:NOPE, 0:TOK], ACT.Square).then_inc(acc_free[o.odd], 1)
            head_std(eng, Nth(0, 1, head_step(l, "k", MLA_HEADS - 1)), QK, QK)
            attention_act(eng, l)
            w = y_cols(l)[-1][1]
            for n in range(2):
                split_hi(eng, Nth(0, 1, t0 + T_WO + n), KD * P, None)
            for k in range(KD):
                eng.activation(h_hi[:, k, 0:w], y_f[:, k, 0:w] if k < 6 else yp_f[:, k - 6, 0:w], ACT.Copy)\
                   .then_inc(y_hi_done, 1)
            for a, b in ((0, 3), (3, 4)):
                for i in steps(eng, a, b):
                    for j in range(2):
                        t, o = Nth(i, 2, t0 + T_WO + j), Nth(i, 2, mo(l, "wo").const + j)
                        split_hi(eng, t + 2, width(t0 + T_WO + 2 + j, 2, a, b), o)

        def head_scale(eng, s, which, h, l, first_step):
            x_f, gain = (q_f, V_GQ) if which == "q" else (k_f, V_GK)
            g = vecs[0:QK, l, gain:gain + 1]
            head = lambda a, b: x_f[0:QK, bass.ds(h, 1), a:b].rearrange("p a t -> p (a t)")
            eng.wait_ge(h_std, s.n(1))
            eng.wait_ge(h_done, s.n())
            eng.reciprocal(rstd[0:QK, :], sq[0:QK, 1, :]).then_inc(h_rstd, 1)
            eng.tensor_tensor(rot_s[0:QK, :], pmid[0:QK, s.odd * 512:s.odd * 512 + SEQ], sin[0:QK, :], ALU.mult)\
               .then_inc(h_step, 1)
            eng.scalar_tensor_tensor(head(0, SEQ), head(0, SEQ), g, cos[0:QK, :], ALU.mult, ALU.mult).then_inc(h_step, 1)
            eng.tensor_scalar(head(SEQ, TOK), head(SEQ, TOK), g, None, ALU.mult).then_inc(h_step, 1)
            eng.wait_ge(h_step, first_step.n(3))
            eng.tensor_tensor(head(0, SEQ), head(0, SEQ), rot_s[0:QK, :], ALU.add).then_inc(h_step, 1)
            eng.wait_ge(h_rstd, s.n(1))
            eng.wait_ge(h_step, first_step.n(4))
            eng.tensor_tensor(head(0, TOK), head(0, TOK), rstd[0:QK, :], ALU.mult).then_inc(h_done, 1)

        def na_scale(eng, l, m):
            s = head_step(l, "na", m)
            gain = V_GNQ if m < 2 else V_GNK
            eng.wait_ge(h_std, s + 1)
            if s:
                eng.wait_ge(h_done, s)
            eng.reciprocal(rstd[:, :], sq[:, 1, :]).then_inc(h_rstd, 1)
            eng.wait_ge(h_rstd, s + 1)
            eng.scalar_tensor_tensor(na_f[:, m, :], na_f[:, m, :], vecs[:, l, gain:gain + 1], rstd[:, :],
                                     ALU.mult, ALU.mult).then_inc(h_done, 1)

        def mix_dve(eng, l):
            t0 = MIX_T0[l]
            mod_vectors(eng, l, 1)
            for dst, gain in ((perm_q, V_GQ), (perm_k, V_GK)):
                eng.tensor_scalar(dst[0:QK, :], perm[0:QK, :], vecs[0:QK, l, gain:gain + 1], None, ALU.mult)\
                   .then_inc(perm_ready, 1)
            norm_dve(eng, X_NORM[l, 1])
            for n, (kind, c) in enumerate(MIX_ORDER):
                t, outs = Nth(0, 1, t0 + n), mix_outs(l, n)
                if kind == "pool":
                    o = outs[0]
                    eng.wait_ge(acc_done, o.n(1))
                    eng.wait_ge(pads_set, 3 * (2 * l + c + 1))
                    eng.tensor_copy(pu[:, PAD:PAD + CTX], pair[o.odd][:, SEQ:TOK])
                    eng.tensor_copy(pu[:, 2 * PAD + CTX:2 * PAD + CTX + SEQ], pair[o.odd][:, 0:SEQ])\
                       .then_inc(acc_free[o.odd], 1)
                elif kind == "wpool":
                    eng.wait_ge(pool_hi_done, 2 * (2 * l + c + 1))
                    for a, b, at in ((0, SEQ, 2 * PAD + CTX), (SEQ, TOK, PAD)):
                        last = eng.tensor_tensor(pool_lo[:, a:b], ps[0][:, at:at + b - a],
                                                 pool_hi[:, a:b].bitcast(F32), ALU.subtract)
                    last.then_inc(pool_lo_done, 1)
                    for g in range(2):
                        o, r = outs[g], slice(g * 64, g * 64 + 64)
                        eng.wait_ge(acc_done, o.n(1))
                        eng.tensor_scalar(yp_f[r, c, :], pair[o.odd][r, 0:TOK], vecs[r, l, V_PSC + c:V_PSC + c + 1],
                                          None, ALU.mult).then_inc(acc_free[o.odd], 1)
                elif kind == "cq":
                    evacuate(eng, outs[0], cq_f[:, c, :])
                elif kind == "ckv":
                    evacuate(eng, outs[0], ck_f[:, c, :])
                elif kind == "vn":
                    evacuate(eng, outs[0], vn_f[:, :, c * P:(c + 1) * P])
                split_lo(eng, t + 2, WIDTHS[t0 + n + 2])
                if (kind, c) == ("cq", 5):
                    norm_dve(eng, CQ_NORM[l])
                if (kind, c) == ("ckv", 1):
                    norm_dve(eng, CK_NORM[l])
                if (kind, c) in (("qn", 1), ("kn", 0), ("kn", 1), ("vn", 0)):
                    na_scale(eng, l, {("qn", 1): 0, ("kn", 0): 1, ("kn", 1): 2, ("vn", 0): 3}[kind, c])
            for a, b in ((0, 3), (3, 4)):
                for i in steps(eng, a, b):
                    for j in range(2):
                        split_lo(eng, Nth(i, 2, t0 + T_Q + j + 2), width(t0 + T_Q + j + 2, 2, a, b))
                    for j in range(2):
                        head_scale(eng, Nth(i, 2, head_step(l, "q", j)), "q", i * 2 + j, l,
                                   Nth(i, 8, 4 * (2 * MLA_HEADS * l + j)))
            for h in range(MLA_HEADS):
                c = h // 4
                if h % 4 == 3:
                    for v in range(2):
                        if v == 1:
                            head_scale(eng, Nth(0, 1, head_step(l, "k", h)), "k", h, l,
                                       Nth(0, 1, 4 * (2 * MLA_HEADS * l + MLA_HEADS + h)))
                        at = (2 * c + v) * P
                        evacuate(eng, mo(l, "kv", c) + (4 + v), v_f[:, :, at:at + P])
                else:
                    head_scale(eng, Nth(0, 1, head_step(l, "k", h)), "k", h, l,
                               Nth(0, 1, 4 * (2 * MLA_HEADS * l + MLA_HEADS + h)))
            attention_dve(eng, l)
            w, cols = y_cols(l)[-1][1], y_cols(l)
            for n in range(2):
                split_lo(eng, Nth(0, 1, t0 + T_WO + n), KD * P)
            for k in range(KD):
                eng.wait_ge(y_hi_done, KD * l + k + 1)
                eng.tensor_tensor(h_lo[:, k, 0:w], y_f[:, k, 0:w] if k < 6 else yp_f[:, k - 6, 0:w],
                                  h_hi[:, k, 0:w].bitcast(F32), ALU.subtract).then_inc(y_lo_done, 1)
            gate_vectors(eng, l, 1)
            for a, b in ((0, 3), (3, 4)):
                for i in steps(eng, a, b):
                    for j in range(2):
                        t, o = Nth(i, 2, t0 + T_WO + j), Nth(i, 2, mo(l, "wo").const + j)
                        residual(eng, o, Nth(i, 2, j).n(), cols)
                        split_lo(eng, t + 2, width(t0 + T_WO + 2 + j, 2, a, b))

        def pool_steps(l, chunks):
            return 12 * l + (0, 5, 12)[chunks]

        def mix_pool(eng, l):
            done = pool_steps(l, 0)
            for c in range(2):
                first = mo(l, "pool", 0).const if c == 0 else mo(l, "y", 1).const + 1
                eng.wait_ge(acc_done, first)
                if c == 1:
                    eng.wait_ge(pool_lo_done, 2 * l + 1)
                for at in (0, PAD + CTX, 2 * PAD + CTX + SEQ):
                    eng.memset(pu[:, at:at + PAD], 0.0).then_inc(pads_set, 1)
                o = mo(l, "pool", c)
                eng.wait_ge(acc_free[o.odd], read_out(o))
                eng.wait_ge(pads_set, 3 * (2 * l + c + 1))
                src, cur, lo, hi = pu, 0, 0, POOLW
                for reach in ((1, 1) if c == 0 else (1, 1, 2, 4)):
                    back, ahead = (1, 0) if src is pu else (reach, reach)
                    lo, hi = lo + back, hi - ahead
                    eng.tensor_tensor(ps[cur][:, lo:hi], src[:, lo - back:hi - back], src[:, lo + ahead:hi + ahead],
                                      ALU.add).then_inc(pool_step, 1)
                    done += 1
                    eng.wait_ge(pool_step, done)
                    src, cur = ps[cur], 1 - cur
                eng.wait_ge(inv_loaded, 16 * (2 * l + c + 1))
                a, b = PAD, POOLW - PAD
                for g in range(2):
                    r = slice(g * 64, g * 64 + 64)
                    eng.tensor_tensor(ps[0][r, a:b], ps[g][r, a:b], inv_cnt[r, a:b], ALU.mult).then_inc(pool_step, 1)
                    done += 1
                eng.wait_ge(pool_step, done)
                eng.tensor_tensor(ps[0][:, a:b], ps[0][:, a:b], pu[:, a:b], ALU.subtract).then_inc(pool_step, 1)
                done += 1
            o = mo(l, "vn", 1)
            eng.wait_ge(acc_done, o.n(1))
            eng.wait_ge(acc_free[mo(l, "kr").odd], read_out(mo(l, "kr")))
            for h in range(MLA_HEADS):
                eng.tensor_copy(k_f[NOPE:QK, h, :], kr_f[NOPE:QK, :]).then_inc(kr_spread, 1)
            attention_pool(eng, l)

        def att_chunks(l):
            return 12 if l < DEPTH - 1 else 8

        ATT_C0 = [0, 6 * 12]
        ATT_SPLITS = 26

        def bodies(eng, l):
            nb = att_chunks(l)
            for kind, count, c0, s0 in (("mla", 4, ATT_C0[l], ATT_SPLITS * l),
                                        ("na", 2, ATT_C0[l] + 4 * nb, ATT_SPLITS * l + 20)):
                for i0, i1 in ((0, 1), (1, count)):
                    for i in steps(eng, i0, i1):
                        yield kind, i, (lambda c, i=i, c0=c0: Nth(i, nb, c0 + c)), \
                            (lambda b, i=i, c0=c0: Nth(i, nb // 2, c0 // 2 + b)), \
                            (lambda n, i=i, s0=s0, per=(5 if kind == "mla" else 3): Nth(i, per, s0 + n)), \
                            (kind == "mla" and i0 == 0)

        def chunk_info(l, c):
            per = att_chunks(l) // 2
            j, q0 = c // per, (c % per) * P
            return j, q0, (PARTS if q0 < SEQ else PARTS[1:])

        def attention_splits(kind, i):
            if kind == "mla":
                h = lambda x, j: x[0:QK, bass.ds(i * 2 + j, 1), :].rearrange("p a t -> p (a t)")
                return [(0, h(q_f, 0), qs_hi[0:QK, :], qs_lo[0:QK, :]), (0, h(k_f, 0), ks_hi[0:QK, :], ks_lo[0:QK, :]),
                        (0, v_f[:, :, bass.ds(i * P, P)], vs_hi[:, :, :], vs_lo[:, :, :]),
                        (1, h(q_f, 1), qs_hi[0:QK, :], qs_lo[0:QK, :]), (1, h(k_f, 1), ks_hi[0:QK, :], ks_lo[0:QK, :])]
            n = lambda m: na_f[:, bass.ds(m, 1), :].rearrange("p a t -> p (a t)")
            return [(0, n(i), qs_hi[:, :], qs_lo[:, :]), (0, n(i + 2), ks_hi[:, :], ks_lo[:, :]),
                    (0, vn_f[:, :, bass.ds(i * P, P)], vs_hi[:, :, :], vs_lo[:, :, :])]

        def attention_pe(eng, l):
            nb = att_chunks(l)
            for kind, i, C, B, S, first in bodies(eng, l):
                for s in range(nb + 2):
                    if s < nb:
                        j, q0, keys = chunk_info(l, s)
                        rows = slice(0, QK) if kind == "mla" else slice(j * NA_DIM, (j + 1) * NA_DIM)
                        if s == 0:
                            eng.wait_ge(a_lo, S(3).n())
                        if s == nb // 2 and kind == "mla":
                            eng.wait_ge(a_lo, S(5).n())
                        if not (first and s < 2):
                            eng.wait_ge(a_exp, C(s).n(-1))
                        elif l:
                            eng.wait_ge(a_exp, ATT_C0[l])
                        for a, b in keys:
                            dst, q = pair[s % 2][:, a:b], slice(q0, q0 + P)
                            eng.matmul(dst, qs_hi[rows, q], ks_hi[rows, a:b], start=True, stop=False)
                            eng.matmul(dst, qs_hi[rows, q], ks_lo[rows, a:b], start=False, stop=False)
                            last = eng.matmul(dst, qs_lo[rows, q], ks_hi[rows, a:b], start=False, stop=True)
                        last.then_inc(a_s, 1)
                    if s >= 3 and s % 2:
                        blk_n = (s - 3) // 2
                        j, q0, keys = chunk_info(l, 2 * blk_n)
                        kc = [k for k in range(TOK // P) if k * P >= keys[0][0]]
                        eng.wait_ge(a_ptl, C(2 * blk_n).n(2))
                        if not (first and blk_n < 2 and l == 0):
                            eng.wait_ge(a_out, B(blk_n).n(-1))
                        dst = psum2[:, (blk_n % 2) * 512:(blk_n % 2) * 512 + 2 * P]
                        for k in kc:
                            eng.matmul(dst, vs_hi[:, k, :], pt_hi[:, k, :], start=k == kc[0], stop=False)
                            eng.matmul(dst, vs_hi[:, k, :], pt_lo[:, k, :], start=False, stop=False)
                            last = eng.matmul(dst, vs_lo[:, k, :], pt_hi[:, k, :], start=False, stop=k == kc[-1])
                        last.then_inc(a_pv, 1)
                    if 1 <= s <= nb:
                        j, q0, keys = chunk_info(l, s - 1)
                        eng.wait_ge(a_prob, C(s - 1).n(1))
                        if not (first and s == 1 and l == 0):
                            eng.wait_ge(a_ptl, C(s - 1).n())
                        for k in range(keys[0][0] // P, TOK // P):
                            last = eng.transpose(pmid[:, k * P:(k + 1) * P], prob[:, (s - 1) % 2, k * P:(k + 1) * P],
                                                 ident[:, :])
                        last.then_inc(a_t, 1)

        def attention_act(eng, l):
            nb = att_chunks(l)
            eng.preload_act_table_set("exp_and_others")
            eng.wait_ge(acc_done, mo(l, "kv", 1).n(6))
            eng.wait_ge(h_done, H_STEPS * (l + 1))
            eng.wait_ge(acc_free[(mo(l, "kv", 1) + 5).odd], read_out(mo(l, "kv", 1) + 5))
            for kind, i, C, B, S, first in bodies(eng, l):
                scale = MLA_SCALE if kind == "mla" else NA_SCALE

                def split(j):
                    for n, (head, src, hi, lo) in enumerate(attention_splits(kind, i)):
                        if head != j:
                            continue
                        if not (first and j == 0 and l == 0):
                            eng.wait_ge(a_s, C(0).n() if j == 0 else C(nb // 2).n())
                            if j == 0:
                                eng.wait_ge(a_pv, B(0).n())
                        eng.activation(hi, src, ACT.Copy).then_inc(a_hi, 1)

                split(0)
                for s in range(nb + 2):
                    if s < nb:
                        j, q0, keys = chunk_info(l, s)
                        a, b = keys[0][0], TOK
                        own = kind == "mla" or q0 >= SEQ
                        eng.wait_ge(a_max, C(s).n(1))
                        if not (first and s < 2 and l == 0):
                            eng.wait_ge(a_t, C(s).n(-1))
                        eng.activation(prob[:, s % 2, a:b], pair[s % 2][:, a:b] if own else prob[:, s % 2, a:b],
                                       ACT.Exp, bias=stat[:, s % 2, 1:2], scale=scale if own else 1.0,
                                       accum_out=stat[:, s % 2, 2:3]).then_inc(a_exp, 1)
                    if s >= 2:
                        c = s - 2
                        j, q0, keys = chunk_info(l, c)
                        eng.wait_ge(a_t, C(c).n(1))
                        if c % 2 == 0 and not (first and c == 0 and l == 0):
                            eng.wait_ge(a_pv, B(c // 2).n())
                        k0 = keys[0][0] // P
                        eng.activation(pt_hi[:, k0:, (c % 2) * P:(c % 2 + 1) * P],
                                       pmid[:, k0 * P:TOK].rearrange("p (k q) -> p k q", q=P), ACT.Copy).then_inc(a_pth, 1)
                    if s == nb // 2 - 1:
                        split(1)

        def attention_pool(eng, l):
            for kind, i, C, B, S, first in bodies(eng, l):
                for n, (head, src, hi, lo) in enumerate(attention_splits(kind, i)):
                    eng.wait_ge(a_hi, S(n).n(1))
                    eng.tensor_tensor(lo, src, hi.bitcast(F32), ALU.subtract).then_inc(a_lo, 1)

        def attention_dve(eng, l):
            nb = att_chunks(l)
            for kind, i, C, B, S, first in bodies(eng, l):
                scale = MLA_SCALE if kind == "mla" else NA_SCALE
                for s in range(nb + 3):
                    if s < nb:
                        j, q0, keys = chunk_info(l, s)
                        a, b = keys[0][0], TOK
                        own = kind == "mla" or q0 >= SEQ
                        st = stat[:, s % 2, :]
                        step0 = C(s)
                        eng.wait_ge(a_s, C(s).n(1))
                        if own:
                            eng.tensor_reduce(st[:, 0:1], pair[s % 2][:, a:b], AX_X, ALU.max).then_inc(a_dve, 1)
                            n = 1
                        else:
                            slots = BIAS_SLOTS // 2 - 1 - 2 * (q0 // P)
                            if s % (nb // 2) == 0:
                                eng.wait_ge(tt_loaded[j], Nth(i, 1, 2 * l).n(1) * 16)
                            if not (first and s < 2 and l == 0):
                                eng.wait_ge(a_t, C(s).n(-1))
                            eng.scalar_tensor_tensor(prob[:, s % 2, 0:SEQ], pair[s % 2][:, 0:SEQ], scale,
                                                     na_tt[:, j, slots * GRID_W:slots * GRID_W + SEQ],
                                                     ALU.mult, ALU.add).then_inc(a_dve, 1)
                            eng.tensor_scalar(prob[:, s % 2, SEQ:TOK], pair[s % 2][:, SEQ:TOK], scale, None, ALU.mult)\
                               .then_inc(a_dve, 1)
                            eng.wait_ge(a_dve, dve_steps(l, kind, i, s, 2))
                            eng.tensor_reduce(st[:, 0:1], prob[:, s % 2, :], AX_X, ALU.max).then_inc(a_dve, 1)
                            n = 3
                        eng.wait_ge(a_dve, dve_steps(l, kind, i, s, n))
                        eng.tensor_scalar(st[:, 1:2], st[:, 0:1], -scale if own else -1.0, None, ALU.mult)\
                           .then_inc(a_max, 1)
                    if 1 <= s <= nb:
                        c = s - 1
                        j, q0, keys = chunk_info(l, c)
                        eng.wait_ge(a_exp, C(c).n(1))
                        eng.reciprocal(stat[:, c % 2, 3:4], stat[:, c % 2, 2:3]).then_inc(a_rsum, 1)
                        eng.wait_ge(a_rsum, C(c).n(1))
                        eng.tensor_scalar(prob[:, c % 2, keys[0][0]:TOK], prob[:, c % 2, keys[0][0]:TOK],
                                          stat[:, c % 2, 3:4], None, ALU.mult).then_inc(a_prob, 1)
                    if 2 <= s < nb + 2:
                        c = s - 2
                        j, q0, keys = chunk_info(l, c)
                        k0 = keys[0][0] // P
                        eng.wait_ge(a_pth, C(c).n(1))
                        cols = slice((c % 2) * P, (c % 2 + 1) * P)
                        eng.tensor_tensor(pt_lo[:, k0:, cols], pmid[:, k0 * P:TOK].rearrange("p (k q) -> p k q", q=P),
                                          pt_hi[:, k0:, cols].bitcast(F32), ALU.subtract).then_inc(a_ptl, 1)
                    if s >= 4 and s % 2 == 0:
                        b = (s - 4) // 2
                        j, q0, keys = chunk_info(l, 2 * b)
                        eng.wait_ge(a_pv, B(b).n(1))
                        r = slice(j * 64, j * 64 + 64)
                        y = y_f[r, bass.ds(i + (0 if kind == "mla" else 4), 1), q0:q0 + 2 * P].rearrange("p a t -> p (a t)")
                        eng.tensor_copy(y, psum2[r, (b % 2) * 512:(b % 2) * 512 + 2 * P]).then_inc(a_out, 1)

        def dve_steps(l, kind, i, s, n):
            def body(kd, layer, upto):
                return sum(1 if kd == "mla" or chunk_info(layer, c)[1] >= SEQ else 3 for c in range(upto))
            c0 = 0
            for layer in range(l):
                c0 += 4 * body("mla", layer, att_chunks(layer)) + 2 * body("na", layer, att_chunks(layer))
            if kind == "na":
                c0 += 4 * body("mla", l, att_chunks(l))
            return Nth(i, body(kind, l, att_chunks(l)), c0 + body(kind, l, s) + n).n()

        blocks = ["ff0"] if stop == "ff0" else ["ff0", "mix0"] if stop == "mix0" else ["ff0", "mix0", "ff1", "ff2", "mix1", "ff3"]
        o_final = {"ff0": FF_O0[0] + FF_TILES, "mix0": MIX_O0[0] + MIX_OUTS}.get(stop, O_END)
        block = ctx.enter_context(nc.Block())

        @block.sync
        def _(sp):
            sp.dma_start(ident[:, :], k_ident).then_inc(const_loaded, 16)
            sp.wait_ge(vec_zero, 1)
            sp.dma_start(vrows[V_C:V_C + KD, 0, :], c.rearrange("a (k p) -> (a k) p", p=P)).then_inc(vec_loaded, 16)
            sp.dma_start(vrows[V_C + KD:V_C + 2 * KD, 0, :], c_ctx.rearrange("(k p) -> k p", p=P))\
              .then_inc(vec_loaded, 16)
            for l in range(DEPTH):
                for row, v in ((V_BMOD, b_mod), (V_GCQ, g_cq), (V_GCKV, g_ckv), (V_PSC, pool_scale)):
                    src = v[l].rearrange("(k p) -> k p", p=P)
                    sp.dma_start(vrows[row:row + src.shape[0], l, :], src).then_inc(vec_loaded, 16)
                for row, v in ((V_GQ, g_mla_q), (V_GK, g_mla_k)):
                    sp.dma_start(vrows[row:row + 1, l, 0:QK], v[l:l + 1, :]).then_inc(vec_loaded, 16)
                for row, v in ((V_GNQ, g_na_q), (V_GNK, g_na_k)):
                    for a in (0, NA_DIM):
                        sp.dma_start(vrows[row:row + 1, l, a:a + NA_DIM], v[l:l + 1, :]).then_inc(vec_loaded, 16)
            for tc in range(TOK // P):
                src = x[0, tc * P:(tc + 1) * P, :] if tc < SEQ // P else ctx_in[0, tc * P - SEQ:(tc + 1) * P - SEQ, :]
                sp.dma_start(x_rows[:, tc, :], src).then_inc(x_loaded, 16)
            for dst, src in ((cos, k_cos), (sin, k_sin), (perm, k_perm)):
                sp.dma_start(dst[0:QK, :], src).then_inc(table_loaded, 16)
            first_loads(sp, blocks[0])
            for m in range(2):
                mod_load(sp, 0, Nth(m, 1, 0))
            for i in steps(sp, 1, START_MOD // 2):
                for m in range(2):
                    mod_load(sp, 0, Nth(i, 2, m))
            for b, following in zip(blocks, blocks[1:] + [None]):
                if b[:2] == "ff":
                    ff_sp(sp, int(b[2]), following)
                else:
                    mix_sp(sp, int(b[3]))
                    first_loads(sp, following)
            for tc in range(SEQ // P):
                sp.wait_ge(out_staged, tc + 1)
                sp.dma_start(out[0, tc * P:(tc + 1) * P, :], out_rows[:, tc % 2, :]).then_inc(out_stored[tc % 2], 16)
            for j in range(2):
                sp.wait_ge(out_stored[j], 16 * (SEQ // P // 2))

        N_VEC = 2 + DEPTH * 10

        @block.gpsimd
        def _(pool):
            pool.memset(vrows[:, :, :], 0.0).then_inc(vec_zero, 1)
            pool.memset(ones[:, :], 1.0).then_inc(const_set, 1)
            pool.memset(eps[:, :], EPS).then_inc(const_set, 1)
            pool.memset(blk[:, :], 0.0).then_inc(blk_set, 1)
            pool.wait_ge(blk_set, 1)
            for a in (0, 64):
                pool.memset(blk[a:a + 64, a:a + 64], 1.0).then_inc(blk_set, 1)
            pool.memset(rp_row[:, :], 0.0).then_inc(bias_pad, 1)
            pool.wait_ge(bias_pad, 1)
            pool.dma_start(rp_row[0:1, P:P + N_RPB], na_rpb.rearrange("l h r c -> (l h r c)").rearrange("(a n) -> a n", a=1))\
                .then_inc(bias_raw, 16)
            pool.wait_ge(bias_raw, 16)
            pool.dma_start(rpb_pad.rearrange("(a n) -> a n", a=1), rp_row[0:1, :]).then_inc(bias_raw, 16)
            pool.wait_ge(bias_raw, 32)
            for par in range(2):
                shifted = bass.AP(rpb_pad.tensor, P + (1 - par) * RPB_C + WIN_C - GRID_W,
                                  [[1, GRID_W], [RPB_R * RPB_C, DEPTH * NA_HEADS], [RPB_C, BIAS_SLOTS], [1, GRID_W]])
                dst = na_bias.rearrange("l h (a q) (s c) -> a q (l h) s c", a=2, c=GRID_W)
                for cq in steps(pool, 0, GRID_W):
                    pool.dma_start(dst[par, cq], shifted[cq * -1 + (GRID_W - 1)]).then_inc(bias_toep, 16)
                    pool.wait_ge(bias_toep, cq * 16 + 16 * (GRID_W * par + 1))
            pool.dma_start(bias_st[:, :, :, :].rearrange("p a s c -> p a (s c)"), na_bias.rearrange("l h p n -> p (l h) n"))\
                .then_inc(bias_toep, 16)
            pool.wait_ge(bias_toep, 16 * (2 * GRID_W + 1))
            n = 0
            for par in range(2):
                rows = slice(par * GRID_W, (par + 1) * GRID_W)
                all_slots = bias_st[rows, :, :, :].rearrange("p a s c -> p (a s) c")
                n_slots = DEPTH * NA_HEADS * BIAS_SLOTS
                for cut, base_v, cm, step in ((slice(0, GRID_W - WIN_C), WIN_C // 2, -1, 1),
                                              (slice(WIN_C, GRID_W), WIN_C // 2 - 1 - WIN_C, 1, -1)):
                    v = all_slots[:, :, cut]
                    if n % 2:
                        pool.wait_ge(bias_cut, n)
                    pool.affine_select(out=v, in_=v, compare_op=ALU.is_ge, fill=NEG, base=base_v,
                                       pattern=[[0, n_slots], [step, GRID_W - WIN_C]], channel_multiplier=cm)\
                        .then_inc(bias_cut, 1)
                    n += 1
            pool.wait_ge(bias_cut, n)
            pool.dma_start(na_bias.rearrange("l h p n -> p (l h) n"), bias_st[:, :, :, :].rearrange("p a s c -> p a (s c)"))\
                .then_inc(bias_stored, 16)
            for b in blocks:
                if b[:3] == "mix":
                    mix_pool(pool, int(b[3]))

        @block.tensor
        def _(pe):
            pe.wait_ge(const_loaded, 16)
            pe.wait_ge(vec_loaded, 16 * N_VEC)
            for l in range(DEPTH):
                pe.transpose(pair[l][:, 0:P], vrows[:, l, :], ident[:, :]).then_inc(acc_done, 1)
            pe.wait_ge(x_loaded, 16 * (TOK // P))
            for tc in range(TOK // P):
                o = 2 + tc
                pe.wait_ge(acc_free[o % 2], o // 2)
                for k in range(KD):
                    last = pe.transpose(pair[o % 2][:, k * P:(k + 1) * P], x_rows[:, tc, k * P:(k + 1) * P],
                                        ident[:, :])
                last.then_inc(acc_done, 1)
            pe.wait_ge(cs_ready, 2)
            pe.wait_ge(const_set, 2)
            for m in range(2):
                mod_product(pe, Nth(m, 1, 0))
            for i in steps(pe, 1, START_MOD // 2):
                for m in range(2):
                    mod_product(pe, Nth(i, 2, m))
            for b in blocks:
                if b[:2] == "ff":
                    inst = int(b[2])
                    norm_pe(pe, X_NORM[inst // 2, 2 * (inst % 2)])
                    ff_pe(pe, inst)
                else:
                    if b == "mix0":
                        pe.wait_ge(table_loaded, 48)
                        pe.wait_ge(blk_set, 3)
                    pe.wait_ge(perm_ready, 2 * int(b[3]) + 2)
                    mix_pe(pe, int(b[3]))
            for tc in range(SEQ // P):
                o = o_final + tc
                if tc == 0:
                    for e in (0, 1):
                        pe.wait_ge(acc_free[(o_final + e) % 2], (o_final + e) // 2)
                pe.wait_ge(acc_free[o % 2], o // 2)
                for k in range(KD):
                    last = pe.transpose(pair[o % 2][:, k * P:(k + 1) * P], xT[:, k, tc * P:(tc + 1) * P],
                                        ident[:, :])
                last.then_inc(acc_done, 1)

        @block.scalar
        def _(act):
            act.wait_ge(acc_free[0], 1)
            for j in range(2):
                act.activation(cs[:, :, j], vecs[:, 0, V_C + j * KD:V_C + (j + 1) * KD], ACT.Silu).then_inc(cs_ready, 1)
            for t in range(2):
                split_hi(act, Nth(t, 1, 0), WIDTHS[t], None)
            act.wait_ge(const_set, 2)
            for b in blocks:
                if b[:2] == "ff":
                    inst = int(b[2])
                    norm_act(act, X_NORM[inst // 2, 2 * (inst % 2)])
                    if inst == 0:
                        act.wait_ge(bias_stored, 16)
                    ff_act(act, inst)
                else:
                    mix_act(act, int(b[3]))

        @block.vector
        def _(dve):
            for l in range(DEPTH):
                dve.wait_ge(acc_done, l + 1)
                dve.tensor_copy(vecs[:, l, :], pair[l][:, 0:P]).then_inc(acc_free[l], 1)
            for tc in range(TOK // P):
                o = 2 + tc
                dve.wait_ge(acc_done, o + 1)
                dve.tensor_copy(xT[:, :, tc * P:(tc + 1) * P], pair[o % 2][:, :].rearrange("p (k t) -> p k t", k=KD))\
                   .then_inc(acc_free[o % 2], 1)
            dve.wait_ge(acc_free[0], 1)
            dve.wait_ge(acc_free[1], 1)
            dve.tensor_scalar(vecs_half[:, :, :], vecs[:, :, :], 0.5, None, ALU.mult).then_inc(vec_half_ready, 1)
            dve.wait_ge(vec_half_ready, 1)
            for t in range(2):
                split_lo(dve, Nth(t, 1, 0), WIDTHS[t])
            for i in steps(dve, 0, START_MOD // 2):
                for m in range(2):
                    mod_read(dve, Nth(i, 2, m))
            for b in blocks:
                if b[:2] == "ff":
                    inst = int(b[2])
                    mod_vectors(dve, inst // 2, 2 * (inst % 2))
                    norm_dve(dve, X_NORM[inst // 2, 2 * (inst % 2)])
                    ff_dve(dve, inst)
                else:
                    if b == "mix0":
                        dve.wait_ge(table_loaded, 48)
                    mix_dve(dve, int(b[3]))
            for tc in range(SEQ // P):
                o = o_final + tc
                dve.wait_ge(acc_done, o + 1)
                if tc >= 2:
                    dve.wait_ge(out_stored[tc % 2], 16 * (tc // 2))
                dve.tensor_copy(out_rows[:, tc % 2, :], pair[o % 2][:, :]).then_inc(out_staged, 1)
                dve.wait_ge(out_staged, tc + 1)
                dve.sem_inc(acc_free[o % 2], 1)


_INS = ["x", "c", "ctx", "c_ctx", "w_mod", "b_mod", "w_ffn_gate", "w_ffn_up", "w_ffn_down", "w_in", "g_cq", "w_q_up",
        "g_ckv", "w_kv_up", "g_mla_q", "g_mla_k", "g_na_q", "g_na_k", "na_rpb", "w_pool", "pool_scale", "w_out"]


def constants():
    ident = np.eye(P, dtype=np.float32)
    a = ROPE // 2
    perm = np.zeros((QK, QK), np.float32)
    cos, sin = np.ones((QK, SEQ), np.float32), np.zeros((QK, SEQ), np.float32)
    t = np.arange(SEQ)
    inv_freq = (10000.0 ** (-np.arange(0, a, 2, dtype=np.float32) / np.float32(a))).astype(np.float32)
    for axis, pos in enumerate((t // GRID_W, t % GRID_W)):
        ang = pos.astype(np.float32)[None, :] * inv_freq[:, None]
        r = NOPE + axis * a
        h = a // 2
        cos[r:r + h], cos[r + h:r + a] = np.cos(ang), np.cos(ang)
        sin[r:r + h], sin[r + h:r + a] = -np.sin(ang), np.sin(ang)
        for i in range(h):
            perm[r + h + i, r + i] = 1.0
            perm[r + i, r + h + i] = 1.0
    inv = np.zeros((P, 2, POOLW), np.float32)
    for g in range(POOL_G):
        w = 2 << g
        for start, n in ((PAD, CTX), (2 * PAD + CTX, SEQ)):
            t = np.arange(n)
            cnt = np.clip(t + w // 2, 0, n) - np.clip(t - w // 2, 0, n)
            inv[(g % 2) * 64:(g % 2) * 64 + 64, g // 2, start:start + n] = (np.float32(1) / cnt.astype(np.float32))
    return dict(k_ident=ident, k_perm=perm, k_cos=cos, k_sin=sin, k_invcnt=inv)





def kernel(**inputs):
    import concourse.bacc as bacc
    from concourse.bass_utils import run_bass_kernel_spmd

    nc = bacc.Bacc("TRN2", target_bir_lowering=False, num_devices=1, dynamic_dma_scratch_size=8192)
    arrays, args = {}, []
    for name, value in [(n, inputs[n]) for n in _INS] + list(constants().items()):
        a = np.ascontiguousarray(value)
        arrays[f"in_{name}"] = a
        args.append(nc.dram_tensor(f"in_{name}", a.shape, mybir.dt.from_np(a.dtype), kind="ExternalInput").ap())
    args.append(nc.dram_tensor("out", (1, SEQ, D_MODEL), F32, kind="ExternalOutput").ap())
    args.append(nc.dram_tensor("rpb_pad", (N_RPB + 2 * P,), F32, kind="Internal").ap())
    args.append(nc.dram_tensor("na_bias", (DEPTH, NA_HEADS, P, BIAS_SLOTS * GRID_W), F32, kind="Internal").ap())
    program(nc, *args, STOP)
    return run_bass_kernel_spmd(nc, [arrays], core_ids=[0]).results[0]["out"]
```

```python
from contextlib import ExitStack

import numpy as np

import concourse.bass as bass
from concourse import mybir

STOP = None
F32 = mybir.dt.float32
F32R = mybir.dt.float32r
ALU = mybir.AluOpType
ACT = mybir.ActivationFunctionType
AX_X = mybir.AxisListType.X

P = 128
D_MODEL = 1024
KD = D_MODEL // P
SEQ, CTX = 512, 256
TOK = SEQ + CTX
PARTS = ((0, SEQ), (SEQ, TOK))
DEPTH = 2
GRID_W = 64
MLA_HEADS, NOPE, ROPE, V_DIM = 8, 64, 32, 64
QK = NOPE + ROPE
Q_RANK, KV_RANK = 768, 256
MLA_SCALE = QK ** -0.5
NA_HEADS, NA_DIM, WIN_R, WIN_C = 4, 64, 8, 16
NA_WIDTH = NA_HEADS * NA_DIM
NA_SCALE = NA_DIM ** -0.5
POOL_G = 4
D_FF = 2816
HALF = D_FF // P // 2
N_MOD = 9
MOD_TILES = N_MOD * KD
EPS = 1e-6
NEG = -1.0e30
C_Q, C_KV, C_KR = 0, Q_RANK, Q_RANK + KV_RANK
C_QN = C_KR + ROPE
C_KN, C_VN, C_POOL = C_QN + NA_WIDTH, C_QN + 2 * NA_WIDTH, C_QN + 3 * NA_WIDTH
RPB_R, RPB_C = 2 * WIN_R - 1, 2 * WIN_C - 1
BIAS_SLOTS = RPB_R - 1
V_BMOD, V_GCQ, V_GCKV, V_PSC, V_GQ, V_GK, V_GNQ, V_GNK, V_C = 0, 72, 78, 80, 82, 83, 84, 85, 86
PAD = 8
POOLW = PAD + CTX + PAD + SEQ + PAD

MIX_ORDER = [("pool", 0), ("cq", 0), ("cq", 1), ("wpool", 0), ("pool", 1), ("cq", 2), ("cq", 3), ("wpool", 1),
             ("cq", 4), ("cq", 5), ("ckv", 0), ("ckv", 1), ("kr", 0), ("qn", 0), ("qn", 1), ("kn", 0), ("kn", 1),
             ("vn", 0), ("vn", 1)]
MIX_COL = {"pool": C_POOL, "cq": C_Q, "ckv": C_KV, "kr": C_KR, "qn": C_QN, "kn": C_KN, "vn": C_VN}
MIX_OUT, _n = {}, 0
for _kind, _c in MIX_ORDER:
    if _kind == "wpool":
        MIX_OUT["y", 2 * _c], MIX_OUT["y", 2 * _c + 1] = _n, _n + 1
        _n += 2
    else:
        MIX_OUT[_kind, _c] = _n
        _n += 1
MIX_OUT["q", 0] = _n
MIX_OUT["kv", 0], MIX_OUT["kv", 1], MIX_OUT["wo", 0] = _n + 8, _n + 14, _n + 20
T_Q = len(MIX_ORDER)
T_KV, T_WO = T_Q + MLA_HEADS, T_Q + MLA_HEADS + 2

FF_TILES = 2 * (2 * HALF + KD)
MIX_TILES = 37
MIX_OUTS = 49
WIDTHS = []
FF_T0, FF_O0, MIX_T0, MIX_O0 = [], [], [], []
N_START = SEQ // P + CTX // P + 2
_o = N_START
for _l in range(DEPTH):
    for _fi in range(2):
        FF_T0.append(len(WIDTHS))
        FF_O0.append(_o)
        WIDTHS += ([KD * P] * (2 * HALF) + [HALF * P] * KD) * 2
        _o += FF_TILES
        if _fi == 0:
            MIX_T0.append(len(WIDTHS))
            MIX_O0.append(_o)
            WIDTHS += [P if kind == "wpool" else KD * P for kind, _ in MIX_ORDER]
            WIDTHS += [Q_RANK // P * QK] * MLA_HEADS + [KV_RANK // P * 4 * P] * 2 + [KD * P] * KD
            _o += MIX_OUTS
N_TILES, O_END = {"ff0": 60, "mix0": MIX_T0[0] + MIX_TILES}.get(STOP, len(WIDTHS)), _o


class Nth:

    def __init__(self, i, stride, const):
        if isinstance(i, int):
            i, stride, const = 0, 0, i * stride + const
        self.i, self.stride, self.const = i, stride, const

    def __add__(self, k):
        return Nth(self.i, self.stride, self.const + k)

    def _at(self, stride, const):
        return self.i * stride + const if stride else const

    def n(self, plus=0):
        return self._at(self.stride, self.const + plus)

    def half(self, plus=0, times=1):
        assert self.stride % 2 == 0
        return self._at(self.stride // 2 * times, (self.const // 2 + plus) * times)

    @property
    def odd(self):
        assert self.stride % 2 == 0
        return self.const % 2


def steps(eng, a, b):
    if b - a == 1:
        yield a
    else:
        with eng.Fori(a, b) as i:
            yield i


def width(t0, stride, a, b):
    w = {WIDTHS[t0 + stride * i] if t0 + stride * i < N_TILES else 0 for i in range(a, b)}
    assert len(w) == 1
    return w.pop()


START_MOD = 2 * KD
FF_SEGS = [
    [[(0, 1, 0, START_MOD, 4), (1, 10, 0, START_MOD, 4), (10, 11, 0, START_MOD, 4)],
     [(0, 3, 0, 60, 4), (3, 10, 1, 60, 4), (10, 11, 1, 60, 4)]],
    [[(0, 1, 1, 104, 2), (1, 10, 1, 104, 2), (10, 11, 1, 104, 2)],
     [(0, 9, 1, 126, 2), (9, 10, 1, 0, 0), (10, 11, 1, 0, 0)]],
    [[(0, 1, 1, 0, 0), (1, 10, 1, 0, 0), (10, 11, 1, 0, 0)], [(0, 10, 1, 0, 0), (10, 11, 1, 0, 0)]],
    [[(0, 1, 1, 0, 0), (1, 10, 1, 0, 0), (10, 11, 1, 0, 0)], [(0, 10, 1, 0, 0), (10, 11, 1, 0, 0)]],
]


def program(nc, x, c, ctx_in, c_ctx, w_mod, b_mod, w_gate, w_up, w_down, w_in, g_cq, w_q_up, g_ckv, w_kv_up,
            g_mla_q, g_mla_k, g_na_q, g_na_k, na_rpb, w_pool, pool_scale, w_out,
            k_ident, k_perm, k_cos, k_sin, k_invcnt, out, na_bias, stop):
    with ExitStack() as ctx:
        def sem(name):
            return ctx.enter_context(nc.semaphore(name))

        base = (nc.sbuf_base + 63) // 64 * 64
        place = {}

        def sb(name, shape, dt, at=None, off=0):
            nonlocal base
            size = int(np.prod(shape[1:])) * 4
            if at is None:
                start, base = base, base + (size + 31) // 32 * 32
            else:
                start = place[at][0] + off
                assert off + size <= place[at][1] + 0, (name, off, size, place[at])
            place[name] = (start, size)
            return nc.alloc_sbuf_tensor_at(name, shape, dt, offset=start)

        xT = sb("xT", [P, KD, TOK], F32)
        sb("wring", [P, 6 * HALF * P], F32)
        slot_bytes = 2 * HALF * P * 4
        w_raw = sb("w_raw", [P, 2, HALF * P], F32, "wring", 0)
        w_hi = sb("w_hi", [P, 2, HALF * P], F32R, "wring", slot_bytes)
        w_lo = sb("w_lo", [P, 2, HALF * P], F32R, "wring", 2 * slot_bytes)
        sb("harea", [P, 2 * KD * TOK], F32)
        h_hi = sb("h_hi", [P, KD, TOK], F32R, "harea", 0)
        h_lo = sb("h_lo", [P, KD, TOK], F32R, "harea", KD * TOK * 4)
        x_rows = sb("x_rows", [P, TOK // P, D_MODEL], F32, "harea", 0)
        out_rows = sb("out_rows", [P, 2, D_MODEL], F32, "harea", 0)
        sb("sarea", [P, 2 * HALF * TOK], F32)
        s_hi = sb("s_hi", [P, HALF, TOK], F32R, "sarea", 0)
        s_lo = sb("s_lo", [P, HALF, TOK], F32R, "sarea", HALF * TOK * 4)
        sb("scratch", [P, 4 * TOK], F32)
        sq = sb("sq", [P, 2, TOK], F32, "scratch", 0)
        hf = sb("hf", [P, 2, TOK], F32, "scratch", 2 * TOK * 4)
        sg = sb("sg", [P, TOK], F32, "scratch", 0)
        sf = sb("sf", [P, TOK], F32, "scratch", 2 * TOK * 4)
        q_f = sb("q_f", [P, MLA_HEADS, TOK], F32, "harea", 0)
        k_f = sb("k_f", [P, MLA_HEADS, TOK], F32, "harea", KD * TOK * 4)
        RQ, RK = Q_RANK // P, KV_RANK // P
        cq_hi = sb("cq_hi", [P, RQ, TOK], F32R, "sarea", 0)
        cq_f = sb("cq_f", [P, RQ, TOK], F32, "sarea", RQ * TOK * 4)
        cq_lo = sb("cq_lo", [P, RQ, TOK], F32R, "sarea", RQ * TOK * 4)
        ck_at = 2 * RQ * TOK * 4
        ck_hi = sb("ck_hi", [P, RK, TOK], F32R, "sarea", ck_at)
        ck_f = sb("ck_f", [P, RK, TOK], F32, "sarea", ck_at + RK * TOK * 4)
        ck_lo = sb("ck_lo", [P, RK, TOK], F32R, "sarea", ck_at + RK * TOK * 4)
        na_at = ck_at + 2 * RK * TOK * 4
        na_f = sb("na_f", [P, 4, TOK], F32, "sarea", na_at)
        vn_f = sb("vn_f", [P, TOK // P, NA_WIDTH], F32, "sarea", na_at + 4 * TOK * 4)
        v_hi = sb("v_hi", [P, TOK // P, MLA_HEADS * V_DIM], F32R, "sarea", 0)
        v_lo = sb("v_lo", [P, TOK // P, MLA_HEADS * V_DIM], F32R, "sarea", 4 * TOK * 4)
        y_f = sb("y_f", [P, 6, TOK], F32, "harea", KD * TOK * 4)
        vn_hi = sb("vn_hi", [P, TOK // P, NA_WIDTH], F32R, "sarea", 14 * TOK * 4)
        vn_lo = sb("vn_lo", [P, TOK // P, NA_WIDTH], F32R, "sarea", na_at + 4 * TOK * 4)
        pu = sb("pu", [P, POOLW], F32, "sarea", na_at)
        pool_lo = sb("pool_lo", [P, TOK], F32R, "sarea", na_at)
        ps = [sb(f"ps{i}", [P, POOLW], F32, "sarea", na_at + (i + 1) * POOLW * 4) for i in range(2)]
        inv_cnt = sb("inv_cnt", [P, POOLW], F32, "sarea", na_at + 3 * POOLW * 4)
        pool_hi = sb("pool_hi", [P, TOK], F32R, "sarea", na_at + 4 * POOLW * 4)
        sb("pbuf", [P, 2 * TOK], F32)
        pt_hi, pt_lo = (sb(n, [P, TOK // P, 4, P], F32R, "wring", 4 * i * TOK * 4) for i, n in enumerate(("pt_hi", "pt_lo")))
        prob = sb("prob", [P, 3, TOK], F32, "wring", 8 * TOK * 4)
        att_set = [[sb(n, [P, TOK], F32R, at, off * TOK * 4) for n, at, off in places]
                   for places in ((("qs_hi0", "sarea", 8), ("qs_lo0", "sarea", 9), ("ks_hi0", "sarea", 10),
                                   ("ks_lo0", "sarea", 11)),
                                  (("qs_hi1", "sarea", 12), ("qs_lo1", "sarea", 13), ("ks_hi1", "pbuf", 0),
                                   ("ks_lo1", "pbuf", 1)))]
        na_tt = sb("na_tt", [P, 2, BIAS_SLOTS * GRID_W], F32, "scratch", 0)
        mod_raw = sb("mod_raw", [P, 2, KD, P], F32)
        yp_f = sb("yp_f", [P, 2, TOK], F32, "mod_raw", 0)
        acc = sb("acc", [P, TOK], F32, "pbuf", 0)
        rstd = sb("rstd", [P, TOK], F32, "pbuf", TOK * 4)
        kr_f = sb("kr_f", [P, TOK], F32)
        rot_s = sb("rot_s", [P, SEQ], F32)
        cos = sb("cos", [P, SEQ], F32)
        sin = sb("sin", [P, SEQ], F32)
        perm = sb("perm", [P, QK], F32)
        perm_q = sb("perm_q", [P, QK], F32)
        perm_k = sb("perm_k", [P, QK], F32)
        blk = sb("blk", [P, P], F32)
        stat = sb("stat", [P, 2, 3], F32)
        ident = sb("ident", [P, P], F32)
        ones = sb("ones", [P, P], F32)
        eps = sb("eps", [P, 1], F32)
        vrows = sb("vrows", [P, DEPTH, P], F32, "sarea", 0)
        vecs = sb("vecs", [P, DEPTH, P], F32)
        vecs_half = sb("vecs_half", [P, DEPTH, P], F32)
        cs = sb("cs", [P, KD, 2], F32)
        mod = sb("mod", [P, DEPTH * MOD_TILES, 2], F32)
        mv = sb("mv", [P, 3, KD, 2], F32)

        pair = [ctx.enter_context(nc.psum_tensor(f"pair{i}", [P, 1024], F32)) for i in range(2)]
        pmid = ctx.enter_context(nc.psum_tensor("pmid", [P, 1024], F32))
        psum2 = ctx.enter_context(nc.psum_tensor("psum2", [P, 1024], F32))
        mod_ps = [pmid[:, 0:2], pmid[:, 512:514]]

        x_loaded, ctx_loaded, const_loaded = sem("x_loaded"), sem("ctx_loaded"), sem("const_loaded")
        vec_zero, vec_loaded = sem("vec_zero"), sem("vec_loaded")
        gain_scaled = sem("gain_scaled")
        const_set, cs_ready, vec_half_ready = sem("const_set"), sem("cs_ready"), sem("vec_half_ready")
        w_loaded = [sem("w_loaded0"), sem("w_loaded1")]
        w_hi_done, w_lo_done = sem("w_hi_done"), sem("w_lo_done")
        acc_done = sem("acc_done")
        acc_free = [sem("acc_free0"), sem("acc_free1")]
        mod_loaded = [sem("mod_loaded0"), sem("mod_loaded1")]
        mod_done = sem("mod_done")
        mod_free = [sem("mod_free0"), sem("mod_free1")]
        mv_ready = sem("mv_ready")
        gate_ready = sem("gate_ready")
        n_sq, n_acc, n_sum, n_std, n_rstd = (sem(f"n_{k}") for k in ("sq", "acc", "sum", "std", "rstd"))
        n_t, n_full, n_hi, n_lo = (sem(f"n_{k}") for k in ("t", "full", "hi", "lo"))
        s_hi_done = sem("s_hi_done")
        bias_neg, bias_filled, bias_stored = sem("bias_neg"), sem("bias_filled"), sem("bias_stored")
        table_loaded, blk_set, perm_ready = sem("table_loaded"), sem("blk_set"), sem("perm_ready")
        inv_loaded = sem("inv_loaded")
        pads_set, pool_step, pool_hi_done, pool_lo_done = (
            sem(n) for n in ("pads_set", "pool_step", "pool_hi_done", "pool_lo_done"))
        kr_spread, kr_sq = sem("kr_spread"), sem("kr_sq")
        h_sum, h_std, h_rstd, h_step, h_done = (sem(f"h_{k}") for k in ("sum", "std", "rstd", "step", "done"))
        w_loaded_pool = sem("w_loaded_pool")
        a_hi, a_lo, v_hi_done = sem("a_hi"), sem("a_lo"), sem("v_hi_done")
        a_s, a_max, a_exp, a_rsum, a_prob, a_t, a_pth, a_ptl, a_pv, a_out, a_bias = (
            sem(f"a_{k}") for k in ("s", "max", "exp", "rsum", "prob", "t", "pth", "ptl", "pv", "out", "bias"))
        tt_loaded = [sem("tt_loaded0"), sem("tt_loaded1")]
        y_hi_done, y_lo_done = sem("y_hi_done"), sem("y_lo_done")
        s_lo_done = sem("s_lo_done")
        out_staged, out_stored = sem("out_staged"), [sem("out_stored0"), sem("out_stored1")]

        def load(eng, t, src, dst):
            if not (t.stride == 0 and t.const < 2):
                eng.wait_ge(w_lo_done, t.n(-1))
            eng.dma_start(dst, src).then_inc(w_loaded[t.odd], 16)

        def split_hi(eng, t, w, done):
            if w == 0:
                return
            if done is not None:
                eng.wait_ge(acc_done, done.n(1))
            eng.wait_ge(w_loaded[t.odd], t.half(1, 16))
            eng.activation(w_hi[:, t.odd, 0:w], w_raw[:, t.odd, 0:w], ACT.Copy).then_inc(w_hi_done, 1)

        def split_lo(eng, t, w):
            if w == 0:
                return
            eng.wait_ge(w_hi_done, t.n(1))
            eng.tensor_tensor(w_lo[:, t.odd, 0:w], w_raw[:, t.odd, 0:w], w_hi[:, t.odd, 0:w].bitcast(F32),
                              ALU.subtract).then_inc(w_lo_done, 1)

        def read_out(o):
            return o.half(1)

        def product(eng, t, o, chunks, lhs, rhs, cols, before_chunk=None):
            if t is not None:
                eng.wait_ge(w_lo_done, t.n(1))
            eng.wait_ge(acc_free[o.odd], o.half())
            for k in range(chunks):
                if before_chunk:
                    before_chunk(k)
                (wh, wl), first, end = lhs(k), k == 0, k == chunks - 1
                for a, b in cols:
                    (rh, rl), dst = rhs(k, a, b), pair[o.odd][0:wh.shape[-1], a:b]
                    eng.matmul(dst, wh, rh, start=first, stop=False)
                    eng.matmul(dst, wh, rl, start=False, stop=False)
                for a, b in cols:
                    (rh, rl), dst = rhs(k, a, b), pair[o.odd][0:wh.shape[-1], a:b]
                    last = eng.matmul(dst, wl, rh, start=False, stop=end)
            last.then_inc(acc_done, 1)

        def wtile(t, per=P):
            return lambda k: (w_hi[:, t.odd, k * per:(k + 1) * per], w_lo[:, t.odd, k * per:(k + 1) * per])

        def h_moving(k, a, b):
            return h_hi[:, k, a:b], h_lo[:, k, a:b]

        norms = []

        def norm_bases(q):
            return sum(n["chunks"] for n in norms[:q]), sum(n["chunks"] - 1 for n in norms[:q])

        def norm_act(eng, q):
            n = norms[q]
            b0, a0 = norm_bases(q)
            w, ch = n["w"], n["chunks"]
            for k in range(ch):
                n["ready"](eng, k)
                if k >= 2:
                    eng.wait_ge(n_acc, a0 + max(1, k - 2))
                eng.activation(sq[:, k % 2, 0:w], n["src"](k), ACT.Square).then_inc(n_sq, 1)
            eng.wait_ge(n_sum, q + 1)
            eng.activation(sq[:, 0, 0:w], psum2[:, 0:w], ACT.Sqrt, bias=eps[:, 0:1],
                           scale=1.0 / (ch * P)).then_inc(n_std, 1)
            if n["mods"]:
                eng.wait_ge(mv_ready, n["mods"])
            for k in range(ch):
                eng.wait_ge(n_t, b0 + k + 1)
                if k >= 2:
                    eng.wait_ge(n_lo, b0 + k - 1)
                if n["shift"]:
                    for p, (a, b) in enumerate(PARTS):
                        if a < w:
                            last = eng.activation(hf[:, k % 2, a:b], sq[:, k % 2, a:b], ACT.Identity,
                                                  bias=n["shift"](k, p), scale=n["scale"](k, p))
                else:
                    last = eng.activation(hf[:, k % 2, 0:w], sq[:, k % 2, 0:w], ACT.Copy, scale=n["scale"](k, 0))
                last.then_inc(n_full, 1)
                eng.wait_ge(n_full, b0 + k + 1)
                eng.activation(n["hi"][:, k, 0:w], hf[:, k % 2, 0:w], ACT.Copy).then_inc(n_hi, 1)

        def norm_dve(eng, q):
            n = norms[q]
            b0, a0 = norm_bases(q)
            w, ch = n["w"], n["chunks"]
            for k in range(1, ch):
                eng.wait_ge(n_sq, b0 + k + 1)
                if k > 1:
                    eng.wait_ge(n_acc, a0 + k - 1)
                eng.tensor_tensor(acc[:, 0:w], sq[:, 0, 0:w] if k == 1 else acc[:, 0:w], sq[:, k % 2, 0:w],
                                  ALU.add).then_inc(n_acc, 1)
            eng.wait_ge(n_std, q + 1)
            eng.reciprocal(rstd[:, 0:w], sq[:, 0, 0:w]).then_inc(n_rstd, 1)
            eng.wait_ge(n_rstd, q + 1)
            for k in range(ch + 1):
                if k < ch:
                    if k >= 2:
                        eng.wait_ge(n_full, b0 + k - 1)
                    eng.tensor_tensor(sq[:, k % 2, 0:w], n["src"](k), rstd[:, 0:w], ALU.mult).then_inc(n_t, 1)
                if k >= 1:
                    eng.wait_ge(n_hi, b0 + k)
                    eng.tensor_tensor(n["lo"][:, k - 1, 0:w], hf[:, (k - 1) % 2, 0:w],
                                      n["hi"][:, k - 1, 0:w].bitcast(F32), ALU.subtract).then_inc(n_lo, 1)

        def norm_pe(eng, q):
            n = norms[q]
            _, a0 = norm_bases(q)
            eng.wait_ge(n_acc, a0 + n["chunks"] - 1)
            for a, b in PARTS:
                if a < n["w"]:
                    last = eng.matmul(psum2[:, a:b], ones[:, :], acc[:, a:b], start=True, stop=True)
            last.then_inc(n_sum, 1)

        def x_ready(o_first, eng_outs):
            def ready(eng, k):
                for o in eng_outs(k):
                    eng.wait_ge(acc_free[o % 2], o // 2 + 1)
            return ready

        def add_x_norm(block, w, outs, mods):
            norms.append(dict(chunks=KD, w=w, src=lambda k: xT[:, k, 0:w], ready=x_ready(0, outs), mods=mods,
                              scale=lambda k, p: mv[:, 0, k, p:p + 1], shift=lambda k, p: mv[:, 1, k, p:p + 1],
                              hi=h_hi, lo=h_lo))

        X_NORM, CQ_NORM, CK_NORM = {}, {}, {}
        mv_count = 0
        for l in range(DEPTH):
            for b in range(3):
                if (l, b) == (0, 0):
                    outs = lambda k: range(DEPTH, N_START) if k == 0 else ()
                else:
                    if b == 1:
                        o_end = FF_O0[2 * l] + FF_TILES
                    elif b == 2:
                        o_end = MIX_O0[l] + MIX_OUTS
                    else:
                        o_end = FF_O0[2 * l - 1] + FF_TILES
                    outs = (lambda o_end: lambda k: (o_end - KD + k,))(o_end)
                mv_count += 4
                X_NORM[l, b] = len(norms)
                add_x_norm((l, b), SEQ if (l, b) == (DEPTH - 1, 2) else TOK, outs, mv_count)
                if b == 1:
                    for kind, where, col, src, hi, lo, ch in (("cq", CQ_NORM, V_GCQ, cq_f, cq_hi, cq_lo, RQ),
                                                              ("ckv", CK_NORM, V_GCKV, ck_f, ck_hi, ck_lo, RK)):
                        where[l] = len(norms)
                        made = [MIX_O0[l] + MIX_OUT[kind, k] for k in range(ch)]
                        norms.append(dict(chunks=ch, w=TOK, src=lambda k, src=src: src[:, k, :], mods=0, shift=None,
                                          ready=x_ready(0, lambda k, made=made: (made[k],)),
                                          scale=lambda k, p, l=l, col=col: vecs[:, l, col + k:col + k + 1],
                                          hi=hi, lo=lo))

        def mod_vectors(eng, l, b):
            tiles = l * MOD_TILES + (3 * b + 2) * KD
            eng.wait_ge(mod_free[0], tiles // 2)
            eng.wait_ge(mod_free[1], tiles // 2)
            for which, group, add in ((0, 3 * b + 1, 1.0), (1, 3 * b, 0.0)):
                u = l * MOD_TILES + group * KD
                for j in range(2):
                    eng.scalar_tensor_tensor(mv[:, which, :, j], mod[:, u:u + KD, j], add,
                                             vecs[:, l, V_BMOD + group * KD:V_BMOD + (group + 1) * KD],
                                             ALU.add, ALU.add).then_inc(mv_ready, 1)

        def gate_vectors(eng, l, b):
            tiles = l * MOD_TILES + (3 * b + 3) * KD
            eng.wait_ge(mod_free[0], tiles // 2)
            eng.wait_ge(mod_free[1], tiles // 2)
            group, u = 3 * b + 2, l * MOD_TILES + (3 * b + 2) * KD
            bias = vecs if b == 1 else vecs_half
            for j in range(2):
                eng.scalar_tensor_tensor(mv[:, 2, :, j], mod[:, u:u + KD, j], 1.0 if b == 1 else 0.5,
                                         bias[:, l, V_BMOD + group * KD:V_BMOD + (group + 1) * KD],
                                         ALU.mult, ALU.add).then_inc(gate_ready, 1)
            eng.wait_ge(gate_ready, 2 * (3 * l + b + 1))

        def mod_load(eng, l, u):
            if not (u.stride == 0 and u.const < 2):
                eng.wait_ge(mod_done, u.n(-1))
            src = w_mod[l].rearrange("(k p) (t m) -> p k t m", p=P, m=P)[:, :, u.n(-l * MOD_TILES), :]
            eng.dma_start(mod_raw[:, u.odd, :, :], src).then_inc(mod_loaded[u.odd], 16)

        def mod_product(eng, u):
            eng.wait_ge(mod_loaded[u.odd], u.half(1, 16))
            if not (u.stride == 0 and u.const < 2):
                eng.wait_ge(mod_free[u.odd], u.half())
            for k in range(KD):
                last = eng.matmul(mod_ps[u.odd], mod_raw[:, u.odd, k, :], cs[:, k, :], start=k == 0,
                                  stop=k == KD - 1)
            last.then_inc(mod_done, 1)

        def mod_read(eng, u):
            eng.wait_ge(mod_done, u.n(1))
            eng.tensor_copy(mod[:, bass.ds(u.n(), 1), :], mod_ps[u.odd].rearrange("p (a b) -> p a b", a=1))\
               .then_inc(mod_free[u.odd], 1)

        def ff_cols(inst):
            return PARTS[:1] if inst == 3 else PARTS

        def ff_pe(eng, inst):
            cols = ff_cols(inst)
            lo0 = norm_bases(X_NORM[inst // 2, 2 * (inst % 2)])[0]
            for half in range(2):
                n0, o0 = FF_T0[inst] + 30 * half, FF_O0[inst] + 30 * half
                for a, b, _, u0, per in FF_SEGS[inst][half]:
                    for i in steps(eng, a, b):
                        for j in range(2):
                            t, o = Nth(i, 2, n0 + j), Nth(i, 2, o0 + j)
                            before = None
                            if half == 0 and (a, b) == (0, 1) and j == 0:
                                before = lambda k: eng.wait_ge(n_lo, lo0 + k + 1)
                            product(eng, t, o, KD, wtile(t), h_moving, cols, before)
                            for m in range(per // 2):
                                mod_product(eng, Nth(i, per, u0 + j * (per // 2) + m))
                for i in steps(eng, 0, KD // 2):
                    for j in range(2):
                        t, o = Nth(i, 2, n0 + 2 * HALF + j), Nth(i, 2, o0 + 2 * HALF + j)
                        if isinstance(i, int) or j == 0:
                            eng.wait_ge(s_lo_done, (2 * inst + half + 1) * HALF)
                        product(eng, t, o, HALF, wtile(t), lambda k, a, b: (s_hi[:, k, a:b], s_lo[:, k, a:b]), cols)

        def ff_up_load(eng, inst, half, i):
            l, fi = divmod(inst, 2)
            for j, w in enumerate((w_gate, w_up)):
                t = Nth(i, 2, FF_T0[inst] + 30 * half + j)
                src = w[l, fi].rearrange("(k p) (f m) -> p k f m", p=P, m=P)
                load(eng, t, src[:, :, i + half * HALF, :], w_raw[:, t.odd, 0:KD * P].rearrange("p (k m) -> p k m", m=P))

        def ff_down_load(eng, inst, half, i):
            l, fi = divmod(inst, 2)
            for j in range(2):
                t = Nth(i, 2, FF_T0[inst] + 30 * half + 2 * HALF + j)
                src = w_down[l, fi].rearrange("(f p) (d m) -> p f d m", p=P, m=P)
                load(eng, t, src[:, half * HALF:(half + 1) * HALF, i * 2 + j, :],
                     w_raw[:, t.odd, :].rearrange("p (k m) -> p k m", m=P))

        def first_loads(eng, b):
            if b is None:
                return
            if b[:2] == "ff":
                ff_up_load(eng, int(b[2]), 0, 0)
            else:
                for n in range(2):
                    mix_tile_load(eng, int(b[3]), n)

        def ff_sp(eng, inst, following):
            if inst == 1:
                eng.wait_ge(y_lo_done, KD)
            for half in range(2):
                for a, b, l, u0, per in FF_SEGS[inst][half]:
                    for i in steps(eng, a, b):
                        if b == HALF:
                            ff_down_load(eng, inst, half, 0)
                        else:
                            ff_up_load(eng, inst, half, i + 1)
                        for m in range(per):
                            mod_load(eng, l, Nth(i, per, u0 + m))
                for i in steps(eng, 1, KD // 2):
                    ff_down_load(eng, inst, half, i)
                if half == 0:
                    ff_up_load(eng, inst, 1, 0)
                else:
                    first_loads(eng, following)

        def ff_act(eng, inst):
            w = ff_cols(inst)[-1][1]
            eng.preload_act_table_set("silu_and_others")
            for half in range(2):
                n0, o0 = FF_T0[inst] + 30 * half, FF_O0[inst] + 30 * half
                s0 = (2 * inst + half) * HALF
                for a, b, _, _, _ in FF_SEGS[inst][half]:
                    for i in steps(eng, a, b):
                        t, o, s = Nth(i, 2, n0), Nth(i, 2, o0), Nth(i, 1, s0)
                        eng.wait_ge(acc_done, o.n(1))
                        eng.activation(sg[:, 0:w], pair[o.odd][:, 0:w], ACT.Silu).then_inc(acc_free[o.odd], 1)
                        split_hi(eng, t + 2, width(n0 + 2, 2, a, b), o)
                        eng.wait_ge(acc_free[(o + 1).odd], read_out(o + 1))
                        eng.activation(s_hi[:, bass.ds(i, 1), 0:w].rearrange("p a t -> p (a t)"), sf[:, 0:w],
                                       ACT.Copy).then_inc(s_hi_done, 1)
                        split_hi(eng, t + 3, width(n0 + 3, 2, a, b), o + 1)
                for a, b in ((0, 3), (3, 4)):
                    for i in steps(eng, a, b):
                        for j in range(2):
                            t, o = Nth(i, 2, n0 + 2 * HALF + j), Nth(i, 2, o0 + 2 * HALF + j)
                            split_hi(eng, t + 2, width(n0 + 2 * HALF + 2 + j, 2, a, b), o)

        def residual(eng, o, d, cols):
            eng.wait_ge(acc_done, o.n(1))
            for p, (a, b) in enumerate(cols):
                last = eng.scalar_tensor_tensor(
                    xT[:, bass.ds(d, 1), a:b].rearrange("p a t -> p (a t)"), pair[o.odd][:, a:b],
                    mv[:, 2, bass.ds(d, 1), p], xT[:, bass.ds(d, 1), a:b].rearrange("p a t -> p (a t)"),
                    ALU.mult, ALU.add)
            last.then_inc(acc_free[o.odd], 1)

        def ff_dve(eng, inst):
            cols = ff_cols(inst)
            w = cols[-1][1]
            l, fi = divmod(inst, 2)
            for half in range(2):
                n0, o0 = FF_T0[inst] + 30 * half, FF_O0[inst] + 30 * half
                s0 = (2 * inst + half) * HALF
                for a, b, _, u0, per in FF_SEGS[inst][half]:
                    for i in steps(eng, a, b):
                        t, o, s = Nth(i, 2, n0), Nth(i, 2, o0), Nth(i, 1, s0)
                        split_lo(eng, t + 2, width(n0 + 2, 2, a, b))
                        for m in range(per // 2):
                            mod_read(eng, Nth(i, per, u0 + m))
                        eng.wait_ge(acc_done, o.n(2))
                        eng.wait_ge(acc_free[o.odd], read_out(o))
                        eng.tensor_tensor(sf[:, 0:w], pair[(o + 1).odd][:, 0:w], sg[:, 0:w],
                                          ALU.mult).then_inc(acc_free[(o + 1).odd], 1)
                        for m in range(per // 2):
                            mod_read(eng, Nth(i, per, u0 + per // 2 + m))
                        eng.wait_ge(s_hi_done, s.n(1))
                        eng.tensor_tensor(s_lo[:, bass.ds(i, 1), 0:w].rearrange("p a t -> p (a t)"), sf[:, 0:w],
                                          s_hi[:, bass.ds(i, 1), 0:w].bitcast(F32).rearrange("p a t -> p (a t)"),
                                          ALU.subtract).then_inc(s_lo_done, 1)
                        split_lo(eng, t + 3, width(n0 + 3, 2, a, b))
                if half == 0:
                    gate_vectors(eng, l, 2 * fi)
                for a, b in ((0, 3), (3, 4)):
                    for i in steps(eng, a, b):
                        for j in range(2):
                            t, o = Nth(i, 2, n0 + 2 * HALF + j), Nth(i, 2, o0 + 2 * HALF + j)
                            residual(eng, o, Nth(i, 2, j).n(), cols)
                            split_lo(eng, t + 2, width(n0 + 2 * HALF + 2 + j, 2, a, b))

        def mo(l, kind, c=0):
            return Nth(0, 1, MIX_O0[l] + MIX_OUT[kind, c])

        def mix_outs(l, n):
            kind, c = MIX_ORDER[n]
            return [mo(l, "y", 2 * c), mo(l, "y", 2 * c + 1)] if kind == "wpool" else [mo(l, kind, c)]

        def mix_last_out(l, n):
            if n < T_Q:
                return mix_outs(l, n)[-1]
            if n < T_KV:
                return mo(l, "q") + (n - T_Q)
            return mo(l, "kv", n - T_KV) + 5

        H_STEPS = 4 + 2 * MLA_HEADS

        def head_step(l, what, h=0):
            return H_STEPS * l + {"na": 0, "q": 4, "k": 4 + MLA_HEADS}[what] + h

        def swapped_product(eng, t, o, chunks, stat, moving):
            eng.wait_ge(w_lo_done, t.n(1))
            eng.wait_ge(acc_free[o.odd], o.half())
            for tc in range(TOK // P):
                dst = pair[o.odd][:, tc * P:(tc + 1) * P]
                for k in range(chunks):
                    (ah, al), (wh, wl) = stat(k, tc), moving(k)
                    if len(wh.shape) == 3:
                        d = dst.rearrange("p (a b) -> p a b", a=wh.shape[1])
                    else:
                        d = dst
                    eng.matmul(d, ah, wh, start=k == 0, stop=False)
                    eng.matmul(d, ah, wl, start=False, stop=False)
                    last = eng.matmul(d, al, wh, start=False, stop=k == chunks - 1)
            last.then_inc(acc_done, 1)

        def head_sum(eng, s, squares_out, rows, ones_ap, rot=None):
            eng.wait_ge(acc_free[squares_out.odd], read_out(squares_out))
            if not (s.stride == 0 and s.const < 1):
                eng.wait_ge(h_std, s.n())
            for a, b in PARTS:
                last = eng.matmul(psum2[0:rows, a:b], ones_ap, sq[0:rows, 0, a:b], start=True, stop=True)
            if rot is not None:
                lhs, rhs = rot
                eng.wait_ge(h_done, s.n(-1))
                last = eng.matmul(pmid[0:QK, s.odd * 512:s.odd * 512 + SEQ], lhs, rhs, start=True, stop=True)
            last.then_inc(h_sum, 1)

        def head_std(eng, s, rows, dim):
            eng.wait_ge(h_sum, s.n(1))
            if not (s.stride == 0 and s.const < 1):
                eng.wait_ge(h_rstd, s.n())
            eng.activation(sq[0:rows, 1, :], psum2[0:rows, 0:TOK], ACT.Sqrt, bias=eps[0:rows, 0:1],
                           scale=1.0 / dim).then_inc(h_std, 1)

        def mix_pe(eng, l):
            t0 = MIX_T0[l]
            q = X_NORM[l, 1]
            norm_pe(eng, q)
            lo0 = norm_bases(q)[0]
            na_out = [mo(l, "qn", 0), mo(l, "qn", 1), mo(l, "kn", 0), mo(l, "kn", 1)]

            def na_sum(m):
                head_sum(eng, Nth(0, 1, head_step(l, "na", m)), na_out[m], P, blk[:, :])

            for n, (kind, c) in enumerate(MIX_ORDER):
                t, outs = Nth(0, 1, t0 + n), mix_outs(l, n)
                if kind == "wpool":
                    eng.wait_ge(pool_lo_done, 2 * l + c + 1)
                    for g in range(2):
                        r = slice(g * 64, g * 64 + 64)
                        product(eng, t, outs[g], 1, lambda k: (w_hi[r, t.odd, 0:P], w_lo[r, t.odd, 0:P]),
                                lambda k, a, b: (pool_hi[r, a:b], pool_lo[r, a:b]), PARTS)
                elif kind == "vn":
                    swapped_product(eng, t, outs[0], KD,
                                    lambda k, tc: (h_hi[:, k, tc * P:(tc + 1) * P], h_lo[:, k, tc * P:(tc + 1) * P]),
                                    wtile(t))
                else:
                    before = (lambda k: eng.wait_ge(n_lo, lo0 + k + 1)) if n == 0 else None
                    product(eng, t, outs[0], KD, wtile(t), h_moving, PARTS, before)
                if (kind, c) == ("ckv", 0):
                    norm_pe(eng, CQ_NORM[l])
                if (kind, c) == ("kr", 0):
                    norm_pe(eng, CK_NORM[l])
                if (kind, c) in (("qn", 1), ("kn", 0), ("kn", 1), ("vn", 0)):
                    na_sum({("qn", 1): 0, ("kn", 0): 1, ("kn", 1): 2, ("vn", 0): 3}[kind, c])
            for i in steps(eng, 0, MLA_HEADS // 2):
                for j in range(2):
                    t, o = Nth(i, 2, t0 + T_Q + j), Nth(i, 2, mo(l, "q").const + j)
                    product(eng, t, o, RQ, wtile(t, QK), lambda k, a, b: (cq_hi[:, k, a:b], cq_lo[:, k, a:b]), PARTS)
                for j in range(2):
                    head_sum(eng, Nth(i, 2, head_step(l, "q", j)), Nth(i, 2, mo(l, "q").const + j), QK,
                             ones[0:QK, 0:QK], (perm_q[0:QK, :], q_f[0:QK, bass.ds(i * 2 + j, 1), 0:SEQ]
                                                .rearrange("p a t -> p (a t)")))
            eng.wait_ge(kr_spread, MLA_HEADS * (l + 1))
            eng.wait_ge(kr_sq, l + 1)
            ck_moving = lambda k, a, b: (ck_hi[:, k, a:b], ck_lo[:, k, a:b])
            k_sum = lambda h: head_sum(eng, Nth(0, 1, head_step(l, "k", h)), mo(l, "kv", h // 4) + h % 4, QK,
                                       ones[0:QK, 0:QK], (perm_k[0:QK, :], k_f[0:QK, h, 0:SEQ]))
            for c in range(2):
                t = Nth(0, 1, t0 + T_KV + c)
                view = [w[:, t.odd, 0:RK * 4 * P].rearrange("p (k h m) -> p k h m", k=RK, m=P) for w in (w_hi, w_lo)]
                for h in range(4):
                    product(eng, t, mo(l, "kv", c) + h, RK, lambda k: (view[0][:, k, h, :], view[1][:, k, h, :]),
                            ck_moving, PARTS)
                    if h:
                        k_sum(4 * c + h - 1)
                for v in range(2):
                    swapped_product(eng, t, mo(l, "kv", c) + (4 + v), RK,
                                    lambda k, tc: (ck_hi[:, k, tc * P:(tc + 1) * P], ck_lo[:, k, tc * P:(tc + 1) * P]),
                                    lambda k: tuple(x[:, k, 2 * v:2 * v + 2, NOPE:] for x in view))
                    if v == 0:
                        k_sum(4 * c + 3)
            attention_pe(eng, l)
            cols = y_cols(l)
            for i0, i1 in ((0, 1), (1, KD // 2)):
                for i in steps(eng, i0, i1):
                    for j in range(2):
                        t, o = Nth(i, 2, t0 + T_WO + j), Nth(i, 2, mo(l, "wo").const + j)
                        before = (lambda k: eng.wait_ge(y_lo_done, KD * l + k + 1)) if i0 == 0 and j == 0 else None
                        product(eng, t, o, KD, wtile(t), h_moving, cols, before)

        def y_cols(l):
            return PARTS if l < DEPTH - 1 else PARTS[:1]

        def mix_tile_load(eng, l, n):
            if isinstance(n, Nth):
                t = n
                h = n.n(-(MIX_T0[l] + T_Q))
                src = w_q_up[l].rearrange("(k p) (h m) -> p k h m", p=P, m=QK)[:, :, h, :]
                load(eng, t, src, w_raw[:, t.odd, 0:RQ * QK].rearrange("p (k m) -> p k m", m=QK))
                return
            t = Nth(0, 1, MIX_T0[l] + n)
            if n >= T_KV:
                c = n - T_KV
                src = w_kv_up[l].rearrange("(k p) n -> p k n", p=P)[:, :, c * 4 * P:(c + 1) * 4 * P]
                load(eng, t, src, w_raw[:, t.odd, 0:RK * 4 * P].rearrange("p (k m) -> p k m", k=RK))
                return
            kind, c = MIX_ORDER[n]
            if kind == "wpool":
                eng.wait_ge(w_lo_done, t.n(-1))
                for half in range(2):
                    eng.dma_start(w_raw[:, t.odd, half * 64:half * 64 + 64],
                                  w_pool[l, 2 * c:2 * c + 2].rearrange("g c d -> (g c) d"))\
                       .then_inc(w_loaded_pool, 16)
                eng.wait_ge(w_loaded_pool, 32 * (2 * l + c + 1))
                eng.sem_inc(w_loaded[t.odd], 16)
                return
            col = MIX_COL[kind] + c * P
            src = w_in[l].rearrange("(k p) n -> p k n", p=P)[:, :, col:col + P]
            load(eng, t, src, w_raw[:, t.odd, 0:KD * P].rearrange("p (k m) -> p k m", m=P))

        def wo_load(eng, l, t):
            d = t.n(-(MIX_T0[l] + T_WO))
            src = w_out[l].rearrange("(k p) (d m) -> p k d m", p=P, m=P)[:, :, d, :]
            load(eng, t, src, w_raw[:, t.odd, 0:KD * P].rearrange("p (k m) -> p k m", m=P))

        def mix_sp(eng, l):
            for n in range(2, T_Q):
                if n == 2:
                    eng.wait_ge(acc_done, MIX_O0[l])
                    eng.dma_start(inv_cnt[:, :], k_invcnt[:, 0, :]).then_inc(inv_loaded, 16)
                mix_tile_load(eng, l, n)
                if MIX_ORDER[n] == ("cq", 3):
                    eng.wait_ge(pool_lo_done, 2 * l + 1)
                    eng.dma_start(inv_cnt[:, :], k_invcnt[:, 1, :]).then_inc(inv_loaded, 16)
            for i in steps(eng, 0, MLA_HEADS // 2):
                for j in range(2):
                    mix_tile_load(eng, l, Nth(i, 2, MIX_T0[l] + T_Q + j))
            for c in range(2):
                mix_tile_load(eng, l, T_KV + c)
            nb = att_chunks(l)
            eng.wait_ge(h_done, H_STEPS * (l + 1))
            eng.wait_ge(bias_stored, 16 * bias_dmas)
            for i in range(2):
                for j in range(2):
                    if i:
                        eng.wait_ge(a_max, ATT_C0[l] + 4 * nb + (nb // 2) * (j + 1))
                    eng.dma_start(na_tt[:, j, :], na_bias[l, 2 * i + j]).then_inc(tt_loaded[j], 16)
            eng.wait_ge(a_out, (ATT_C0[l] + 6 * nb) // 2)
            for i in steps(eng, 0, KD // 2):
                for j in range(2):
                    wo_load(eng, l, Nth(i, 2, MIX_T0[l] + T_WO + j))

        def evacuate(eng, o, dst, scale=None):
            eng.wait_ge(acc_done, o.n(1))
            src = pair[o.odd][:, 0:TOK]
            if len(dst.shape) == 3:
                src = src.rearrange("p (a b) -> p a b", a=dst.shape[1])
            eng.tensor_copy(dst, src).then_inc(acc_free[o.odd], 1)

        def values(l, m):
            o = mo(l, "kv", m // 2) + (4 + m % 2)
            return o, pair[o.odd][:, 0:TOK].rearrange("p (a b) -> p a b", b=P), slice(m * P, (m + 1) * P)

        def values_hi(eng, l, m):
            o, src, at = values(l, m)
            eng.wait_ge(acc_done, o.n(1))
            eng.activation(v_hi[:, :, at], src, ACT.Copy).then_inc(v_hi_done, 1)

        def values_lo(eng, l, m):
            o, src, at = values(l, m)
            eng.wait_ge(v_hi_done, MLA_HEADS // 2 * l + m + 1)
            eng.tensor_tensor(v_lo[:, :, at], src, v_hi[:, :, at].bitcast(F32), ALU.subtract).then_inc(acc_free[o.odd], 1)

        def mix_act(eng, l):
            t0 = MIX_T0[l]
            norm_act(eng, X_NORM[l, 1])
            eng.preload_act_table_set("sqrt_and_others")
            na_out = [mo(l, "qn", 0), mo(l, "qn", 1), mo(l, "kn", 0), mo(l, "kn", 1)]
            for n, (kind, c) in enumerate(MIX_ORDER):
                t, outs = Nth(0, 1, t0 + n), mix_outs(l, n)
                if kind == "wpool":
                    eng.wait_ge(pool_step, pool_steps(l, c + 1))
                    for a, b, at in ((0, SEQ, 2 * PAD + CTX), (SEQ, TOK, PAD)):
                        eng.activation(pool_hi[:, a:b], ps[0][:, at:at + b - a], ACT.Copy).then_inc(pool_hi_done, 1)
                if kind == "kr":
                    eng.wait_ge(acc_done, outs[0].n(1))
                    eng.activation(kr_f[NOPE:QK, :], pair[outs[0].odd][0:ROPE, 0:TOK], ACT.Copy)\
                       .then_inc(acc_free[outs[0].odd], 1)
                if kind in ("qn", "kn"):
                    m = c + 2 * (kind == "kn")
                    eng.wait_ge(acc_done, outs[0].n(1))
                    eng.activation(na_f[:, m, :], pair[outs[0].odd][:, 0:TOK], ACT.Copy)
                    if m:
                        head_std(eng, Nth(0, 1, head_step(l, "na", m - 1)), P, NA_DIM)
                    eng.activation(sq[:, 0, :], pair[outs[0].odd][:, 0:TOK], ACT.Square)\
                       .then_inc(acc_free[outs[0].odd], 1)
                split_hi(eng, t + 2, WIDTHS[t0 + n + 2], outs[-1])
                if (kind, c) == ("vn", 0):
                    head_std(eng, Nth(0, 1, head_step(l, "na", 3)), P, NA_DIM)
                if (kind, c) == ("cq", 5):
                    norm_act(eng, CQ_NORM[l])
                if (kind, c) == ("ckv", 1):
                    norm_act(eng, CK_NORM[l])
            for a, b in ((0, 3), (3, 4)):
                for i in steps(eng, a, b):
                    for j in range(2):
                        t, o = Nth(i, 2, t0 + T_Q + j), Nth(i, 2, mo(l, "q").const + j)
                        s = Nth(i, 2, head_step(l, "q", j))
                        eng.wait_ge(acc_done, o.n(1))
                        eng.activation(q_f[0:QK, bass.ds(i * 2 + j, 1), :].rearrange("p a t -> p (a t)"),
                                       pair[o.odd][0:QK, 0:TOK], ACT.Copy)
                        if j == 1:
                            head_std(eng, s + (-1), QK, QK)
                        eng.activation(sq[0:QK, 0, :], pair[o.odd][0:QK, 0:TOK], ACT.Square)\
                           .then_inc(acc_free[o.odd], 1)
                        split_hi(eng, t + 2, width(t0 + T_Q + j + 2, 2, a, b), o)
                    head_std(eng, s, QK, QK)
            eng.activation(sq[NOPE:QK, 0, :], kr_f[NOPE:QK, :], ACT.Square).then_inc(kr_sq, 1)
            for h in range(MLA_HEADS):
                o, s = mo(l, "kv", h // 4) + h % 4, Nth(0, 1, head_step(l, "k", h))
                eng.wait_ge(acc_done, o.n(1))
                eng.activation(k_f[0:NOPE, h, :], pair[o.odd][0:NOPE, 0:TOK], ACT.Copy)
                if h % 4:
                    head_std(eng, s + (-1), QK, QK)
                eng.activation(sq[0:NOPE, 0, :], pair[o.odd][0:NOPE, 0:TOK], ACT.Square).then_inc(acc_free[o.odd], 1)
                if h % 4 == 3:
                    values_hi(eng, l, h // 2 - 1)
                    head_std(eng, s, QK, QK)
                    values_hi(eng, l, h // 2)
            attention_act(eng, l)
            w = y_cols(l)[-1][1]
            for n in range(2):
                split_hi(eng, Nth(0, 1, t0 + T_WO + n), KD * P, None)
            for k in range(KD):
                eng.activation(h_hi[:, k, 0:w], y_f[:, k, 0:w] if k < 6 else yp_f[:, k - 6, 0:w], ACT.Copy)\
                   .then_inc(y_hi_done, 1)
            for a, b in ((0, 3), (3, 4)):
                for i in steps(eng, a, b):
                    for j in range(2):
                        t, o = Nth(i, 2, t0 + T_WO + j), Nth(i, 2, mo(l, "wo").const + j)
                        split_hi(eng, t + 2, width(t0 + T_WO + 2 + j, 2, a, b), o)

        def head_scale(eng, s, which, h, l, first_step):
            x_f, gain = (q_f, V_GQ) if which == "q" else (k_f, V_GK)
            g = vecs[0:QK, l, gain:gain + 1]
            head = lambda a, b: x_f[0:QK, bass.ds(h, 1), a:b].rearrange("p a t -> p (a t)")
            eng.wait_ge(h_std, s.n(1))
            eng.wait_ge(h_done, s.n())
            eng.reciprocal(rstd[0:QK, :], sq[0:QK, 1, :]).then_inc(h_rstd, 1)
            eng.tensor_tensor(rot_s[0:QK, :], pmid[0:QK, s.odd * 512:s.odd * 512 + SEQ], sin[0:QK, :], ALU.mult)\
               .then_inc(h_step, 1)
            eng.scalar_tensor_tensor(head(0, SEQ), head(0, SEQ), g, cos[0:QK, :], ALU.mult, ALU.mult).then_inc(h_step, 1)
            eng.tensor_scalar(head(SEQ, TOK), head(SEQ, TOK), g, None, ALU.mult).then_inc(h_step, 1)
            eng.wait_ge(h_step, first_step.n(3))
            eng.tensor_tensor(head(0, SEQ), head(0, SEQ), rot_s[0:QK, :], ALU.add).then_inc(h_step, 1)
            eng.wait_ge(h_rstd, s.n(1))
            eng.wait_ge(h_step, first_step.n(4))
            eng.tensor_tensor(head(0, TOK), head(0, TOK), rstd[0:QK, :], ALU.mult).then_inc(h_done, 1)

        def na_scale(eng, l, m):
            s = head_step(l, "na", m)
            gain = V_GNQ if m < 2 else V_GNK
            eng.wait_ge(h_std, s + 1)
            if s:
                eng.wait_ge(h_done, s)
            eng.reciprocal(rstd[:, :], sq[:, 1, :]).then_inc(h_rstd, 1)
            eng.wait_ge(h_rstd, s + 1)
            eng.scalar_tensor_tensor(na_f[:, m, :], na_f[:, m, :], vecs[:, l, gain:gain + 1], rstd[:, :],
                                     ALU.mult, ALU.mult).then_inc(h_done, 1)

        def mix_dve(eng, l):
            t0 = MIX_T0[l]
            mod_vectors(eng, l, 1)
            eng.wait_ge(gain_scaled, 2)
            for dst, gain in ((perm_q, V_GQ), (perm_k, V_GK)):
                eng.tensor_scalar(dst[0:QK, :], perm[0:QK, :], vecs[0:QK, l, gain:gain + 1], None, ALU.mult)\
                   .then_inc(perm_ready, 1)
            norm_dve(eng, X_NORM[l, 1])
            for n, (kind, c) in enumerate(MIX_ORDER):
                t, outs = Nth(0, 1, t0 + n), mix_outs(l, n)
                if kind == "pool":
                    o = outs[0]
                    eng.wait_ge(acc_done, o.n(1))
                    eng.wait_ge(pads_set, 3 * (2 * l + c + 1))
                    eng.tensor_copy(pu[:, PAD:PAD + CTX], pair[o.odd][:, SEQ:TOK])
                    eng.tensor_copy(pu[:, 2 * PAD + CTX:2 * PAD + CTX + SEQ], pair[o.odd][:, 0:SEQ])\
                       .then_inc(acc_free[o.odd], 1)
                elif kind == "wpool":
                    eng.wait_ge(pool_hi_done, 2 * (2 * l + c + 1))
                    for a, b, at in ((0, SEQ, 2 * PAD + CTX), (SEQ, TOK, PAD)):
                        last = eng.tensor_tensor(pool_lo[:, a:b], ps[0][:, at:at + b - a],
                                                 pool_hi[:, a:b].bitcast(F32), ALU.subtract)
                    last.then_inc(pool_lo_done, 1)
                    for g in range(2):
                        o, r = outs[g], slice(g * 64, g * 64 + 64)
                        eng.wait_ge(acc_done, o.n(1))
                        eng.tensor_scalar(yp_f[r, c, :], pair[o.odd][r, 0:TOK], vecs[r, l, V_PSC + c:V_PSC + c + 1],
                                          None, ALU.mult).then_inc(acc_free[o.odd], 1)
                elif kind == "cq":
                    evacuate(eng, outs[0], cq_f[:, c, :])
                elif kind == "ckv":
                    evacuate(eng, outs[0], ck_f[:, c, :])
                elif kind == "vn":
                    evacuate(eng, outs[0], vn_f[:, :, c * P:(c + 1) * P])
                split_lo(eng, t + 2, WIDTHS[t0 + n + 2])
                if (kind, c) == ("cq", 5):
                    norm_dve(eng, CQ_NORM[l])
                if (kind, c) == ("ckv", 1):
                    norm_dve(eng, CK_NORM[l])
                if (kind, c) in (("qn", 1), ("kn", 0), ("kn", 1), ("vn", 0)):
                    na_scale(eng, l, {("qn", 1): 0, ("kn", 0): 1, ("kn", 1): 2, ("vn", 0): 3}[kind, c])
            for a, b in ((0, 3), (3, 4)):
                for i in steps(eng, a, b):
                    for j in range(2):
                        split_lo(eng, Nth(i, 2, t0 + T_Q + j + 2), width(t0 + T_Q + j + 2, 2, a, b))
                    for j in range(2):
                        head_scale(eng, Nth(i, 2, head_step(l, "q", j)), "q", i * 2 + j, l,
                                   Nth(i, 8, 4 * (2 * MLA_HEADS * l + j)))
            for h in range(MLA_HEADS):
                c = h // 4
                if h % 4 == 3:
                    for v in range(2):
                        if v == 1:
                            head_scale(eng, Nth(0, 1, head_step(l, "k", h)), "k", h, l,
                                       Nth(0, 1, 4 * (2 * MLA_HEADS * l + MLA_HEADS + h)))
                        values_lo(eng, l, 2 * c + v)
                else:
                    head_scale(eng, Nth(0, 1, head_step(l, "k", h)), "k", h, l,
                               Nth(0, 1, 4 * (2 * MLA_HEADS * l + MLA_HEADS + h)))
            attention_dve(eng, l)
            w, cols = y_cols(l)[-1][1], y_cols(l)
            for n in range(2):
                split_lo(eng, Nth(0, 1, t0 + T_WO + n), KD * P)
            for k in range(KD):
                eng.wait_ge(y_hi_done, KD * l + k + 1)
                eng.tensor_tensor(h_lo[:, k, 0:w], y_f[:, k, 0:w] if k < 6 else yp_f[:, k - 6, 0:w],
                                  h_hi[:, k, 0:w].bitcast(F32), ALU.subtract).then_inc(y_lo_done, 1)
            gate_vectors(eng, l, 1)
            for a, b in ((0, 3), (3, 4)):
                for i in steps(eng, a, b):
                    for j in range(2):
                        t, o = Nth(i, 2, t0 + T_WO + j), Nth(i, 2, mo(l, "wo").const + j)
                        residual(eng, o, Nth(i, 2, j).n(), cols)
                        split_lo(eng, t + 2, width(t0 + T_WO + 2 + j, 2, a, b))

        def pool_steps(l, chunks):
            return 12 * l + (0, 5, 12)[chunks]

        def mix_pool(eng, l):
            done = pool_steps(l, 0)
            for c in range(2):
                first = mo(l, "pool", 0).const if c == 0 else mo(l, "y", 1).const + 1
                eng.wait_ge(acc_done, first)
                if c == 1:
                    eng.wait_ge(pool_lo_done, 2 * l + 1)
                for at in (0, PAD + CTX, 2 * PAD + CTX + SEQ):
                    eng.memset(pu[:, at:at + PAD], 0.0).then_inc(pads_set, 1)
                o = mo(l, "pool", c)
                eng.wait_ge(acc_free[o.odd], read_out(o))
                eng.wait_ge(pads_set, 3 * (2 * l + c + 1))
                src, cur, lo, hi = pu, 0, 0, POOLW
                for reach in ((1, 1) if c == 0 else (1, 1, 2, 4)):
                    back, ahead = (1, 0) if src is pu else (reach, reach)
                    lo, hi = lo + back, hi - ahead
                    eng.tensor_tensor(ps[cur][:, lo:hi], src[:, lo - back:hi - back], src[:, lo + ahead:hi + ahead],
                                      ALU.add).then_inc(pool_step, 1)
                    done += 1
                    eng.wait_ge(pool_step, done)
                    src, cur = ps[cur], 1 - cur
                eng.wait_ge(inv_loaded, 16 * (2 * l + c + 1))
                a, b = PAD, POOLW - PAD
                for g in range(2):
                    r = slice(g * 64, g * 64 + 64)
                    eng.tensor_tensor(ps[0][r, a:b], ps[g][r, a:b], inv_cnt[r, a:b], ALU.mult).then_inc(pool_step, 1)
                    done += 1
                eng.wait_ge(pool_step, done)
                eng.tensor_tensor(ps[0][:, a:b], ps[0][:, a:b], pu[:, a:b], ALU.subtract).then_inc(pool_step, 1)
                done += 1
            o = mo(l, "vn", 1)
            eng.wait_ge(acc_done, o.n(1))
            eng.wait_ge(acc_free[mo(l, "kr").odd], read_out(mo(l, "kr")))
            for h in range(MLA_HEADS):
                eng.tensor_copy(k_f[NOPE:QK, h, :], kr_f[NOPE:QK, :]).then_inc(kr_spread, 1)
            attention_pool(eng, l)

        def att_chunks(l):
            return 12 if l < DEPTH - 1 else 8

        ATT_C0 = [0, 6 * 12]
        ATT_SPLITS = 21

        def chunk_info(l, c):
            pair_n, c = divmod(c, att_chunks(l))
            per = att_chunks(l) // 2
            j, q0 = c // per, (c % per) * P
            kind, i = ("mla", pair_n) if pair_n < 4 else ("na", pair_n - 4)
            return kind, i, j, q0, (PARTS if q0 < SEQ else PARTS[1:])

        def n_chunks(l):
            return 6 * att_chunks(l)

        def att_group(l, c):
            kind, i, j, q0, _ = chunk_info(l, c)
            return (2 * i + j, q0 == 0) if kind == "mla" else (MLA_HEADS + i, q0 == 0 and j == 0)

        def group_first(l, g):
            per = att_chunks(l) // 2
            return g * per if g < MLA_HEADS else (MLA_HEADS + 2 * (g - MLA_HEADS)) * per

        GROUPS = MLA_HEADS + 2

        def splits(g):
            qh, ql, kh, kl = att_set[g % 2]
            if g < MLA_HEADS:
                return 2 * g, [(q_f[0:QK, g, :], qh[0:QK, :], ql[0:QK, :]), (k_f[0:QK, g, :], kh[0:QK, :], kl[0:QK, :])]
            i = g - MLA_HEADS
            out = [(na_f[:, i, :], qh[:, :], ql[:, :]), (na_f[:, i + 2, :], kh[:, :], kl[:, :])]
            if i == 0:
                out.append((vn_f[:, :, :], vn_hi[:, :, :], vn_lo[:, :, :]))
            return 2 * MLA_HEADS + 3 * i, out

        def own_scores(l, c):
            kind, _, _, q0, _ = chunk_info(l, c)
            return kind == "mla" or q0 >= SEQ

        def bias_steps(l, c):
            return sum(2 for layer in range(l + 1) for x in range(c if layer == l else n_chunks(layer))
                       if not own_scores(layer, x))

        def wait_if(eng, semaphore, value):
            if value > 0:
                eng.wait_ge(semaphore, value)

        def attention_pe(eng, l):
            c0, n = ATT_C0[l], n_chunks(l)
            for v in (4, 5):
                o = mo(l, "kv", 1) + v
                eng.wait_ge(acc_free[o.odd], read_out(o))
            for s in range(n + 4):
                if s < n:
                    kind, i, j, q0, keys = chunk_info(l, s)
                    g, new = att_group(l, s)
                    qh, ql, kh, kl = att_set[g % 2]
                    rows = slice(0, QK) if kind == "mla" else slice(j * NA_DIM, (j + 1) * NA_DIM)
                    if new:
                        eng.wait_ge(a_lo, ATT_SPLITS * l + splits(g)[0] + len(splits(g)[1]))
                    wait_if(eng, a_exp, c0 + s - 1)
                    for a, b in keys:
                        dst, q = pair[s % 2][:, a:b], slice(q0, q0 + P)
                        eng.matmul(dst, qh[rows, q], kh[rows, a:b], start=True, stop=False)
                        eng.matmul(dst, qh[rows, q], kl[rows, a:b], start=False, stop=False)
                        last = eng.matmul(dst, ql[rows, q], kh[rows, a:b], start=False, stop=True)
                    last.then_inc(a_s, 1)
                if 2 <= s < n + 2:
                    c = s - 2
                    keys = chunk_info(l, c)[4]
                    eng.wait_ge(a_prob, c0 + c + 1)
                    wait_if(eng, a_ptl, c0 + c)
                    for k in range(keys[0][0] // P, TOK // P):
                        last = eng.transpose(pmid[:, k * P:(k + 1) * P], prob[:, c % 3, k * P:(k + 1) * P], ident[:, :])
                    last.then_inc(a_t, 1)
                if s >= 4:
                    b, part = (s - 4) // 2, s % 2
                    kind, i, j, q0, keys = chunk_info(l, 2 * b)
                    kc = [k for k in range(TOK // P) if k * P >= keys[0][0]]
                    if part == 0:
                        eng.wait_ge(a_ptl, c0 + 2 * b + 2)
                        wait_if(eng, a_out, c0 // 2 + b - 1)
                    vh, vl = (v_hi, v_lo) if kind == "mla" else (vn_hi, vn_lo)
                    dst = psum2[:, (b % 2) * 512:(b % 2) * 512 + 2 * P].rearrange("p (c q) -> p c q", c=2)
                    slots = slice(2 * (b % 2), 2 * (b % 2) + 2)
                    for k in kc[:len(kc) // 2] if part == 0 else kc[len(kc) // 2:]:
                        ph, pl = pt_hi[:, k, slots, :], pt_lo[:, k, slots, :]
                        eng.matmul(dst, vh[:, k, i * P:(i + 1) * P], ph, start=k == kc[0], stop=False)
                        eng.matmul(dst, vh[:, k, i * P:(i + 1) * P], pl, start=False, stop=False)
                        last = eng.matmul(dst, vl[:, k, i * P:(i + 1) * P], ph, start=False, stop=k == kc[-1])
                    if part:
                        last.then_inc(a_pv, 1)

        def attention_act(eng, l):
            c0, n = ATT_C0[l], n_chunks(l)
            eng.preload_act_table_set("exp_and_others")
            eng.wait_ge(acc_done, mo(l, "kv", 1).n(6))
            eng.wait_ge(h_done, H_STEPS * (l + 1))

            def split(g):
                for src, hi, lo in splits(g)[1]:
                    eng.activation(hi, src, ACT.Copy).then_inc(a_hi, 1)

            split(0)
            for s in range(n + 5):
                if s < n:
                    kind, i, j, q0, keys = chunk_info(l, s)
                    a, b = keys[0][0], TOK
                    eng.wait_ge(a_max, c0 + s + 1)
                    wait_if(eng, a_t, c0 + s - 2)
                    eng.activation(prob[:, s % 3, a:b], pair[s % 2][:, a:b] if own_scores(l, s) else prob[:, s % 3, a:b],
                                   ACT.Exp, bias=stat[:, s % 2, 0:1], accum_out=stat[:, s % 2, 1:2]).then_inc(a_exp, 1)
                if 2 <= s < n + 2:
                    c = s - 2
                    k0 = chunk_info(l, c)[4][0][0] // P
                    eng.wait_ge(a_t, c0 + c + 1)
                    if c >= 4:
                        eng.wait_ge(a_pv, c0 // 2 + (c - 4) // 2 + 1)
                    eng.activation(pt_hi[:, k0:, c % 4, :], pmid[:, k0 * P:TOK].rearrange("p (k q) -> p k q", q=P),
                                   ACT.Copy).then_inc(a_pth, 1)
                if s >= 6 and s % 2 == 0:
                    b = (s - 6) // 2
                    kind, i, j, q0, _ = chunk_info(l, 2 * b)
                    r, bank = slice(j * 64, j * 64 + 64), (b % 2) * 512
                    eng.wait_ge(a_pv, c0 // 2 + b + 1)
                    eng.activation(y_f[r, i if kind == "mla" else 4 + i, q0:q0 + 2 * P], psum2[r, bank:bank + 2 * P],
                                   ACT.Copy).then_inc(a_out, 1)
                if s < n:
                    g, new = att_group(l, s)
                    if new and g + 1 < GROUPS:
                        eng.wait_ge(a_s, c0 + s)
                        split(g + 1)

        def attention_pool(eng, l):
            n = n_chunks(l)

            def split(g):
                first, operands = splits(g)
                for m, (src, hi, lo) in enumerate(operands):
                    eng.wait_ge(a_hi, ATT_SPLITS * l + first + m + 1)
                    eng.tensor_tensor(lo, src, hi.bitcast(F32), ALU.subtract).then_inc(a_lo, 1)

            split(0)
            for s in range(n):
                g, new = att_group(l, s)
                if new and g + 1 < GROUPS:
                    split(g + 1)

        def attention_dve(eng, l):
            c0, n = ATT_C0[l], n_chunks(l)
            for s in range(n + 2):
                if s < n:
                    kind, i, j, q0, keys = chunk_info(l, s)
                    a, b = keys[0][0], TOK
                    scores = pair[s % 2][:, a:b]
                    eng.wait_ge(a_s, c0 + s + 1)
                    if not own_scores(l, s):
                        first = (BIAS_SLOTS // 2 - 1 - 2 * (q0 // P)) * GRID_W
                        if q0 == 0:
                            eng.wait_ge(tt_loaded[j], 16 * (2 * l + i + 1))
                        eng.wait_ge(a_t, c0 + s - 2)
                        eng.tensor_tensor(prob[:, s % 3, 0:SEQ], pair[s % 2][:, 0:SEQ], na_tt[:, j, first:first + SEQ],
                                          ALU.add).then_inc(a_bias, 1)
                        eng.tensor_copy(prob[:, s % 3, SEQ:TOK], pair[s % 2][:, SEQ:TOK]).then_inc(a_bias, 1)
                        eng.wait_ge(a_bias, bias_steps(l, s) + 2)
                        scores = prob[:, s % 3, :]
                    eng.tensor_reduce(stat[:, s % 2, 0:1], scores, AX_X, ALU.max, negate=True).then_inc(a_max, 1)
                if 1 <= s <= n:
                    c = s - 1
                    p = prob[:, c % 3, chunk_info(l, c)[4][0][0]:TOK]
                    eng.wait_ge(a_exp, c0 + c + 1)
                    eng.reciprocal(stat[:, c % 2, 2:3], stat[:, c % 2, 1:2]).then_inc(a_rsum, 1)
                    eng.wait_ge(a_rsum, c0 + c + 1)
                    eng.tensor_scalar(p, p, stat[:, c % 2, 2:3], None, ALU.mult).then_inc(a_prob, 1)
                if s >= 2:
                    c = s - 2
                    k0 = chunk_info(l, c)[4][0][0] // P
                    eng.wait_ge(a_pth, c0 + c + 1)
                    eng.tensor_tensor(pt_lo[:, k0:, c % 4, :], pmid[:, k0 * P:TOK].rearrange("p (k q) -> p k q", q=P),
                                      pt_hi[:, k0:, c % 4, :].bitcast(F32), ALU.subtract).then_inc(a_ptl, 1)

        blocks = ["ff0"] if stop == "ff0" else ["ff0", "mix0"] if stop == "mix0" else ["ff0", "mix0", "ff1", "ff2", "mix1", "ff3"]
        bias_dmas = 2 * (DEPTH * NA_HEADS + WIN_C - 1)
        o_final = {"ff0": FF_O0[0] + FF_TILES, "mix0": MIX_O0[0] + MIX_OUTS}.get(stop, O_END)
        block = ctx.enter_context(nc.Block())

        @block.sync
        def _(sp):
            sp.dma_start(ident[:, :], k_ident).then_inc(const_loaded, 16)
            sp.wait_ge(vec_zero, 1)
            sp.dma_start(vrows[V_C:V_C + KD, 0, :], c.rearrange("a (k p) -> (a k) p", p=P)).then_inc(vec_loaded, 16)
            sp.dma_start(vrows[V_C + KD:V_C + 2 * KD, 0, :], c_ctx.rearrange("(k p) -> k p", p=P))\
              .then_inc(vec_loaded, 16)
            for l in range(DEPTH):
                for row, v in ((V_BMOD, b_mod), (V_GCQ, g_cq), (V_GCKV, g_ckv), (V_PSC, pool_scale)):
                    src = v[l].rearrange("(k p) -> k p", p=P)
                    sp.dma_start(vrows[row:row + src.shape[0], l, :], src).then_inc(vec_loaded, 16)
                for row, v in ((V_GQ, g_mla_q), (V_GK, g_mla_k)):
                    sp.dma_start(vrows[row:row + 1, l, 0:QK], v[l:l + 1, :]).then_inc(vec_loaded, 16)
                for row, v in ((V_GNQ, g_na_q), (V_GNK, g_na_k)):
                    for a in (0, NA_DIM):
                        sp.dma_start(vrows[row:row + 1, l, a:a + NA_DIM], v[l:l + 1, :]).then_inc(vec_loaded, 16)
            for tc in range(TOK // P):
                src = x[0, tc * P:(tc + 1) * P, :] if tc < SEQ // P else ctx_in[0, tc * P - SEQ:(tc + 1) * P - SEQ, :]
                sp.dma_start(x_rows[:, tc, :], src).then_inc(x_loaded, 16)
            for dst, src in ((cos, k_cos), (sin, k_sin), (perm, k_perm)):
                sp.dma_start(dst[0:QK, :], src).then_inc(table_loaded, 16)
            first_loads(sp, blocks[0])
            for m in range(2):
                mod_load(sp, 0, Nth(m, 1, 0))
            for i in steps(sp, 1, START_MOD // 2):
                for m in range(2):
                    mod_load(sp, 0, Nth(i, 2, m))
            for b, following in zip(blocks, blocks[1:] + [None]):
                if b[:2] == "ff":
                    ff_sp(sp, int(b[2]), following)
                else:
                    mix_sp(sp, int(b[3]))
                    first_loads(sp, following)
            for tc in range(SEQ // P):
                sp.wait_ge(out_staged, tc + 1)
                sp.dma_start(out[0, tc * P:(tc + 1) * P, :], out_rows[:, tc % 2, :]).then_inc(out_stored[tc % 2], 16)
            for j in range(2):
                sp.wait_ge(out_stored[j], 16 * (SEQ // P // 2))

        N_VEC = 2 + DEPTH * 10

        @block.gpsimd
        def _(pool):
            pool.memset(vrows[:, :, :], 0.0).then_inc(vec_zero, 1)
            pool.memset(ones[:, :], 1.0).then_inc(const_set, 1)
            pool.memset(eps[:, :], EPS).then_inc(const_set, 1)
            pool.memset(blk[:, :], 0.0).then_inc(blk_set, 1)
            pool.wait_ge(blk_set, 1)
            for a in (0, 64):
                pool.memset(blk[a:a + 64, a:a + 64], 1.0).then_inc(blk_set, 1)
            pool.wait_ge(blk_set, 3)
            pool.memset(rot_s[:, :], NEG).then_inc(bias_neg, 1)
            pool.wait_ge(bias_neg, 1)
            fill = na_bias.rearrange("l h p (a n) -> a (l h) p n", a=2)
            for half in range(2):
                for i in steps(pool, 0, DEPTH * NA_HEADS):
                    pool.dma_start(fill[half, i], rot_s[:, 0:BIAS_SLOTS * GRID_W // 2]).then_inc(bias_filled, 16)
            pool.wait_ge(bias_filled, 16 * 2 * DEPTH * NA_HEADS)
            windows = na_bias.rearrange("l h (a q) (s c) -> a (l h) q s c", a=2, c=GRID_W)
            table = na_rpb.rearrange("l h r c -> (l h) r c")
            heads = DEPTH * NA_HEADS
            for par in range(2):
                slots = slice(1 - par, 1 - par + BIAS_SLOTS)
                for lh in steps(pool, 0, heads):
                    first, n = WIN_C // 2, GRID_W - WIN_C + 1
                    at = windows[par, lh, first, 0, 0]
                    dst = bass.AP(at.tensor, at.offset, [[BIAS_SLOTS * GRID_W + 1, n], [GRID_W, BIAS_SLOTS], [1, WIN_C]])
                    row = table[lh, slots, WIN_C - 1 - WIN_C // 2:2 * WIN_C - 1 - WIN_C // 2]
                    src = bass.AP(row.tensor, row.offset, [[0, n], [RPB_C, BIAS_SLOTS], [1, WIN_C]])
                    pool.dma_start(dst, src).then_inc(bias_stored, 16)
                for cq, start in [(q, 0) for q in range(WIN_C // 2)] + \
                        [(q, GRID_W - WIN_C) for q in range(GRID_W - WIN_C // 2 + 1, GRID_W)]:
                    off = start - cq + WIN_C - 1
                    pool.dma_start(windows[par, :, cq, :, start:start + WIN_C], table[:, slots, off:off + WIN_C])\
                        .then_inc(bias_stored, 16)
            for b in blocks:
                if b[:3] == "mix":
                    mix_pool(pool, int(b[3]))

        @block.tensor
        def _(pe):
            pe.wait_ge(const_loaded, 16)
            pe.wait_ge(vec_loaded, 16 * N_VEC)
            for l in range(DEPTH):
                pe.transpose(pair[l][:, 0:P], vrows[:, l, :], ident[:, :]).then_inc(acc_done, 1)
            pe.wait_ge(x_loaded, 16 * (TOK // P))
            for tc in range(TOK // P):
                o = 2 + tc
                pe.wait_ge(acc_free[o % 2], o // 2)
                for k in range(KD):
                    last = pe.transpose(pair[o % 2][:, k * P:(k + 1) * P], x_rows[:, tc, k * P:(k + 1) * P],
                                        ident[:, :])
                last.then_inc(acc_done, 1)
            pe.wait_ge(cs_ready, 2)
            pe.wait_ge(const_set, 2)
            for m in range(2):
                mod_product(pe, Nth(m, 1, 0))
            for i in steps(pe, 1, START_MOD // 2):
                for m in range(2):
                    mod_product(pe, Nth(i, 2, m))
            for b in blocks:
                if b[:2] == "ff":
                    inst = int(b[2])
                    norm_pe(pe, X_NORM[inst // 2, 2 * (inst % 2)])
                    ff_pe(pe, inst)
                else:
                    if b == "mix0":
                        pe.wait_ge(table_loaded, 48)
                        pe.wait_ge(blk_set, 3)
                    pe.wait_ge(perm_ready, 2 * int(b[3]) + 2)
                    mix_pe(pe, int(b[3]))
            for tc in range(SEQ // P):
                o = o_final + tc
                if tc == 0:
                    for e in (0, 1):
                        pe.wait_ge(acc_free[(o_final + e) % 2], (o_final + e) // 2)
                pe.wait_ge(acc_free[o % 2], o // 2)
                for k in range(KD):
                    last = pe.transpose(pair[o % 2][:, k * P:(k + 1) * P], xT[:, k, tc * P:(tc + 1) * P],
                                        ident[:, :])
                last.then_inc(acc_done, 1)

        @block.scalar
        def _(act):
            act.wait_ge(acc_free[0], 1)
            for j in range(2):
                act.activation(cs[:, :, j], vecs[:, 0, V_C + j * KD:V_C + (j + 1) * KD], ACT.Silu).then_inc(cs_ready, 1)
            for t in range(2):
                split_hi(act, Nth(t, 1, 0), WIDTHS[t], None)
            act.wait_ge(const_set, 2)
            for b in blocks:
                if b[:2] == "ff":
                    inst = int(b[2])
                    norm_act(act, X_NORM[inst // 2, 2 * (inst % 2)])
                    ff_act(act, inst)
                else:
                    mix_act(act, int(b[3]))

        @block.vector
        def _(dve):
            for l in range(DEPTH):
                dve.wait_ge(acc_done, l + 1)
                dve.tensor_copy(vecs[:, l, :], pair[l][:, 0:P]).then_inc(acc_free[l], 1)
            for tc in range(TOK // P):
                o = 2 + tc
                dve.wait_ge(acc_done, o + 1)
                dve.tensor_copy(xT[:, :, tc * P:(tc + 1) * P], pair[o % 2][:, :].rearrange("p (k t) -> p k t", k=KD))\
                   .then_inc(acc_free[o % 2], 1)
            dve.wait_ge(acc_free[0], 1)
            dve.wait_ge(acc_free[1], 1)
            dve.tensor_scalar(vecs_half[:, :, :], vecs[:, :, :], 0.5, None, ALU.mult).then_inc(vec_half_ready, 1)
            dve.wait_ge(vec_half_ready, 1)
            for col, scale in ((V_GQ, MLA_SCALE), (V_GNQ, NA_SCALE)):
                gains = vecs[:, :, col:col + 1].rearrange("p l a -> p (l a)")
                dve.tensor_scalar(gains, gains, scale, None, ALU.mult).then_inc(gain_scaled, 1)
            for t in range(2):
                split_lo(dve, Nth(t, 1, 0), WIDTHS[t])
            for i in steps(dve, 0, START_MOD // 2):
                for m in range(2):
                    mod_read(dve, Nth(i, 2, m))
            for b in blocks:
                if b[:2] == "ff":
                    inst = int(b[2])
                    mod_vectors(dve, inst // 2, 2 * (inst % 2))
                    norm_dve(dve, X_NORM[inst // 2, 2 * (inst % 2)])
                    ff_dve(dve, inst)
                else:
                    if b == "mix0":
                        dve.wait_ge(table_loaded, 48)
                        dve.wait_ge(bias_filled, 16 * 2 * DEPTH * NA_HEADS)
                    mix_dve(dve, int(b[3]))
            for tc in range(SEQ // P):
                o = o_final + tc
                dve.wait_ge(acc_done, o + 1)
                if tc >= 2:
                    dve.wait_ge(out_stored[tc % 2], 16 * (tc // 2))
                dve.tensor_copy(out_rows[:, tc % 2, :], pair[o % 2][:, :]).then_inc(out_staged, 1)
                dve.wait_ge(out_staged, tc + 1)
                dve.sem_inc(acc_free[o % 2], 1)


_INS = ["x", "c", "ctx", "c_ctx", "w_mod", "b_mod", "w_ffn_gate", "w_ffn_up", "w_ffn_down", "w_in", "g_cq", "w_q_up",
        "g_ckv", "w_kv_up", "g_mla_q", "g_mla_k", "g_na_q", "g_na_k", "na_rpb", "w_pool", "pool_scale", "w_out"]


def constants():
    ident = np.eye(P, dtype=np.float32)
    a = ROPE // 2
    perm = np.zeros((QK, QK), np.float32)
    cos, sin = np.ones((QK, SEQ), np.float32), np.zeros((QK, SEQ), np.float32)
    t = np.arange(SEQ)
    inv_freq = (10000.0 ** (-np.arange(0, a, 2, dtype=np.float32) / np.float32(a))).astype(np.float32)
    for axis, pos in enumerate((t // GRID_W, t % GRID_W)):
        ang = pos.astype(np.float32)[None, :] * inv_freq[:, None]
        r = NOPE + axis * a
        h = a // 2
        cos[r:r + h], cos[r + h:r + a] = np.cos(ang), np.cos(ang)
        sin[r:r + h], sin[r + h:r + a] = -np.sin(ang), np.sin(ang)
        for i in range(h):
            perm[r + h + i, r + i] = 1.0
            perm[r + i, r + h + i] = 1.0
    inv = np.zeros((P, 2, POOLW), np.float32)
    for g in range(POOL_G):
        w = 2 << g
        for start, n in ((PAD, CTX), (2 * PAD + CTX, SEQ)):
            t = np.arange(n)
            cnt = np.clip(t + w // 2, 0, n) - np.clip(t - w // 2, 0, n)
            inv[(g % 2) * 64:(g % 2) * 64 + 64, g // 2, start:start + n] = (np.float32(1) / cnt.astype(np.float32))
    return dict(k_ident=ident, k_perm=perm, k_cos=cos, k_sin=sin, k_invcnt=inv)





def kernel(**inputs):
    import concourse.bacc as bacc
    from concourse.bass_utils import run_bass_kernel_spmd

    nc = bacc.Bacc("TRN2", target_bir_lowering=False, num_devices=1, dynamic_dma_scratch_size=8192)
    arrays, args = {}, []
    for name, value in [(n, inputs[n]) for n in _INS] + list(constants().items()):
        a = np.ascontiguousarray(value)
        arrays[f"in_{name}"] = a
        args.append(nc.dram_tensor(f"in_{name}", a.shape, mybir.dt.from_np(a.dtype), kind="ExternalInput").ap())
    args.append(nc.dram_tensor("out", (1, SEQ, D_MODEL), F32, kind="ExternalOutput").ap())
    args.append(nc.dram_tensor("na_bias", (DEPTH, NA_HEADS, P, BIAS_SLOTS * GRID_W), F32, kind="Internal").ap())
    program(nc, *args, STOP)
    return run_bass_kernel_spmd(nc, [arrays], core_ids=[0]).results[0]["out"]
```

```python
from contextlib import ExitStack

import numpy as np

import concourse.bass as bass
from concourse import mybir

F32 = mybir.dt.float32
F32R = mybir.dt.float32r
ALU = mybir.AluOpType
ACT = mybir.ActivationFunctionType
AX_X = mybir.AxisListType.X

P = 128
D_MODEL = 1024
KD = D_MODEL // P
SEQ, CTX = 512, 256
TOK = SEQ + CTX
PARTS = ((0, SEQ), (SEQ, TOK))
DEPTH = 2
GRID_W = 64
MLA_HEADS, NOPE, ROPE, V_DIM = 8, 64, 32, 64
QK = NOPE + ROPE
Q_RANK, KV_RANK = 768, 256
MLA_SCALE = QK ** -0.5
NA_HEADS, NA_DIM, WIN_R, WIN_C = 4, 64, 8, 16
NA_WIDTH = NA_HEADS * NA_DIM
NA_SCALE = NA_DIM ** -0.5
POOL_G = 4
D_FF = 2816
HALF = D_FF // P // 2
N_MOD = 9
MOD_TILES = N_MOD * KD
EPS = 1e-6
NEG = -1.0e30
C_Q, C_KV, C_KR = 0, Q_RANK, Q_RANK + KV_RANK
C_QN = C_KR + ROPE
C_KN, C_VN, C_POOL = C_QN + NA_WIDTH, C_QN + 2 * NA_WIDTH, C_QN + 3 * NA_WIDTH
RPB_R, RPB_C = 2 * WIN_R - 1, 2 * WIN_C - 1
BIAS_SLOTS = RPB_R - 1
STATS = 6
V_BMOD, V_GCQ, V_GCKV, V_PSC, V_GQ, V_GK, V_GNQ, V_GNK, V_C = 0, 72, 78, 80, 82, 83, 84, 85, 86
PAD = 8
POOLW = PAD + CTX + PAD + SEQ + PAD

MIX_ORDER = [("pool", 0), ("cq", 0), ("cq", 1), ("cq", 2), ("wpool", 0), ("pool", 1), ("cq", 3), ("cq", 4), ("cq", 5),
             ("wpool", 1), ("ckv", 0), ("ckv", 1), ("kr", 0), ("qn", 0), ("qn", 1), ("kn", 0), ("kn", 1),
             ("vn", 0), ("vn", 1)]
MIX_COL = {"pool": C_POOL, "cq": C_Q, "ckv": C_KV, "kr": C_KR, "qn": C_QN, "kn": C_KN, "vn": C_VN}
MIX_OUT, _n = {}, 0
for _kind, _c in MIX_ORDER:
    if _kind == "wpool":
        MIX_OUT["y", 2 * _c], MIX_OUT["y", 2 * _c + 1] = _n, _n + 1
        _n += 2
    else:
        MIX_OUT[_kind, _c] = _n
        _n += 1
MIX_OUT["q", 0] = _n
MIX_OUT["kv", 0], MIX_OUT["kv", 1], MIX_OUT["wo", 0] = _n + 8, _n + 14, _n + 20
T_Q = len(MIX_ORDER)
T_KV, T_WO = T_Q + MLA_HEADS, T_Q + MLA_HEADS + 2

FF_TILES = 2 * (2 * HALF + KD)
MIX_OUTS = 49
WIDTHS = []
FF_T0, FF_O0, MIX_T0, MIX_O0 = [], [], [], []
N_START = SEQ // P + CTX // P + 2
_o = N_START
for _l in range(DEPTH):
    for _fi in range(2):
        FF_T0.append(len(WIDTHS))
        FF_O0.append(_o)
        WIDTHS += ([KD * P] * (2 * HALF) + [HALF * P] * KD) * 2
        _o += FF_TILES
        if _fi == 0:
            MIX_T0.append(len(WIDTHS))
            MIX_O0.append(_o)
            WIDTHS += [P if kind == "wpool" else KD * P for kind, _ in MIX_ORDER]
            WIDTHS += [Q_RANK // P * QK] * MLA_HEADS + [KV_RANK // P * 4 * P] * 2 + [KD * P] * KD
            _o += MIX_OUTS
N_TILES, O_END = len(WIDTHS), _o


class Nth:

    def __init__(self, i, stride, const):
        if isinstance(i, int):
            i, stride, const = 0, 0, i * stride + const
        self.i, self.stride, self.const = i, stride, const

    def __add__(self, k):
        return Nth(self.i, self.stride, self.const + k)

    def _at(self, stride, const):
        return self.i * stride + const if stride else const

    def n(self, plus=0):
        return self._at(self.stride, self.const + plus)

    def half(self, plus=0, times=1):
        assert self.stride % 2 == 0
        return self._at(self.stride // 2 * times, (self.const // 2 + plus) * times)

    @property
    def odd(self):
        assert self.stride % 2 == 0
        return self.const % 2


def steps(eng, a, b):
    if b - a == 1:
        yield a
    else:
        with eng.Fori(a, b) as i:
            yield i


def width(t0, stride, a, b):
    w = {WIDTHS[t0 + stride * i] if t0 + stride * i < N_TILES else 0 for i in range(a, b)}
    assert len(w) == 1
    return w.pop()


START_MOD = 2 * KD
MOD_GROUP = 4
FF_SEGS = [
    [[(0, 1, 0, 8), (1, 10, 0, 8), (10, 11, 0, 8)], [(0, 1, 0, 20), (1, 10, 0, 20), (10, 11, 0, 20)]],
    [[(0, 1, 0, 32), (1, 4, 0, 32), (4, 10, 1, 32), (10, 11, 1, 32)], [(0, 1, 1, 43), (1, 10, 1, 43), (10, 11, 1, 43)]],
    [[(0, 1, 1, 54), (1, 10, 1, 54), (10, 11, 1, 54)], [(0, 1, 1, 65), (1, 7, 1, 65), (7, 10, 1, None), (10, 11, 1, None)]],
    [[(0, 1, 1, None), (1, 10, 1, None), (10, 11, 1, None)], [(0, 10, 1, None), (10, 11, 1, None)]],
]


def last_pair(inst, half):
    return max((v0 + b - 1 for _, b, _, v0 in FF_SEGS[inst][half] if v0 is not None), default=None)


FF_EXTRA = [[19, 31], [None] * 2, [None] * 2, [None] * 2]


def program(nc, x, c, ctx_in, c_ctx, w_mod, b_mod, w_gate, w_up, w_down, w_in, g_cq, w_q_up, g_ckv, w_kv_up,
            g_mla_q, g_mla_k, g_na_q, g_na_k, na_rpb, w_pool, pool_scale, w_out,
            k_ident, k_perm, k_cos, k_sin, k_invcnt, out, na_bias):
    with ExitStack() as ctx:
        def sem(name):
            return ctx.enter_context(nc.semaphore(name))

        base = (nc.sbuf_base + 63) // 64 * 64
        place = {}

        def sb(name, shape, dt, at=None, off=0):
            nonlocal base
            size = int(np.prod(shape[1:])) * 4
            if at is None:
                start, base = base, base + (size + 31) // 32 * 32
            else:
                start = place[at][0] + off
                assert off + size <= place[at][1] + 0, (name, off, size, place[at])
            place[name] = (start, size)
            return nc.alloc_sbuf_tensor_at(name, shape, dt, offset=start)

        xT = sb("xT", [P, KD, TOK], F32)
        sb("wring", [P, 6 * HALF * P], F32)
        slot_bytes = 2 * HALF * P * 4
        w_raw = sb("w_raw", [P, 2, HALF * P], F32, "wring", 0)
        w_hi = sb("w_hi", [P, 2, HALF * P], F32R, "wring", slot_bytes)
        w_lo = sb("w_lo", [P, 2, HALF * P], F32R, "wring", 2 * slot_bytes)
        sb("harea", [P, 2 * KD * TOK], F32)
        h_hi = sb("h_hi", [P, KD, TOK], F32R, "harea", 0)
        h_lo = sb("h_lo", [P, KD, TOK], F32R, "harea", KD * TOK * 4)
        x_rows = sb("x_rows", [P, TOK // P, D_MODEL], F32, "harea", 0)
        out_rows = sb("out_rows", [P, 2, D_MODEL], F32, "harea", 0)
        sb("sarea", [P, 2 * HALF * TOK], F32)
        s_hi = sb("s_hi", [P, HALF, TOK], F32R, "sarea", 0)
        s_lo = sb("s_lo", [P, HALF, TOK], F32R, "sarea", HALF * TOK * 4)
        sb("scratch", [P, 4 * TOK], F32)
        sq = sb("sq", [P, 2, TOK], F32, "scratch", 0)
        hs = sb("hs", [P, 2, TOK], F32, "scratch", 2 * TOK * 4)
        sg = sb("sg", [P, TOK], F32, "scratch", 0)
        sf = sb("sf", [P, TOK], F32, "scratch", 2 * TOK * 4)
        q_f = sb("q_f", [P, MLA_HEADS, TOK], F32, "harea", 0)
        k_f = sb("k_f", [P, MLA_HEADS, TOK], F32, "harea", KD * TOK * 4)
        RQ, RK = Q_RANK // P, KV_RANK // P
        cq_hi = sb("cq_hi", [P, RQ, TOK], F32R, "sarea", 0)
        cq_f = sb("cq_f", [P, RQ, TOK], F32, "sarea", RQ * TOK * 4)
        cq_lo = sb("cq_lo", [P, RQ, TOK], F32R, "sarea", RQ * TOK * 4)
        ck_at = 2 * RQ * TOK * 4
        ck_hi = sb("ck_hi", [P, RK, TOK], F32R, "sarea", ck_at)
        ck_f = sb("ck_f", [P, RK, TOK], F32, "sarea", ck_at + RK * TOK * 4)
        ck_lo = sb("ck_lo", [P, RK, TOK], F32R, "sarea", ck_at + RK * TOK * 4)
        na_at = ck_at + 2 * RK * TOK * 4
        na_f = sb("na_f", [P, 4, TOK], F32, "sarea", na_at)
        vn_f = sb("vn_f", [P, TOK // P, NA_WIDTH], F32, "sarea", na_at + 4 * TOK * 4)
        v_hi = sb("v_hi", [P, TOK // P, MLA_HEADS * V_DIM], F32R, "sarea", 0)
        v_lo = sb("v_lo", [P, TOK // P, MLA_HEADS * V_DIM], F32R, "sarea", 4 * TOK * 4)
        y_f = sb("y_f", [P, 6, TOK], F32, "harea", KD * TOK * 4)
        vn_hi = sb("vn_hi", [P, TOK // P, NA_WIDTH], F32R, "sarea", 14 * TOK * 4)
        vn_lo = sb("vn_lo", [P, TOK // P, NA_WIDTH], F32R, "sarea", na_at + 4 * TOK * 4)
        wo_first = sb("wo_first", [P, 2, KD * P], F32, "sarea", 8 * TOK * 4)
        pu = sb("pu", [P, POOLW], F32, "sarea", na_at)
        pool_lo = sb("pool_lo", [P, TOK], F32R, "sarea", na_at)
        ps = [sb(f"ps{i}", [P, POOLW], F32, "sarea", na_at + (i + 1) * POOLW * 4) for i in range(2)]
        inv_cnt = sb("inv_cnt", [P, POOLW], F32, "sarea", na_at + 3 * POOLW * 4)
        pool_hi = sb("pool_hi", [P, TOK], F32R, "sarea", na_at + 4 * POOLW * 4)
        sb("pbuf", [P, 2 * TOK], F32)
        pt_hi, pt_lo = (sb(n, [P, TOK // P, 4, P], F32R, "wring", 4 * i * TOK * 4) for i, n in enumerate(("pt_hi", "pt_lo")))
        prob = sb("prob", [P, 3, TOK], F32, "wring", 8 * TOK * 4)
        att_set = [[sb(n, [P, TOK], F32R, at, off * TOK * 4) for n, at, off in places]
                   for places in ((("qs_hi0", "sarea", 8), ("qs_lo0", "sarea", 9), ("ks_hi0", "sarea", 10),
                                   ("ks_lo0", "sarea", 11)),
                                  (("qs_hi1", "sarea", 12), ("qs_lo1", "sarea", 13), ("ks_hi1", "pbuf", 0),
                                   ("ks_lo1", "pbuf", 1)))]
        na_tt = sb("na_tt", [P, 2, BIAS_SLOTS * GRID_W], F32, "scratch", 0)
        mod_raw = sb("mod_raw", [P, KD, 2 * P], F32)
        mod_acc = sb("mod_acc", [P, 2, 2 * P], F32)
        yp_f = sb("yp_f", [P, 2, TOK], F32, "mod_raw", 0)
        acc = sb("acc", [P, TOK], F32, "pbuf", 0)
        nstat = sb("nstat", [P, 2, TOK // P], F32)
        hstat = sb("hstat", [P, 2, 2, 2 * (TOK // P)], F32)
        kr_f = sb("kr_f", [P, TOK], F32)
        rot_s = sb("rot_s", [P, SEQ], F32)
        cos = sb("cos", [P, SEQ], F32)
        sin = sb("sin", [P, SEQ], F32)
        perm = sb("perm", [P, QK], F32)
        perm_q = sb("perm_q", [P, QK], F32)
        perm_k = sb("perm_k", [P, QK], F32)
        blk = sb("blk", [P, P], F32)
        stat = sb("stat", [P, STATS, 3], F32)
        ident = sb("ident", [P, P], F32)
        ones = sb("ones", [P, P], F32)
        eps = sb("eps", [P, 1], F32)
        mod_first = sb("mod_first", [P, KD, START_MOD * P], F32, "sarea", 0)
        vrows = sb("vrows", [P, DEPTH, P], F32, "sarea", START_MOD * KD * P * 4)
        vecs = sb("vecs", [P, DEPTH, P], F32)
        vecs_half = sb("vecs_half", [P, DEPTH, P], F32)
        cs = sb("cs", [P, KD, 2], F32)
        mod = sb("mod", [P, DEPTH * MOD_TILES, 2], F32)
        mv = sb("mv", [P, 3, KD, 2], F32)

        pair = [ctx.enter_context(nc.psum_tensor(f"pair{i}", [P, 1024], F32)) for i in range(2)]
        pmid = ctx.enter_context(nc.psum_tensor("pmid", [P, 1024], F32))
        psum2 = ctx.enter_context(nc.psum_tensor("psum2", [P, 1024], F32))
        mod_ps = [pmid[:, 0:2], pmid[:, 512:514]]

        x_loaded, const_loaded = sem("x_loaded"), sem("const_loaded")
        vec_zero, vec_loaded = sem("vec_zero"), sem("vec_loaded")
        gain_scaled = sem("gain_scaled")
        const_set, cs_ready, vec_half_ready = sem("const_set"), sem("cs_ready"), sem("vec_half_ready")
        w_loaded = [sem("w_loaded0"), sem("w_loaded1")]
        w_hi_done, w_lo_done = sem("w_hi_done"), sem("w_lo_done")
        acc_done = sem("acc_done")
        acc_free = [sem("acc_free0"), sem("acc_free1")]
        mod_loaded, mod_step, mod_summed, mod_pair_read = (
            sem(f"mod_{k}") for k in ("loaded", "step", "summed", "pair_read"))
        mod_first_loaded = [sem(f"mod_first_loaded{i}") for i in range(START_MOD // MOD_GROUP)]
        mod_done = sem("mod_done")
        mod_free = [sem("mod_free0"), sem("mod_free1")]
        mv_ready = sem("mv_ready")
        gate_ready = sem("gate_ready")
        n_sq, n_acc, n_sum, n_std, n_rstd = (sem(f"n_{k}") for k in ("sq", "acc", "sum", "std", "rstd"))
        n_bc, n_t, n_hi, n_lo = (sem(f"n_{k}") for k in ("bc", "t", "hi", "lo"))
        s_hi_done = sem("s_hi_done")
        bias_neg, bias_filled, bias_stored = sem("bias_neg"), sem("bias_filled"), sem("bias_stored")
        table_loaded, blk_set, perm_ready = sem("table_loaded"), sem("blk_set"), sem("perm_ready")
        inv_loaded = sem("inv_loaded")
        pads_set, pool_step, pool_hi_done, pool_lo_done = (
            sem(n) for n in ("pads_set", "pool_step", "pool_hi_done", "pool_lo_done"))
        kr_spread, h_sq = sem("kr_spread"), sem("h_sq")
        h_sum, h_rstd, h_bc, h_step, h_done = (sem(f"h_{k}") for k in ("sum", "rstd", "bc", "step", "done"))
        w_loaded_pool = sem("w_loaded_pool")
        a_hi, a_lo, v_hi_done = sem("a_hi"), sem("a_lo"), sem("v_hi_done")
        a_s, a_max, a_exp, a_rsum, a_copied, a_t, a_pth, a_ptl, a_pv, a_out, a_bias = (
            sem(f"a_{k}") for k in ("s", "max", "exp", "rsum", "copied", "t", "pth", "ptl", "pv", "out", "bias"))
        a_latent_t, a_latent_hi, a_latent_lo = (sem(f"a_latent_{k}") for k in ("t", "hi", "lo"))
        tt_loaded = [sem("tt_loaded0"), sem("tt_loaded1")]
        y_hi_done, y_lo_done, y_last_done = sem("y_hi_done"), sem("y_lo_done"), sem("y_last_done")
        s_lo_done = sem("s_lo_done")
        out_staged, out_stored = sem("out_staged"), [sem("out_stored0"), sem("out_stored1")]

        def load(eng, t, src, dst):
            if not (t.stride == 0 and t.const < 2):
                eng.wait_ge(w_lo_done, t.n(-1))
            eng.dma_start(dst, src).then_inc(w_loaded[t.odd], 16)

        def split_hi(eng, t, w, done, raw=w_raw):
            if w == 0:
                return
            if done is not None:
                eng.wait_ge(acc_done, done.n(1))
            eng.wait_ge(w_loaded[t.odd], t.half(1, 16))
            eng.activation(w_hi[:, t.odd, 0:w], raw[:, t.odd, 0:w], ACT.Copy).then_inc(w_hi_done, 1)

        def split_lo(eng, t, w, raw=w_raw):
            if w == 0:
                return
            eng.wait_ge(w_hi_done, t.n(1))
            eng.tensor_tensor(w_lo[:, t.odd, 0:w], raw[:, t.odd, 0:w], w_hi[:, t.odd, 0:w].bitcast(F32),
                              ALU.subtract).then_inc(w_lo_done, 1)

        def read_out(o):
            return o.half(1)

        def product(eng, t, o, chunks, lhs, rhs, cols):
            products(eng, [(t, o, lhs)], chunks, rhs, cols)

        def products(eng, outs, chunks, rhs, cols, before_chunk=None):
            for t, o, _ in outs:
                if t is not None:
                    eng.wait_ge(w_lo_done, t.n(1))
                eng.wait_ge(acc_free[o.odd], o.half())
            for k in range(chunks):
                if before_chunk:
                    before_chunk(k)
                first, end = k == 0, k == chunks - 1
                for _, o, lhs in outs:
                    wh, wl = lhs(k)
                    for a, b in cols:
                        (rh, rl), dst = rhs(k, a, b), pair[o.odd][0:wh.shape[-1], a:b]
                        eng.matmul(dst, wh, rh, start=first, stop=False)
                        eng.matmul(dst, wh, rl, start=False, stop=False)
                    for a, b in cols:
                        (rh, rl), dst = rhs(k, a, b), pair[o.odd][0:wh.shape[-1], a:b]
                        last = eng.matmul(dst, wl, rh, start=False, stop=end)
                    if end:
                        last.then_inc(acc_done, 1)

        def wtile(t, per=P):
            return lambda k: (w_hi[:, t.odd, k * per:(k + 1) * per], w_lo[:, t.odd, k * per:(k + 1) * per])

        def h_moving(k, a, b):
            return h_hi[:, k, a:b], h_lo[:, k, a:b]

        norms = []

        def norm_bases(q):
            return sum(n["chunks"] for n in norms[:q]), sum(n["chunks"] + 1 for n in norms[:q])

        def norm_square(eng, q, k):
            n, (_, a0) = norms[q], norm_bases(q)
            w = n["w"]
            if n["after"]:
                eng.wait_ge(n_lo, n["after"])
            if not (a0 == 0 and k.const == 0):
                eng.wait_ge(n_acc, k.n(a0))
            eng.activation(sq[:, k.odd, 0:w], n["src"](k.n()), ACT.Square).then_inc(n_sq, 1)

        def norm_clear(eng, q):
            if q:
                eng.wait_ge(n_sum, q)
            eng.memset(acc[:, 0:norms[q]["w"]], 0.0).then_inc(n_acc, 1)

        def norm_add(eng, q, k):
            w, (b0, a0) = norms[q]["w"], norm_bases(q)
            eng.wait_ge(n_sq, k.n(norms[q]["squares"] + 1))
            eng.wait_ge(n_acc, k.n(a0 + 1))
            eng.tensor_tensor(acc[:, 0:w], acc[:, 0:w], sq[:, k.odd, 0:w], ALU.add).then_inc(n_acc, 1)

        def norm_sum(eng, q):
            n, (_, a0) = norms[q], norm_bases(q)
            eng.wait_ge(n_acc, a0 + n["chunks"] + 1)
            for tc in range(n["w"] // P):
                last = eng.matmul(n["psum"][:, tc:tc + 1], acc[:, tc * P:(tc + 1) * P], ones[:, 0:1], start=True, stop=True)
            last.then_inc(n_sum, 1)

        def norm_std(eng, q):
            n = norms[q]
            m = n["w"] // P
            eng.wait_ge(n_sum, q + 1)
            if q:
                eng.wait_ge(n_rstd, q)
            eng.activation(nstat[:, 0, 0:m], n["psum"][:, 0:m], ACT.Sqrt, bias=eps[:, 0:1],
                           scale=1.0 / (n["chunks"] * P)).then_inc(n_std, 1)

        def norm_rstd(eng, q):
            m = norms[q]["w"] // P
            eng.wait_ge(n_std, q + 1)
            if q:
                eng.wait_ge(n_bc, q)
            eng.reciprocal(nstat[:, 1, 0:m], nstat[:, 0, 0:m]).then_inc(n_rstd, 1)

        def norm_spread(eng, q):
            n = norms[q]
            eng.wait_ge(n_rstd, q + 1)
            for tc in range(n["w"] // P):
                last = eng.matmul(n["psum"][:, tc * P:(tc + 1) * P], nstat[:, 1, tc:tc + 1].broadcast_to([P, P]),
                                  ident[:, :], start=True, stop=True)
            last.then_inc(n_bc, 1)

        def norm_scale(eng, q, k):
            n, (b0, _) = norms[q], norm_bases(q)
            if k == 0:
                eng.wait_ge(n_bc, q + 1)
                eng.wait_ge(n_acc, n["adds"])
            if b0 + max(0, k - 1):
                eng.wait_ge(n_lo, b0 + max(0, k - 1))
            cols = [(p, a, b) for p, (a, b) in enumerate(PARTS) if a < n["w"]] if n["shift"] else [(0, 0, n["w"])]
            for p, a, b in cols:
                last = eng.scalar_tensor_tensor(sq[:, k % 2, a:b], n["src"](k)[:, a:b], n["scale"](k, p),
                                                n["psum"][:, a:b], ALU.mult, ALU.mult)
            last.then_inc(n_t, 1)

        def norm_hi(eng, q, k):
            n, (b0, _) = norms[q], norm_bases(q)
            eng.wait_ge(n_t, b0 + k + 1)
            if n["shift"]:
                for p, (a, b) in enumerate(PARTS):
                    if a < n["w"]:
                        last = eng.activation(n["hi"][:, k, a:b], sq[:, k % 2, a:b], ACT.Identity, bias=n["shift"](k, p))
            else:
                last = eng.activation(n["hi"][:, k, :], sq[:, k % 2, :], ACT.Copy)
            last.then_inc(n_hi, 1)

        def norm_lo(eng, q, k):
            n, (b0, _) = norms[q], norm_bases(q)
            eng.wait_ge(n_hi, b0 + k + 1)
            if n["shift"]:
                for p, (a, b) in enumerate(PARTS):
                    if a < n["w"]:
                        last = eng.scalar_tensor_tensor(n["lo"][:, k, a:b], sq[:, k % 2, a:b], n["shift"](k, p),
                                                        n["hi"][:, k, a:b].bitcast(F32), ALU.add, ALU.subtract)
            else:
                last = eng.tensor_tensor(n["lo"][:, k, :], sq[:, k % 2, :], n["hi"][:, k, :].bitcast(F32), ALU.subtract)
            last.then_inc(n_lo, 1)

        def x_norm_pe(eng, q):
            norm_sum(eng, q)
            norm_spread(eng, q)

        def x_norm_act(eng, q):
            norm_std(eng, q)
            eng.wait_ge(mv_ready, norms[q]["mods"])
            for k in range(KD):
                norm_hi(eng, q, k)

        def x_norm_dve(eng, q):
            norm_rstd(eng, q)
            eng.wait_ge(mv_ready, norms[q]["mods"])
            for k in range(KD + 1):
                if k < KD:
                    norm_scale(eng, q, k)
                if k:
                    norm_lo(eng, q, k - 1)

        def x_chunk(k, w):
            return xT[:, k, 0:w] if isinstance(k, int) else xT[:, bass.ds(k, 1), 0:w].rearrange("p a t -> p (a t)")

        def add_norm(**n):
            b0, a0 = norm_bases(len(norms))
            norms.append(dict(dict(squares=b0, after=b0, adds=a0 + n["chunks"] + 1), **n))

        X_NORM, CQ_NORM, CK_NORM = {}, {}, {}
        mv_count = 0
        for l in range(DEPTH):
            for b in range(3):
                mv_count += 4
                X_NORM[l, b] = len(norms)
                w = SEQ if (l, b) == (DEPTH - 1, 2) else TOK
                add_norm(chunks=KD, w=w, src=lambda k, w=w: x_chunk(k, w), psum=psum2, mods=mv_count,
                         scale=lambda k, p: mv[:, 0, k, p:p + 1], shift=lambda k, p: mv[:, 1, k, p:p + 1],
                         hi=h_hi, lo=h_lo)
                if b == 1:
                    gain = lambda col: lambda k, p, l=l: vecs[:, l, col + k:col + k + 1]
                    q = CQ_NORM[l] = len(norms)
                    add_norm(chunks=RQ, w=TOK, src=lambda k: cq_f[:, k, :], psum=psum2, scale=gain(V_GCQ), shift=None,
                             hi=cq_hi, lo=cq_lo)
                    norms[q]["adds"] += RK + 1
                    CK_NORM[l] = q + 1
                    add_norm(chunks=RK, w=TOK, src=lambda k: ck_f[:, k, :], psum=pmid, scale=gain(V_GCKV), shift=None,
                             hi=ck_hi, lo=ck_lo, after=norms[q]["after"])

        def mod_ready(eng, tiles):
            for j in range(2):
                eng.wait_ge(mod_free[j], PAIR_0)
            if tiles > START_MOD:
                eng.wait_ge(mod_pair_read, tiles // 2 - PAIR_0)

        def mod_vectors(eng, l, b):
            mod_ready(eng, l * MOD_TILES + (3 * b + 2) * KD)
            for which, group, add in ((0, 3 * b + 1, 1.0), (1, 3 * b, 0.0)):
                u = l * MOD_TILES + group * KD
                for j in range(2):
                    eng.scalar_tensor_tensor(mv[:, which, :, j], mod[:, u:u + KD, j], add,
                                             vecs[:, l, V_BMOD + group * KD:V_BMOD + (group + 1) * KD],
                                             ALU.add, ALU.add).then_inc(mv_ready, 1)

        def gate_vectors(eng, l, b):
            mod_ready(eng, l * MOD_TILES + (3 * b + 3) * KD)
            group, u = 3 * b + 2, l * MOD_TILES + (3 * b + 2) * KD
            bias = vecs if b == 1 else vecs_half
            for j in range(2):
                eng.scalar_tensor_tensor(mv[:, 2, :, j], mod[:, u:u + KD, j], 1.0 if b == 1 else 0.5,
                                         bias[:, l, V_BMOD + group * KD:V_BMOD + (group + 1) * KD],
                                         ALU.mult, ALU.add).then_inc(gate_ready, 1)
            eng.wait_ge(gate_ready, 2 * (3 * l + b + 1))

        def mod_product(eng, u):
            eng.wait_ge(mod_first_loaded[u // MOD_GROUP], 16)
            if u >= 2:
                eng.wait_ge(mod_free[u % 2], u // 2)
            for k in range(KD):
                last = eng.matmul(mod_ps[u % 2], mod_first[:, k, u * P:(u + 1) * P], cs[:, k, :], start=k == 0,
                                  stop=k == KD - 1)
            last.then_inc(mod_done, 1)

        def mod_read(eng, u):
            eng.wait_ge(mod_done, u + 1)
            eng.tensor_copy(mod[:, u, :], mod_ps[u % 2]).then_inc(mod_free[u % 2], 1)

        PAIR_0, PAIR_STEPS = START_MOD // 2, 2 * KD

        def mod_load(eng, l, v):
            if not (v.stride == 0 and v.const == PAIR_0):
                eng.wait_ge(mod_step, v.n(-PAIR_0) * PAIR_STEPS)
            src = w_mod[l].rearrange("(k p) (t m) -> p k t m", p=P, m=2 * P)[:, :, v.n(-l * MOD_TILES // 2), :]
            eng.dma_start(mod_raw[:, :, :], src).then_inc(mod_loaded, 16)

        def mod_accumulate(eng, v, part):
            if part == 0:
                eng.wait_ge(mod_loaded, v.n(1 - PAIR_0) * 16)
                if not (v.stride == 0 and v.const == PAIR_0):
                    eng.wait_ge(mod_summed, v.n(-PAIR_0))
            for k in range(part * KD // 2, (part + 1) * KD // 2):
                for j in range(2):
                    if k == 0:
                        eng.tensor_scalar(mod_acc[:, j, :], mod_raw[:, k, :], cs[:, k, j:j + 1], None, ALU.mult)\
                           .then_inc(mod_step, 1)
                    else:
                        eng.wait_ge(mod_step, v.n(-PAIR_0) * PAIR_STEPS + (2 * k + j - 1))
                        eng.scalar_tensor_tensor(mod_acc[:, j, :], mod_raw[:, k, :], cs[:, k, j:j + 1],
                                                 mod_acc[:, j, :], ALU.mult, ALU.add).then_inc(mod_step, 1)

        def mod_sum(eng, v):
            eng.wait_ge(mod_step, v.n(1 - PAIR_0) * PAIR_STEPS)
            if not (v.stride == 0 and v.const == PAIR_0):
                eng.wait_ge(mod_pair_read, v.n(-PAIR_0))
            for m in range(2):
                for j in range(2):
                    last = eng.matmul(pmid[:, 2 * m + j:2 * m + j + 1], mod_acc[:, j, m * P:(m + 1) * P], ones[:, 0:1],
                                      start=True, stop=True)
            last.then_inc(mod_summed, 1)

        def mod_pair_out(eng, v):
            eng.wait_ge(mod_summed, v.n(1 - PAIR_0))
            eng.tensor_copy(mod[:, bass.ds(v.n() * 2, 2), :], pmid[:, 0:4].rearrange("p (a b) -> p a b", b=2))\
               .then_inc(mod_pair_read, 1)

        NEXT_BLOCK = {0: (0, 1), 1: (1, 0), 2: (1, 1)}

        def ff_cols(inst):
            return PARTS[:1] if inst == 3 else PARTS

        def ff_pe(eng, inst):
            cols = ff_cols(inst)
            lo0 = norm_bases(X_NORM[inst // 2, 2 * (inst % 2)])[0]
            ready = lambda k: eng.wait_ge(n_lo, lo0 + k + 1)
            for half in range(2):
                n0, o0 = FF_T0[inst] + 30 * half, FF_O0[inst] + 30 * half
                for a, b, _, v0 in FF_SEGS[inst][half]:
                    for i in steps(eng, a, b):
                        opening = half == 0 and (a, b) == (0, 1)
                        if opening:
                            products(eng, [(t, o, wtile(t)) for t, o in
                                           ((Nth(i, 2, n0 + j), Nth(i, 2, o0 + j)) for j in range(2))],
                                     KD, h_moving, cols, ready)
                        for j in range(2):
                            t, o = Nth(i, 2, n0 + j), Nth(i, 2, o0 + j)
                            if not opening:
                                product(eng, t, o, KD, wtile(t), h_moving, cols)
                            if j == 0 and a and v0 is not None:
                                mod_sum(eng, Nth(i, 1, v0 - 1))
                last, extra = last_pair(inst, half), FF_EXTRA[inst][half]
                s0 = (2 * inst + half) * HALF
                split = lambda k: eng.wait_ge(s_lo_done, s0 + k + 1)
                for a, b in ((0, 1), (1, KD // 2)):
                    for i in steps(eng, a, b):
                        for j in range(2):
                            t, o = Nth(i, 2, n0 + 2 * HALF + j), Nth(i, 2, o0 + 2 * HALF + j)
                            products(eng, [(t, o, wtile(t))], HALF, lambda k, a, b: (s_hi[:, k, a:b], s_lo[:, k, a:b]),
                                     cols, split if isinstance(i, int) and j == 0 else None)
                            if extra and isinstance(i, int) and j == 0:
                                mod_sum(eng, Nth(0, 1, last))
                if last:
                    mod_sum(eng, Nth(0, 1, extra or last))

        def ff_up_load(eng, inst, half, i):
            l, fi = divmod(inst, 2)
            for j, w in enumerate((w_gate, w_up)):
                t = Nth(i, 2, FF_T0[inst] + 30 * half + j)
                src = w[l, fi].rearrange("(k p) (f m) -> p k f m", p=P, m=P)
                load(eng, t, src[:, :, i + half * HALF, :], w_raw[:, t.odd, 0:KD * P].rearrange("p (k m) -> p k m", m=P))

        def ff_down_load(eng, inst, half, i):
            l, fi = divmod(inst, 2)
            for j in range(2):
                t = Nth(i, 2, FF_T0[inst] + 30 * half + 2 * HALF + j)
                src = w_down[l, fi].rearrange("(f p) (d m) -> p f d m", p=P, m=P)
                load(eng, t, src[:, half * HALF:(half + 1) * HALF, i * 2 + j, :],
                     w_raw[:, t.odd, :].rearrange("p (k m) -> p k m", m=P))

        def first_loads(eng, b):
            if b is None:
                return
            if b[:2] == "ff":
                ff_up_load(eng, int(b[2]), 0, 0)
            else:
                for n in range(2):
                    mix_tile_load(eng, int(b[3]), n)

        def ff_sp(eng, inst, following):
            if inst == 1:
                eng.wait_ge(y_lo_done, KD - 1)
            for half in range(2):
                for a, b, l, v0 in FF_SEGS[inst][half]:
                    for i in steps(eng, a, b):
                        if b == HALF:
                            ff_down_load(eng, inst, half, 0)
                        else:
                            ff_up_load(eng, inst, half, i + 1)
                        if v0 is not None:
                            mod_load(eng, l, Nth(i, 1, v0))
                if FF_EXTRA[inst][half]:
                    mod_load(eng, inst // 2, Nth(0, 1, FF_EXTRA[inst][half]))
                for i in steps(eng, 1, KD // 2):
                    ff_down_load(eng, inst, half, i)
                if half == 0:
                    ff_up_load(eng, inst, 1, 0)
                else:
                    first_loads(eng, following)

        def ff_act(eng, inst):
            w = ff_cols(inst)[-1][1]
            eng.preload_act_table_set("silu_and_others")
            for half in range(2):
                n0, o0 = FF_T0[inst] + 30 * half, FF_O0[inst] + 30 * half
                s0 = (2 * inst + half) * HALF
                for a, b, _, _ in FF_SEGS[inst][half]:
                    for i in steps(eng, a, b):
                        t, o, s = Nth(i, 2, n0), Nth(i, 2, o0), Nth(i, 1, s0)
                        eng.wait_ge(acc_done, o.n(1))
                        eng.activation(sg[:, 0:w], pair[o.odd][:, 0:w], ACT.Silu).then_inc(acc_free[o.odd], 1)
                        split_hi(eng, t + 2, width(n0 + 2, 2, a, b), o)
                        eng.wait_ge(acc_free[(o + 1).odd], read_out(o + 1))
                        eng.activation(s_hi[:, bass.ds(i, 1), 0:w].rearrange("p a t -> p (a t)"), sf[:, 0:w],
                                       ACT.Copy).then_inc(s_hi_done, 1)
                        split_hi(eng, t + 3, width(n0 + 3, 2, a, b), o + 1)
                squares = half == 1 and inst < 3
                if squares:
                    eng.preload_act_table_set("sqrt_and_others")
                for a, b in ((0, 3), (3, 4)):
                    for i in steps(eng, a, b):
                        for j in range(2):
                            t, o = Nth(i, 2, n0 + 2 * HALF + j), Nth(i, 2, o0 + 2 * HALF + j)
                            w_next = width(n0 + 2 * HALF + 2 + j, 2, a, b)
                            urgent = squares and a == 3 and j == 1
                            if not urgent:
                                split_hi(eng, t + 2, w_next, o)
                            if squares:
                                eng.wait_ge(acc_free[o.odd], read_out(o))
                                norm_square(eng, X_NORM[NEXT_BLOCK[inst]], Nth(i, 2, j))
                            if urgent:
                                split_hi(eng, t + 2, w_next, o)

        def residual(eng, o, d, cols):
            eng.wait_ge(acc_done, o.n(1))
            for p, (a, b) in enumerate(cols):
                last = eng.scalar_tensor_tensor(
                    xT[:, bass.ds(d, 1), a:b].rearrange("p a t -> p (a t)"), pair[o.odd][:, a:b],
                    mv[:, 2, bass.ds(d, 1), p], xT[:, bass.ds(d, 1), a:b].rearrange("p a t -> p (a t)"),
                    ALU.mult, ALU.add)
            last.then_inc(acc_free[o.odd], 1)

        def ff_dve(eng, inst):
            cols = ff_cols(inst)
            w = cols[-1][1]
            l, fi = divmod(inst, 2)
            for half in range(2):
                n0, o0 = FF_T0[inst] + 30 * half, FF_O0[inst] + 30 * half
                s0 = (2 * inst + half) * HALF
                for a, b, _, v0 in FF_SEGS[inst][half]:
                    for i in steps(eng, a, b):
                        t, o, s = Nth(i, 2, n0), Nth(i, 2, o0), Nth(i, 1, s0)
                        split_lo(eng, t + 2, width(n0 + 2, 2, a, b))
                        if v0 is not None:
                            if a:
                                mod_pair_out(eng, Nth(i, 1, v0 - 1))
                            mod_accumulate(eng, Nth(i, 1, v0), 0)
                        eng.wait_ge(acc_done, o.n(2))
                        eng.wait_ge(acc_free[o.odd], read_out(o))
                        eng.tensor_tensor(sf[:, 0:w], pair[(o + 1).odd][:, 0:w], sg[:, 0:w],
                                          ALU.mult).then_inc(acc_free[(o + 1).odd], 1)
                        eng.wait_ge(s_hi_done, s.n(1))
                        eng.tensor_tensor(s_lo[:, bass.ds(i, 1), 0:w].rearrange("p a t -> p (a t)"), sf[:, 0:w],
                                          s_hi[:, bass.ds(i, 1), 0:w].bitcast(F32).rearrange("p a t -> p (a t)"),
                                          ALU.subtract).then_inc(s_lo_done, 1)
                        split_lo(eng, t + 3, width(n0 + 3, 2, a, b))
                        if v0 is not None:
                            mod_accumulate(eng, Nth(i, 1, v0), 1)
                last, extra = last_pair(inst, half), FF_EXTRA[inst][half]
                if extra:
                    mod_pair_out(eng, Nth(0, 1, last))
                    for part in range(2):
                        mod_accumulate(eng, Nth(0, 1, extra), part)
                if half == 0:
                    gate_vectors(eng, l, 2 * fi)
                elif inst < 3:
                    norm_clear(eng, X_NORM[NEXT_BLOCK[inst]])
                for a, b in ((0, 3), (3, 4)):
                    for i in steps(eng, a, b):
                        for j in range(2):
                            t, o = Nth(i, 2, n0 + 2 * HALF + j), Nth(i, 2, o0 + 2 * HALF + j)
                            residual(eng, o, Nth(i, 2, j).n(), cols)
                            w_next, squares = width(n0 + 2 * HALF + 2 + j, 2, a, b), half == 1 and inst < 3
                            urgent = squares and a == 3 and j == 1
                            if not urgent:
                                split_lo(eng, t + 2, w_next)
                            if squares:
                                norm_add(eng, X_NORM[NEXT_BLOCK[inst]], Nth(i, 2, j))
                            if urgent:
                                split_lo(eng, t + 2, w_next)
                if last:
                    mod_pair_out(eng, Nth(0, 1, extra or last))

        def mo(l, kind, c=0):
            return Nth(0, 1, MIX_O0[l] + MIX_OUT[kind, c])

        def mix_outs(l, n):
            kind, c = MIX_ORDER[n]
            return [mo(l, "y", 2 * c), mo(l, "y", 2 * c + 1)] if kind == "wpool" else [mo(l, kind, c)]

        H_STEPS = 4 + 2 * MLA_HEADS

        def head_step(l, what, h=0):
            return H_STEPS * l + {"na": 0, "q": 4, "k": 4 + MLA_HEADS}[what] + h

        def swapped_product(eng, t, o, half, chunks, stat, moving):
            eng.wait_ge(w_lo_done, t.n(1))
            eng.wait_ge(acc_free[o.odd], o.half())
            for at, tc in enumerate(range(3 * half, 3 * half + 3)):
                dst = at * 2 * P
                out = pair[o.odd][:, dst:dst + 2 * P].rearrange("p (a b) -> p a b", a=2)
                for k in range(chunks):
                    (ah, al), (wh, wl) = stat(k, tc), moving(k)
                    d = out if wh.shape[1] == 2 else pair[o.odd][:, dst:dst + 2 * P].rearrange("p (a b) -> p a b", a=4)
                    eng.matmul(d, ah, wh, start=k == 0, stop=False)
                    eng.matmul(d, ah, wl, start=False, stop=False)
                    last = eng.matmul(d, al, wh, start=False, stop=k == chunks - 1)
            last.then_inc(acc_done, 1)

        def head_sum(eng, s, o, rows, cols_ap, rot=None):
            n = cols_ap.shape[-1]
            eng.wait_ge(h_sq, s.n(1))
            for tc in range(TOK // P):
                at = TOK + tc * n
                last = eng.matmul(pair[o.odd][:, at:at + n], hs[0:rows, s.odd, tc * P:(tc + 1) * P], cols_ap,
                                  start=True, stop=True)
            last.then_inc(h_sum, 1)
            if rot is not None:
                lhs, rhs = rot
                eng.wait_ge(h_done, s.n(-1))
                eng.matmul(pmid[0:QK, s.odd * 512:s.odd * 512 + SEQ], lhs, rhs, start=True, stop=True)

        def head_spread(eng, s, rows, n, after):
            eng.wait_ge(h_rstd, s.n(1))
            after()
            for tc in range(TOK // P):
                for h in range(n):
                    inv, per = hstat[:, s.odd, 1, tc * n + h:tc * n + h + 1], rows // n
                    last = eng.matmul(psum2[h * per:(h + 1) * per, tc * P:(tc + 1) * P], inv.broadcast_to([P, per]),
                                      ident[:, :], start=True, stop=True)
            last.then_inc(h_bc, 1)

        def head_square(eng, s, o, rows):
            if not (s.stride == 0 and s.const < 2):
                eng.wait_ge(h_sum, s.n(-1))
            eng.activation(hs[0:rows, s.odd, :], pair[o.odd][0:rows, 0:TOK], ACT.Square).then_inc(h_sq, 1)

        def head_std(eng, s, o, n, dim):
            eng.wait_ge(h_sum, s.n(1))
            if not (s.stride == 0 and s.const < 2):
                eng.wait_ge(h_rstd, s.n(-1))
            m = n * (TOK // P)
            eng.activation(hstat[:, s.odd, 0, 0:m], pair[o.odd][:, TOK:TOK + m], ACT.Sqrt, bias=eps[:, 0:1],
                           scale=1.0 / dim).then_inc(acc_free[o.odd], 1)

        def head_rstd(eng, s, o, n):
            eng.wait_ge(acc_free[o.odd], read_out(o))
            if not (s.stride == 0 and s.const < 2):
                eng.wait_ge(h_bc, s.n(-1))
            m = n * (TOK // P)
            eng.reciprocal(hstat[:, s.odd, 1, 0:m], hstat[:, s.odd, 0, 0:m]).then_inc(h_rstd, 1)

        EVENTS = list(range(12)) + ["v0", "v1"] + list(range(12, 16)) + ["v2", "v3"]

        def head_before(e, back):
            h = EVENTS[e - back] if 0 <= e - back < len(EVENTS) else None
            return h if isinstance(h, int) else None

        def head_out(l, h):
            return mo(l, "q") + h if h < MLA_HEADS else mo(l, "kv", (h - MLA_HEADS) // 4) + (h - MLA_HEADS) % 4

        def chunk_at(x_f, h, w):
            return x_f[0:QK, bass.ds(h, 1), 0:w].rearrange("p a t -> p (a t)")

        LATENT_SCALING = {("kr", 0): (("cq", 0), ("cq", 1)), ("qn", 0): (("cq", 2), ("cq", 3)),
                          ("qn", 1): (("cq", 4), ("cq", 5)), ("kn", 0): (("ck", 0),), ("kn", 1): (("ck", 1),)}
        NA_STEPS = {("qn", 1): 1, ("kn", 0): 2, ("kn", 1): 3, ("vn", 0): 4, ("vn", 1): 5}

        def mix_pe(eng, l):
            t0 = MIX_T0[l]
            q = X_NORM[l, 1]
            x_norm_pe(eng, q)
            lo0 = norm_bases(q)[0]
            ready = lambda k: eng.wait_ge(n_lo, lo0 + k + 1)
            na_outs = [mo(l, "qn", 0), mo(l, "qn", 1), mo(l, "kn", 0), mo(l, "kn", 1)]
            ck_scaled = norm_bases(CQ_NORM[l])[0] + RQ

            def na_sum(m):
                head_sum(eng, Nth(0, 1, head_step(l, "na", m)), na_outs[m], P, blk[:, 0:P:NA_DIM])

            def na_spread(m):
                s = head_step(l, "na", m)
                after = (lambda: eng.wait_ge(n_t, ck_scaled)) if m == 0 else (lambda: eng.wait_ge(h_done, s))
                head_spread(eng, Nth(0, 1, s), P, 2, after)

            products(eng, [(Nth(0, 1, t0 + n), mix_outs(l, n)[0], wtile(Nth(0, 1, t0 + n))) for n in range(2)],
                     KD, h_moving, PARTS, ready)
            for n, (kind, c) in enumerate(MIX_ORDER):
                t, outs = Nth(0, 1, t0 + n), mix_outs(l, n)
                if n < 2:
                    continue
                if kind == "wpool":
                    eng.wait_ge(pool_lo_done, 2 * l + c + 1)
                    for g in range(2):
                        r = slice(g * 64, g * 64 + 64)
                        product(eng, t, outs[g], 1, lambda k: (w_hi[r, t.odd, 0:P], w_lo[r, t.odd, 0:P]),
                                lambda k, a, b: (pool_hi[r, a:b], pool_lo[r, a:b]), PARTS)
                elif kind == "vn":
                    swapped_product(eng, Nth(0, 1, t0 + T_Q - 1), outs[0], c, KD,
                                    lambda k, tc: (h_hi[:, k, tc * P:(tc + 1) * P], h_lo[:, k, tc * P:(tc + 1) * P]),
                                    lambda k: (w_hi[:, :, k * P:(k + 1) * P], w_lo[:, :, k * P:(k + 1) * P]))
                else:
                    product(eng, t, outs[0], KD, wtile(t), h_moving, PARTS)
                if (kind, c) == ("ckv", 0):
                    norm_sum(eng, CQ_NORM[l])
                if (kind, c) == ("ckv", 1):
                    norm_spread(eng, CQ_NORM[l])
                if (kind, c) == ("kr", 0):
                    norm_sum(eng, CK_NORM[l])
                if (kind, c) == ("qn", 0):
                    norm_spread(eng, CK_NORM[l])
                m = NA_STEPS.get((kind, c), 0)
                if 1 <= m <= 4:
                    na_sum(m - 1)
                if 2 <= m <= 5:
                    na_spread(m - 2)

            def head_step_of(i, h):
                return Nth(i, 2, head_step(l, "q", h))

            def heads_before(e, i=0, x=lambda h: 0):
                h = head_before(e, 1)
                if h is not None:
                    if h < MLA_HEADS:
                        o, rot = Nth(i, 2, head_out(l, h).const), (perm_q[0:QK, :], chunk_at(q_f, i * 2 + h, SEQ))
                    else:
                        o, rot = head_out(l, h), (perm_k[0:QK, :], k_f[0:QK, h - MLA_HEADS, 0:SEQ])
                    if h == MLA_HEADS:
                        eng.wait_ge(kr_spread, MLA_HEADS * (l + 1))
                    head_sum(eng, head_step_of(i, h), o, QK, ones[0:QK, 0:1], rot)
                h = head_before(e, 2)
                if h is not None:
                    s = head_step_of(i, h)
                    head_spread(eng, s, QK, 1, lambda: eng.wait_ge(h_done, s.n()))

            eng.wait_ge(perm_ready, 2 * (l + 1))
            for a, b in ((0, 1), (1, MLA_HEADS // 2)):
                for i in steps(eng, a, b):
                    for j in range(2):
                        t, o = Nth(i, 2, t0 + T_Q + j), Nth(i, 2, mo(l, "q").const + j)
                        product(eng, t, o, RQ, wtile(t, QK), lambda k, a, b: (cq_hi[:, k, a:b], cq_lo[:, k, a:b]), PARTS)
                        if isinstance(i, int):
                            heads_before(j)
                        else:
                            h = j - 1
                            head_sum(eng, Nth(i, 2, head_step(l, "q", h)), Nth(i, 2, mo(l, "q").const + h), QK,
                                     ones[0:QK, 0:1], (perm_q[0:QK, :], chunk_at(q_f, i * 2 + h, SEQ)))
                            s = Nth(i, 2, head_step(l, "q", h - 1))
                            head_spread(eng, s, QK, 1, lambda: eng.wait_ge(h_done, s.n()))
            ck_moving = lambda k, a, b: (ck_hi[:, k, a:b], ck_lo[:, k, a:b])
            for e in range(MLA_HEADS, len(EVENTS) + 2):
                if e < len(EVENTS):
                    event = EVENTS[e]
                    c = (event - MLA_HEADS) // 4 if isinstance(event, int) else int(event[1]) // 2
                    t = Nth(0, 1, t0 + T_KV + c)
                    view = [w[:, t.odd, 0:RK * 4 * P].rearrange("p (k h m) -> p k h m", k=RK, m=P) for w in (w_hi, w_lo)]
                    if isinstance(event, int):
                        h = event % 4
                        product(eng, t, mo(l, "kv", c) + h, RK, lambda k: (view[0][:, k, h, :], view[1][:, k, h, :]),
                                ck_moving, PARTS)
                    else:
                        v = int(event[1]) % 2
                        swapped_product(eng, t, mo(l, "kv", c) + (4 + v), v, RK,
                                        lambda k, tc: (ck_hi[:, k, tc * P:(tc + 1) * P], ck_lo[:, k, tc * P:(tc + 1) * P]),
                                        lambda k: tuple(x[:, k, :, NOPE:] for x in view))
                heads_before(e)
            attention_pe(eng, l)
            cols = y_cols(l)
            for i0, i1 in ((0, 1), (1, KD // 2)):
                for i in steps(eng, i0, i1):
                    for j in range(2):
                        t, o = Nth(i, 2, t0 + T_WO + j), Nth(i, 2, mo(l, "wo").const + j)
                        before = None
                        if i0 == 0 and j == 0:
                            eng.wait_ge(y_lo_done, (KD - 1) * (l + 1))
                            before = lambda k: eng.wait_ge(y_last_done, l + 1) if k == 5 else None
                        products(eng, [(t, o, wtile(t))], KD, h_moving, cols, before)

        def y_cols(l):
            return PARTS if l < DEPTH - 1 else PARTS[:1]

        def mix_tile_load(eng, l, n):
            if isinstance(n, Nth):
                t = n
                h = n.n(-(MIX_T0[l] + T_Q))
                src = w_q_up[l].rearrange("(k p) (h m) -> p k h m", p=P, m=QK)[:, :, h, :]
                load(eng, t, src, w_raw[:, t.odd, 0:RQ * QK].rearrange("p (k m) -> p k m", m=QK))
                return
            t = Nth(0, 1, MIX_T0[l] + n)
            if n >= T_KV:
                c = n - T_KV
                src = w_kv_up[l].rearrange("(k p) n -> p k n", p=P)[:, :, c * 4 * P:(c + 1) * 4 * P]
                load(eng, t, src, w_raw[:, t.odd, 0:RK * 4 * P].rearrange("p (k m) -> p k m", k=RK))
                return
            kind, c = MIX_ORDER[n]
            if kind == "wpool":
                eng.wait_ge(w_lo_done, t.n(-1))
                for half in range(2):
                    eng.dma_start(w_raw[:, t.odd, half * 64:half * 64 + 64],
                                  w_pool[l, 2 * c:2 * c + 2].rearrange("g c d -> (g c) d"))\
                       .then_inc(w_loaded_pool, 16)
                eng.wait_ge(w_loaded_pool, 32 * (2 * l + c + 1))
                eng.sem_inc(w_loaded[t.odd], 16)
                return
            col = MIX_COL[kind] + c * P
            src = w_in[l].rearrange("(k p) n -> p k n", p=P)[:, :, col:col + P]
            load(eng, t, src, w_raw[:, t.odd, 0:KD * P].rearrange("p (k m) -> p k m", m=P))

        def wo_load(eng, l, t, raw=w_raw):
            d = t.n(-(MIX_T0[l] + T_WO))
            src = w_out[l].rearrange("(k p) (d m) -> p k d m", p=P, m=P)[:, :, d, :]
            load(eng, t, src, raw[:, t.odd, 0:KD * P].rearrange("p (k m) -> p k m", m=P))

        def mix_sp(eng, l):
            for n in range(2, T_Q):
                if n == 2:
                    eng.wait_ge(acc_done, MIX_O0[l])
                    eng.dma_start(inv_cnt[:, :], k_invcnt[:, 0, :]).then_inc(inv_loaded, 16)
                mix_tile_load(eng, l, n)
                if MIX_ORDER[n] == ("cq", 4):
                    eng.wait_ge(pool_lo_done, 2 * l + 1)
                    eng.dma_start(inv_cnt[:, :], k_invcnt[:, 1, :]).then_inc(inv_loaded, 16)
            for i in steps(eng, 0, MLA_HEADS // 2):
                for j in range(2):
                    mix_tile_load(eng, l, Nth(i, 2, MIX_T0[l] + T_Q + j))
            for c in range(2):
                mix_tile_load(eng, l, T_KV + c)
            nb = att_chunks(l)
            eng.wait_ge(h_done, H_STEPS * (l + 1))
            eng.wait_ge(bias_stored, 16 * bias_dmas)
            for i in range(2):
                for j in range(2):
                    if i:
                        eng.wait_ge(a_max, ATT_C0[l] + 4 * nb + (nb // 2) * (j + 1))
                    eng.dma_start(na_tt[:, j, :], na_bias[l, 2 * i + j]).then_inc(tt_loaded[j], 16)
            eng.wait_ge(a_s, ATT_C0[l] + group_first(l, MLA_HEADS + 1))
            for j in range(2):
                wo_load(eng, l, Nth(j, 1, MIX_T0[l] + T_WO), wo_first)
            eng.wait_ge(a_out, (ATT_C0[l] + 6 * nb) // 2)
            for i in steps(eng, 1, KD // 2):
                for j in range(2):
                    wo_load(eng, l, Nth(i, 2, MIX_T0[l] + T_WO + j))

        def evacuate(eng, o, dst, scale=None):
            eng.wait_ge(acc_done, o.n(1))
            src = pair[o.odd][:, 0:TOK]
            if len(dst.shape) == 3:
                src = src.rearrange("p (a b) -> p a b", a=dst.shape[1])
            eng.tensor_copy(dst, src).then_inc(acc_free[o.odd], 1)

        def values(l, m):
            o = mo(l, "kv", m // 2) + (4 + m % 2)
            blocks, cols = slice(3 * (m % 2), 3 * (m % 2) + 3), slice((m // 2) * 2 * P, (m // 2 + 1) * 2 * P)
            return o, pair[o.odd][:, 0:TOK].rearrange("p (a b) -> p a b", a=3), (slice(0, P), blocks, cols)

        def values_hi(eng, l, m):
            o, src, at = values(l, m)
            eng.wait_ge(acc_done, o.n(1))
            eng.activation(v_hi[at], src, ACT.Copy).then_inc(v_hi_done, 1)

        def values_lo(eng, l, m):
            o, src, at = values(l, m)
            eng.wait_ge(v_hi_done, MLA_HEADS // 2 * l + m + 1)
            eng.tensor_tensor(v_lo[at], src, v_hi[at].bitcast(F32), ALU.subtract).then_inc(acc_free[o.odd], 1)

        def mix_act(eng, l):
            t0 = MIX_T0[l]
            x_norm_act(eng, X_NORM[l, 1])
            na_outs = [mo(l, "qn", 0), mo(l, "qn", 1), mo(l, "kn", 0), mo(l, "kn", 1)]
            for n, (kind, c) in enumerate(MIX_ORDER):
                t, outs = Nth(0, 1, t0 + n), mix_outs(l, n)
                if MIX_ORDER[n + 1:] and MIX_ORDER[n + 1][0] == "wpool":
                    eng.wait_ge(pool_step, pool_steps(l, MIX_ORDER[n + 1][1] + 1))
                    for a, b, at in ((0, SEQ, 2 * PAD + CTX), (SEQ, TOK, PAD)):
                        eng.activation(pool_hi[:, a:b], ps[0][:, at:at + b - a], ACT.Copy).then_inc(pool_hi_done, 1)
                if kind == "kr":
                    eng.wait_ge(acc_done, outs[0].n(1))
                    eng.activation(kr_f[NOPE:QK, :], pair[outs[0].odd][0:ROPE, 0:TOK], ACT.Copy)\
                       .then_inc(acc_free[outs[0].odd], 1)
                if kind in ("qn", "kn"):
                    m = c + 2 * (kind == "kn")
                    eng.wait_ge(acc_done, outs[0].n(1))
                    eng.activation(na_f[:, m, :], pair[outs[0].odd][:, 0:TOK], ACT.Copy)
                    head_square(eng, Nth(0, 1, head_step(l, "na", m)), outs[0], P)
                m = NA_STEPS.get((kind, c), 0)
                if 1 <= m <= 4:
                    head_std(eng, Nth(0, 1, head_step(l, "na", m - 1)), na_outs[m - 1], 2, NA_DIM)
                if (kind, c) == ("vn", 1):
                    for m in range(2):
                        split_hi(eng, t + (1 + m), WIDTHS[t0 + n + 1 + m], outs[-1])
                elif kind != "vn":
                    split_hi(eng, t + 2, WIDTHS[t0 + n + 2], outs[-1])
                if kind in ("cq", "ckv"):
                    o = outs[0]
                    eng.wait_ge(acc_free[o.odd], read_out(o))
                    norm_square(eng, (CQ_NORM if kind == "cq" else CK_NORM)[l], Nth(c, 0, c))
                if (kind, c) == ("ckv", 0):
                    norm_std(eng, CQ_NORM[l])
                if (kind, c) == ("kr", 0):
                    norm_std(eng, CK_NORM[l])
                for which, k in LATENT_SCALING.get((kind, c), ()):
                    norm_hi(eng, (CQ_NORM if which == "cq" else CK_NORM)[l], k)
            for a, b in ((0, 1), (1, 3), (3, 4)):
                for i in steps(eng, a, b):
                    for j in range(2):
                        t, o = Nth(i, 2, t0 + T_Q + j), Nth(i, 2, mo(l, "q").const + j)
                        s = Nth(i, 2, head_step(l, "q", j))
                        eng.wait_ge(acc_done, o.n(1))
                        eng.activation(chunk_at(q_f, i * 2 + j, TOK), pair[o.odd][0:QK, 0:TOK], ACT.Copy)
                        head_square(eng, s, o, QK)
                        split_hi(eng, t + 2, width(t0 + T_Q + j + 2, 2, a, b), o)
                        if not (isinstance(i, int) and i == 0 and j == 0):
                            head_std(eng, s + (-1), o + (-1), 1, QK)
            for e in range(MLA_HEADS, len(EVENTS) + 1):
                event = EVENTS[e] if e < len(EVENTS) else None
                if isinstance(event, int):
                    h = event - MLA_HEADS
                    o, s = head_out(l, event), Nth(0, 1, head_step(l, "q", event))
                    if h < 2:
                        eng.wait_ge(h_sum, s.n(-1))
                        eng.activation(hs[NOPE:QK, s.odd, :], kr_f[NOPE:QK, :], ACT.Square)
                    eng.wait_ge(acc_done, o.n(1))
                    eng.activation(k_f[0:NOPE, h, :], pair[o.odd][0:NOPE, 0:TOK], ACT.Copy)
                    head_square(eng, s, o, NOPE)
                elif event:
                    values_hi(eng, l, int(event[1]))
                h = head_before(e, 1)
                if h is not None:
                    head_std(eng, Nth(0, 1, head_step(l, "q", h)), head_out(l, h), 1, QK)
                if event == "v2":
                    eng.wait_ge(h_done, head_step(l, "k", 0) + 1)
                    attention_split_hi(eng, 0)
            attention_act(eng, l)
            w = y_cols(l)[-1][1]
            split_hi(eng, Nth(0, 1, t0 + T_WO), KD * P, None, wo_first)
            eng.wait_ge(a_out, y_done(l, 5))
            y_hi(eng, l, 5)
            split_hi(eng, Nth(0, 1, t0 + T_WO + 1), KD * P, None, wo_first)
            eng.preload_act_table_set("sqrt_and_others")
            for a, b in ((0, 3), (3, 4)):
                for i in steps(eng, a, b):
                    for j in range(2):
                        t, o = Nth(i, 2, t0 + T_WO + j), Nth(i, 2, mo(l, "wo").const + j)
                        urgent = a == 3 and j == 1
                        if not urgent:
                            split_hi(eng, t + 2, width(t0 + T_WO + 2 + j, 2, a, b), o)
                        eng.wait_ge(acc_free[o.odd], read_out(o))
                        norm_square(eng, X_NORM[l, 2], Nth(i, 2, j))
                        if urgent:
                            split_hi(eng, t + 2, width(t0 + T_WO + 2 + j, 2, a, b), o)

        def head_scale(eng, s, which, h, l, first_step):
            x_f, gain = (q_f, V_GQ) if which == "q" else (k_f, V_GK)
            g = vecs[0:QK, l, gain:gain + 1]
            head = lambda a, b: x_f[0:QK, bass.ds(h, 1), a:b].rearrange("p a t -> p (a t)")
            eng.wait_ge(h_bc, s.n(1))
            eng.wait_ge(h_done, s.n())
            eng.tensor_tensor(rot_s[0:QK, :], pmid[0:QK, s.odd * 512:s.odd * 512 + SEQ], sin[0:QK, :], ALU.mult)\
               .then_inc(h_step, 1)
            eng.scalar_tensor_tensor(head(0, SEQ), head(0, SEQ), g, cos[0:QK, :], ALU.mult, ALU.mult).then_inc(h_step, 1)
            eng.wait_ge(h_step, first_step.n(2))
            eng.tensor_tensor(head(0, SEQ), head(0, SEQ), rot_s[0:QK, :], ALU.add).then_inc(h_step, 1)
            eng.scalar_tensor_tensor(head(SEQ, TOK), head(SEQ, TOK), g, psum2[0:QK, SEQ:TOK], ALU.mult, ALU.mult)\
               .then_inc(h_step, 1)
            eng.wait_ge(h_step, first_step.n(4))
            eng.tensor_tensor(head(0, SEQ), head(0, SEQ), psum2[0:QK, 0:SEQ], ALU.mult).then_inc(h_done, 1)

        def na_scale(eng, l, m):
            s = head_step(l, "na", m)
            gain = V_GNQ if m < 2 else V_GNK
            eng.wait_ge(h_bc, s + 1)
            eng.scalar_tensor_tensor(na_f[:, m, :], na_f[:, m, :], vecs[:, l, gain:gain + 1], psum2[:, 0:TOK],
                                     ALU.mult, ALU.mult).then_inc(h_done, 1)

        def mix_dve(eng, l):
            t0 = MIX_T0[l]
            mod_vectors(eng, l, 1)
            x_norm_dve(eng, X_NORM[l, 1])
            eng.wait_ge(gain_scaled, 2)
            for dst, gain in ((perm_q, V_GQ), (perm_k, V_GK)):
                eng.tensor_scalar(dst[0:QK, :], perm[0:QK, :], vecs[0:QK, l, gain:gain + 1], None, ALU.mult)\
                   .then_inc(perm_ready, 1)
            na_outs = [mo(l, "qn", 0), mo(l, "qn", 1), mo(l, "kn", 0), mo(l, "kn", 1)]
            for n, (kind, c) in enumerate(MIX_ORDER):
                t, outs = Nth(0, 1, t0 + n), mix_outs(l, n)
                if MIX_ORDER[n + 1:] and MIX_ORDER[n + 1][0] == "wpool":
                    eng.wait_ge(pool_hi_done, 2 * (2 * l + MIX_ORDER[n + 1][1] + 1))
                    for a, b, at in ((0, SEQ, 2 * PAD + CTX), (SEQ, TOK, PAD)):
                        last = eng.tensor_tensor(pool_lo[:, a:b], ps[0][:, at:at + b - a],
                                                 pool_hi[:, a:b].bitcast(F32), ALU.subtract)
                    last.then_inc(pool_lo_done, 1)
                if kind == "pool":
                    o = outs[0]
                    eng.wait_ge(acc_done, o.n(1))
                    eng.wait_ge(pads_set, 3 * (2 * l + c + 1))
                    eng.tensor_copy(pu[:, PAD:PAD + CTX], pair[o.odd][:, SEQ:TOK])
                    eng.tensor_copy(pu[:, 2 * PAD + CTX:2 * PAD + CTX + SEQ], pair[o.odd][:, 0:SEQ])\
                       .then_inc(acc_free[o.odd], 1)
                elif kind == "wpool":
                    for g in range(2):
                        o, r = outs[g], slice(g * 64, g * 64 + 64)
                        eng.wait_ge(acc_done, o.n(1))
                        eng.tensor_scalar(yp_f[r, c, :], pair[o.odd][r, 0:TOK], vecs[r, l, V_PSC + c:V_PSC + c + 1],
                                          None, ALU.mult).then_inc(acc_free[o.odd], 1)
                elif kind == "cq":
                    evacuate(eng, outs[0], cq_f[:, c, :])
                elif kind == "ckv":
                    evacuate(eng, outs[0], ck_f[:, c, :])
                elif kind == "vn":
                    o, first = outs[0], Nth(0, 1, t0 + T_Q - 2).odd
                    eng.wait_ge(acc_done, o.n(1))
                    for slot in range(2):
                        cols = slice(((slot - first) % 2) * P, ((slot - first) % 2 + 1) * P)
                        src = pair[o.odd][:, 0:TOK].rearrange("p (a s b) -> p a s b", a=3, b=P)[:, :, slot, :]
                        last = eng.tensor_copy(vn_f[:, 3 * c:3 * c + 3, cols], src)
                    last.then_inc(acc_free[o.odd], 1)
                if (kind, c) == ("vn", 1):
                    for m in range(2):
                        split_lo(eng, t + (1 + m), WIDTHS[t0 + n + 1 + m])
                elif kind != "vn":
                    split_lo(eng, t + 2, WIDTHS[t0 + n + 2])
                if kind in ("cq", "ckv"):
                    q = (CQ_NORM if kind == "cq" else CK_NORM)[l]
                    if c == 0:
                        norm_clear(eng, q)
                    norm_add(eng, q, Nth(c, 0, c))
                if (kind, c) == ("ckv", 0):
                    norm_rstd(eng, CQ_NORM[l])
                for which, k in LATENT_SCALING.get((kind, c), ()):
                    q = (CQ_NORM if which == "cq" else CK_NORM)[l]
                    norm_scale(eng, q, k)
                    norm_lo(eng, q, k)
                if (kind, c) == ("kr", 0):
                    norm_rstd(eng, CK_NORM[l])
                m = NA_STEPS.get((kind, c), 0)
                if 1 <= m <= 4:
                    head_rstd(eng, Nth(0, 1, head_step(l, "na", m - 1)), na_outs[m - 1], 2)
                if 2 <= m <= 5:
                    na_scale(eng, l, m - 2)

            def heads_before(i, h, recip, scale):
                if recip:
                    head_rstd(eng, Nth(i, 2, head_step(l, "q", h - 1)), Nth(i, 2, mo(l, "q").const + h - 1), 1)
                if scale:
                    head_scale(eng, Nth(i, 2, head_step(l, "q", h - 2)), "q", i * 2 + h - 2, l,
                               Nth(i, 8, 4 * (2 * MLA_HEADS * l + h - 2)))

            for a, b in ((0, 1), (1, 3), (3, 4)):
                for i in steps(eng, a, b):
                    for j in range(2):
                        split_lo(eng, Nth(i, 2, t0 + T_Q + j + 2), width(t0 + T_Q + j + 2, 2, a, b))
                        late = not (isinstance(i, int) and i == 0)
                        heads_before(i, j, late or j > 0, late)
            for e in range(MLA_HEADS, len(EVENTS) + 2):
                if e < len(EVENTS) and not isinstance(EVENTS[e], int):
                    values_lo(eng, l, int(EVENTS[e][1]))
                h = head_before(e, 1)
                if h is not None:
                    head_rstd(eng, Nth(0, 1, head_step(l, "q", h)), head_out(l, h), 1)
                h = head_before(e, 2)
                if h is not None:
                    which, at = ("q", h) if h < MLA_HEADS else ("k", h - MLA_HEADS)
                    head_scale(eng, Nth(0, 1, head_step(l, "q", h)), which, at, l, Nth(0, 1, 4 * (2 * MLA_HEADS * l + h)))
            attention_dve(eng, l)
            w, cols = y_cols(l)[-1][1], y_cols(l)
            split_lo(eng, Nth(0, 1, t0 + T_WO), KD * P, wo_first)
            eng.wait_ge(y_hi_done, KD * (l + 1))
            eng.tensor_tensor(h_lo[:, 5, 0:w], y_src(5, w), h_hi[:, 5, 0:w].bitcast(F32), ALU.subtract)\
               .then_inc(y_last_done, 1)
            split_lo(eng, Nth(0, 1, t0 + T_WO + 1), KD * P, wo_first)
            gate_vectors(eng, l, 1)
            norm_clear(eng, X_NORM[l, 2])
            for a, b in ((0, 3), (3, 4)):
                for i in steps(eng, a, b):
                    for j in range(2):
                        t, o = Nth(i, 2, t0 + T_WO + j), Nth(i, 2, mo(l, "wo").const + j)
                        residual(eng, o, Nth(i, 2, j).n(), cols)
                        urgent = a == 3 and j == 1
                        if not urgent:
                            split_lo(eng, t + 2, width(t0 + T_WO + 2 + j, 2, a, b))
                        norm_add(eng, X_NORM[l, 2], Nth(i, 2, j))
                        if urgent:
                            split_lo(eng, t + 2, width(t0 + T_WO + 2 + j, 2, a, b))

        def pool_steps(l, chunks):
            return 12 * l + (0, 5, 12)[chunks]

        def mix_pool(eng, l):
            done = pool_steps(l, 0)
            for c in range(2):
                first = mo(l, "pool", 0).const if c == 0 else mo(l, "y", 1).const + 1
                eng.wait_ge(acc_done, first)
                if c == 1:
                    eng.wait_ge(pool_lo_done, 2 * l + 1)
                for at in (0, PAD + CTX, 2 * PAD + CTX + SEQ):
                    eng.memset(pu[:, at:at + PAD], 0.0).then_inc(pads_set, 1)
                o = mo(l, "pool", c)
                eng.wait_ge(acc_free[o.odd], read_out(o))
                eng.wait_ge(pads_set, 3 * (2 * l + c + 1))
                src, cur, lo, hi = pu, 0, 0, POOLW
                for reach in ((1, 1) if c == 0 else (1, 1, 2, 4)):
                    back, ahead = (1, 0) if src is pu else (reach, reach)
                    lo, hi = lo + back, hi - ahead
                    eng.tensor_tensor(ps[cur][:, lo:hi], src[:, lo - back:hi - back], src[:, lo + ahead:hi + ahead],
                                      ALU.add).then_inc(pool_step, 1)
                    done += 1
                    eng.wait_ge(pool_step, done)
                    src, cur = ps[cur], 1 - cur
                eng.wait_ge(inv_loaded, 16 * (2 * l + c + 1))
                a, b = PAD, POOLW - PAD
                for g in range(2):
                    r = slice(g * 64, g * 64 + 64)
                    eng.tensor_tensor(ps[0][r, a:b], ps[g][r, a:b], inv_cnt[r, a:b], ALU.mult).then_inc(pool_step, 1)
                    done += 1
                eng.wait_ge(pool_step, done)
                eng.tensor_tensor(ps[0][:, a:b], ps[0][:, a:b], pu[:, a:b], ALU.subtract).then_inc(pool_step, 1)
                done += 1
            o = mo(l, "vn", 1)
            eng.wait_ge(acc_done, o.n(1))
            eng.wait_ge(acc_free[mo(l, "kr").odd], read_out(mo(l, "kr")))
            for h in range(MLA_HEADS):
                eng.tensor_copy(k_f[NOPE:QK, h, :], kr_f[NOPE:QK, :]).then_inc(kr_spread, 1)
            attention_pool(eng, l)

        def att_chunks(l):
            return 12 if l < DEPTH - 1 else 8

        ATT_C0 = [0, 6 * 12]
        ATT_SPLITS = 21

        def chunk_info(l, c):
            pair_n, c = divmod(c, att_chunks(l))
            per = att_chunks(l) // 2
            j, q0 = c // per, (c % per) * P
            kind, i = ("mla", pair_n) if pair_n < 4 else ("na", pair_n - 4)
            return kind, i, j, q0, (PARTS if q0 < SEQ else PARTS[1:])

        def n_chunks(l):
            return 6 * att_chunks(l)

        def att_group(l, c):
            kind, i, j, q0, _ = chunk_info(l, c)
            return (2 * i + j, q0 == 0) if kind == "mla" else (MLA_HEADS + i, q0 == 0 and j == 0)

        def group_first(l, g):
            per = att_chunks(l) // 2
            return g * per if g < MLA_HEADS else (MLA_HEADS + 2 * (g - MLA_HEADS)) * per

        GROUPS = MLA_HEADS + 2

        def splits(g):
            qh, ql, kh, kl = att_set[g % 2]
            if g < MLA_HEADS:
                return 2 * g, [(q_f[0:QK, g, :], qh[0:QK, :], ql[0:QK, :]), (k_f[0:QK, g, :], kh[0:QK, :], kl[0:QK, :])]
            i = g - MLA_HEADS
            out = [(na_f[:, i, :], qh[:, :], ql[:, :]), (na_f[:, i + 2, :], kh[:, :], kl[:, :])]
            if i == 0:
                out.append((vn_f[:, :, :], vn_hi[:, :, :], vn_lo[:, :, :]))
            return 2 * MLA_HEADS + 3 * i, out

        def own_scores(l, c):
            kind, _, _, q0, _ = chunk_info(l, c)
            return kind == "mla" or q0 >= SEQ

        def latent_parts(l, c):
            return sum(1 for layer in range(l + 1) for x in range(c if layer == l else n_chunks(layer))
                       if chunk_info(layer, x)[3] < SEQ)

        def bias_steps(l, c):
            return sum(2 for layer in range(l + 1) for x in range(c if layer == l else n_chunks(layer))
                       if not own_scores(layer, x))

        Y_ORDER = [0, 1, 2, 3, 6, 7, 4, 5]

        def y_split_at(l, s):
            pair_n, at = divmod(s, att_chunks(l))
            return {1: [0], 2: [1], 3: [2], 4: [3, 6, 7], 5: [4]}.get(pair_n, []) if at == 7 else []

        def y_done(l, k):
            return (ATT_C0[l] + (k + 1) * att_chunks(l)) // 2

        def y_src(k, w):
            return y_f[:, k, 0:w] if k < 6 else yp_f[:, k - 6, 0:w]

        def y_hi(eng, l, k):
            w = y_cols(l)[-1][1]
            eng.activation(h_hi[:, k, 0:w], y_src(k, w), ACT.Copy).then_inc(y_hi_done, 1)

        def wait_if(eng, semaphore, value):
            if value > 0:
                eng.wait_ge(semaphore, value)

        def attention_pe(eng, l):
            c0, n = ATT_C0[l], n_chunks(l)
            for v in (4, 5):
                o = mo(l, "kv", 1) + v
                eng.wait_ge(acc_free[o.odd], read_out(o))
            for s in range(n + 4):
                if s < n:
                    kind, i, j, q0, keys = chunk_info(l, s)
                    g, new = att_group(l, s)
                    qh, ql, kh, kl = att_set[g % 2]
                    rows = slice(0, QK) if kind == "mla" else slice(j * NA_DIM, (j + 1) * NA_DIM)
                    if new:
                        eng.wait_ge(a_lo, ATT_SPLITS * l + splits(g)[0] + len(splits(g)[1]))
                    wait_if(eng, a_exp, c0 + s - 1)
                    for a, b in keys:
                        dst, q = pair[s % 2][:, a:b], slice(q0, q0 + P)
                        eng.matmul(dst, qh[rows, q], kh[rows, a:b], start=True, stop=False)
                        eng.matmul(dst, qh[rows, q], kl[rows, a:b], start=False, stop=False)
                        last = eng.matmul(dst, ql[rows, q], kh[rows, a:b], start=False, stop=True)
                    last.then_inc(a_s, 1)
                if 2 <= s < n + 2:
                    c = s - 2
                    keys = chunk_info(l, c)[4]
                    eng.wait_ge(a_exp, c0 + c + 1)
                    for part, (a, b) in enumerate(PARTS):
                        if a < keys[0][0]:
                            continue
                        if part == 0:
                            wait_if(eng, a_latent_lo, latent_parts(l, c))
                        else:
                            wait_if(eng, a_ptl, c0 + c)
                        for k in range(a // P, b // P):
                            last = eng.transpose(pmid[:, k * P:(k + 1) * P], prob[:, c % 3, k * P:(k + 1) * P], ident[:, :])
                        last.then_inc((a_latent_t, a_t)[part], 1)
                if s >= 4:
                    b, part = (s - 4) // 2, s % 2
                    kind, i, j, q0, keys = chunk_info(l, 2 * b)
                    kc = [k for k in range(TOK // P) if k * P >= keys[0][0]]
                    if part == 0:
                        eng.wait_ge(a_ptl, c0 + 2 * b + 2)
                        wait_if(eng, a_out, c0 // 2 + b - 1)
                        eng.wait_ge(a_rsum, c0 + 2 * b + 2)
                        for h in range(2):
                            at = (b % 2) * 512 + (2 + h) * P
                            eng.matmul(psum2[:, at:at + P], stat[:, (2 * b + h) % STATS, 2:3].broadcast_to([P, P]),
                                       ident[:, :], start=True, stop=True)
                    vh, vl = (v_hi, v_lo) if kind == "mla" else (vn_hi, vn_lo)
                    dst = psum2[:, (b % 2) * 512:(b % 2) * 512 + 2 * P].rearrange("p (c q) -> p c q", c=2)
                    slots = slice(2 * (b % 2), 2 * (b % 2) + 2)
                    for k in kc[:len(kc) // 2] if part == 0 else kc[len(kc) // 2:]:
                        ph, pl = pt_hi[:, k, slots, :], pt_lo[:, k, slots, :]
                        eng.matmul(dst, vh[:, k, i * P:(i + 1) * P], ph, start=k == kc[0], stop=False)
                        eng.matmul(dst, vh[:, k, i * P:(i + 1) * P], pl, start=False, stop=False)
                        last = eng.matmul(dst, vl[:, k, i * P:(i + 1) * P], ph, start=False, stop=k == kc[-1])
                    if part:
                        last.then_inc(a_pv, 1)

        def attention_split_hi(eng, g):
            for src, hi, lo in splits(g)[1]:
                eng.activation(hi, src, ACT.Copy).then_inc(a_hi, 1)

        def attention_act(eng, l):
            c0, n = ATT_C0[l], n_chunks(l)
            eng.preload_act_table_set("exp_and_others")
            eng.wait_ge(acc_done, mo(l, "kv", 1).n(6))
            eng.wait_ge(h_done, H_STEPS * (l + 1))

            def split(g):
                attention_split_hi(eng, g)

            for s in range(n + 5):
                for k in y_split_at(l, s):
                    if k < 6:
                        eng.wait_ge(a_out, y_done(l, k))
                    y_hi(eng, l, k)
                if 2 <= s < n + 2:
                    c = s - 2
                    if c >= 4:
                        eng.wait_ge(a_pv, c0 // 2 + (c - 4) // 2 + 1)
                    for a, b in chunk_info(l, c)[4]:
                        if a == 0:
                            eng.wait_ge(a_latent_t, latent_parts(l, c) + 1)
                        else:
                            eng.wait_ge(a_t, c0 + c + 1)
                        eng.activation(pt_hi[:, a // P:b // P, c % 4, :], pmid[:, a:b].rearrange("p (k q) -> p k q", q=P),
                                       ACT.Copy).then_inc(a_latent_hi if a == 0 else a_pth, 1)
                if s >= 6 and s % 2 == 0:
                    b = (s - 6) // 2
                    kind, i, j, q0, _ = chunk_info(l, 2 * b)
                    r, bank = slice(j * 64, j * 64 + 64), (b % 2) * 512
                    eng.wait_ge(a_pv, c0 // 2 + b + 1)
                    eng.activation(y_f[r, i if kind == "mla" else 4 + i, q0:q0 + 2 * P], psum2[r, bank:bank + 2 * P],
                                   ACT.Copy).then_inc(a_copied, 1)
                if s < n:
                    kind, i, j, q0, keys = chunk_info(l, s)
                    a, b = keys[0][0], TOK
                    eng.wait_ge(a_max, c0 + s + 1)
                    wait_if(eng, a_t, c0 + s - 2)
                    eng.activation(prob[:, s % 3, a:b], pair[s % 2][:, a:b] if own_scores(l, s) else prob[:, s % 3, a:b],
                                   ACT.Exp, bias=stat[:, s % STATS, 0:1], accum_out=stat[:, s % STATS, 1:2]).then_inc(a_exp, 1)
                if s < n:
                    g, new = att_group(l, s)
                    if new and g + 1 < GROUPS:
                        eng.wait_ge(a_s, c0 + s)
                        split(g + 1)

        def attention_pool(eng, l):
            n, w = n_chunks(l), y_cols(l)[-1][1]

            def split(g):
                first, operands = splits(g)
                for m, (src, hi, lo) in enumerate(operands):
                    eng.wait_ge(a_hi, ATT_SPLITS * l + first + m + 1)
                    eng.tensor_tensor(lo, src, hi.bitcast(F32), ALU.subtract).then_inc(a_lo, 1)

            split(0)
            for s in range(n):
                g, new = att_group(l, s)
                if new and g + 1 < GROUPS:
                    split(g + 1)
                for k in y_split_at(l, s):
                    eng.wait_ge(y_hi_done, KD * l + Y_ORDER.index(k) + 1)
                    eng.tensor_tensor(h_lo[:, k, 0:w], y_src(k, w), h_hi[:, k, 0:w].bitcast(F32), ALU.subtract)\
                       .then_inc(y_lo_done, 1)

        def attention_dve(eng, l):
            c0, n = ATT_C0[l], n_chunks(l)
            for s in range(n + 5):
                if s < n:
                    kind, i, j, q0, keys = chunk_info(l, s)
                    a, b = keys[0][0], TOK
                    scores = pair[s % 2][:, a:b]
                    eng.wait_ge(a_s, c0 + s + 1)
                    if not own_scores(l, s):
                        first = (BIAS_SLOTS // 2 - 1 - 2 * (q0 // P)) * GRID_W
                        if q0 == 0:
                            eng.wait_ge(tt_loaded[j], 16 * (2 * l + i + 1))
                        eng.wait_ge(a_t, c0 + s - 2)
                        eng.tensor_tensor(prob[:, s % 3, 0:SEQ], pair[s % 2][:, 0:SEQ], na_tt[:, j, first:first + SEQ],
                                          ALU.add).then_inc(a_bias, 1)
                        eng.tensor_copy(prob[:, s % 3, SEQ:TOK], pair[s % 2][:, SEQ:TOK]).then_inc(a_bias, 1)
                        eng.wait_ge(a_bias, bias_steps(l, s) + 2)
                        scores = prob[:, s % 3, :]
                    eng.tensor_reduce(stat[:, s % STATS, 0:1], scores, AX_X, ALU.max, negate=True).then_inc(a_max, 1)
                if 1 <= s <= n:
                    c = s - 1
                    eng.wait_ge(a_exp, c0 + c + 1)
                    if c >= STATS:
                        eng.wait_ge(a_pv, c0 // 2 + (c - STATS) // 2 + 1)
                    eng.reciprocal(stat[:, c % STATS, 2:3], stat[:, c % STATS, 1:2]).then_inc(a_rsum, 1)
                if s >= 6 and s % 2 == 0:
                    b = (s - 6) // 2
                    kind, i, j, q0, _ = chunk_info(l, 2 * b)
                    r, bank = slice(j * 64, j * 64 + 64), (b % 2) * 512
                    y = y_f[r, i if kind == "mla" else 4 + i, q0:q0 + 2 * P]
                    eng.wait_ge(a_copied, c0 // 2 + b + 1)
                    eng.tensor_tensor(y, y, psum2[r, bank + 2 * P:bank + 4 * P], ALU.mult).then_inc(a_out, 1)
                if 2 <= s < n + 2:
                    c = s - 2
                    for a, b in chunk_info(l, c)[4]:
                        if a == 0:
                            eng.wait_ge(a_latent_hi, latent_parts(l, c) + 1)
                        else:
                            eng.wait_ge(a_pth, c0 + c + 1)
                        eng.tensor_tensor(pt_lo[:, a // P:b // P, c % 4, :], pmid[:, a:b].rearrange("p (k q) -> p k q", q=P),
                                          pt_hi[:, a // P:b // P, c % 4, :].bitcast(F32), ALU.subtract)\
                           .then_inc(a_latent_lo if a == 0 else a_ptl, 1)

        blocks = ["ff0", "mix0", "ff1", "ff2", "mix1", "ff3"]
        bias_dmas = 2 * (DEPTH * NA_HEADS + WIN_C - 1)
        o_final = O_END
        block = ctx.enter_context(nc.Block())

        def first_mod_load(eng, n):
            cols = slice(n * MOD_GROUP * P, (n + 1) * MOD_GROUP * P)
            eng.dma_start(mod_first[:, :, cols], w_mod[0].rearrange("(k p) m -> p k m", p=P)[:, :, cols])\
               .then_inc(mod_first_loaded[n], 16)

        @block.sync
        def _(sp):
            sp.dma_start(ident[:, :], k_ident).then_inc(const_loaded, 16)
            sp.wait_ge(vec_zero, 1)
            sp.dma_start(vrows[V_C:V_C + KD, 0, :], c.rearrange("a (k p) -> (a k) p", p=P)).then_inc(vec_loaded, 16)
            sp.dma_start(vrows[V_C + KD:V_C + 2 * KD, 0, :], c_ctx.rearrange("(k p) -> k p", p=P))\
              .then_inc(vec_loaded, 16)
            for l in range(DEPTH):
                for row, v in ((V_BMOD, b_mod), (V_GCQ, g_cq), (V_GCKV, g_ckv), (V_PSC, pool_scale)):
                    src = v[l].rearrange("(k p) -> k p", p=P)
                    sp.dma_start(vrows[row:row + src.shape[0], l, :], src).then_inc(vec_loaded, 16)
                for row, v in ((V_GQ, g_mla_q), (V_GK, g_mla_k)):
                    sp.dma_start(vrows[row:row + 1, l, 0:QK], v[l:l + 1, :]).then_inc(vec_loaded, 16)
                for row, v in ((V_GNQ, g_na_q), (V_GNK, g_na_k)):
                    for a in (0, NA_DIM):
                        sp.dma_start(vrows[row:row + 1, l, a:a + NA_DIM], v[l:l + 1, :]).then_inc(vec_loaded, 16)
            for tc in range(TOK // P):
                src = x[0, tc * P:(tc + 1) * P, :] if tc < SEQ // P else ctx_in[0, tc * P - SEQ:(tc + 1) * P - SEQ, :]
                sp.dma_start(x_rows[:, tc, :], src).then_inc(x_loaded, 16)
            for dst, src in ((cos, k_cos), (sin, k_sin), (perm, k_perm)):
                sp.dma_start(dst[0:QK, :], src).then_inc(table_loaded, 16)
            for n in range(0, START_MOD // MOD_GROUP, 2):
                first_mod_load(sp, n)
            first_loads(sp, blocks[0])
            for b, following in zip(blocks, blocks[1:] + [None]):
                if b[:2] == "ff":
                    ff_sp(sp, int(b[2]), following)
                else:
                    mix_sp(sp, int(b[3]))
                    first_loads(sp, following)
            for tc in range(SEQ // P):
                sp.wait_ge(out_staged, tc + 1)
                sp.dma_start(out[0, tc * P:(tc + 1) * P, :], out_rows[:, tc % 2, :]).then_inc(out_stored[tc % 2], 16)
            for j in range(2):
                sp.wait_ge(out_stored[j], 16 * (SEQ // P // 2))

        N_VEC = 2 + DEPTH * 10

        @block.gpsimd
        def _(pool):
            pool.memset(vrows[:, :, :], 0.0).then_inc(vec_zero, 1)
            pool.memset(ones[:, :], 1.0).then_inc(const_set, 1)
            pool.memset(eps[:, :], EPS).then_inc(const_set, 1)
            pool.memset(blk[:, :], 0.0).then_inc(blk_set, 1)
            pool.wait_ge(blk_set, 1)
            for a in (0, 64):
                pool.memset(blk[a:a + 64, a:a + 64], 1.0).then_inc(blk_set, 1)
            pool.wait_ge(blk_set, 3)
            pool.memset(rot_s[:, :], NEG).then_inc(bias_neg, 1)
            pool.wait_ge(bias_neg, 1)
            pool.wait_ge(mod_done, START_MOD)
            fill = na_bias.rearrange("l h p (a n) -> a (l h) p n", a=2)
            for half in range(2):
                for i in steps(pool, 0, DEPTH * NA_HEADS):
                    pool.dma_start(fill[half, i], rot_s[:, 0:BIAS_SLOTS * GRID_W // 2]).then_inc(bias_filled, 16)
            pool.wait_ge(bias_filled, 16 * 2 * DEPTH * NA_HEADS)
            windows = na_bias.rearrange("l h (a q) (s c) -> a (l h) q s c", a=2, c=GRID_W)
            table = na_rpb.rearrange("l h r c -> (l h) r c")
            heads = DEPTH * NA_HEADS
            for par in range(2):
                slots = slice(1 - par, 1 - par + BIAS_SLOTS)
                for lh in steps(pool, 0, heads):
                    first, n = WIN_C // 2, GRID_W - WIN_C + 1
                    at = windows[par, lh, first, 0, 0]
                    dst = bass.AP(at.tensor, at.offset, [[BIAS_SLOTS * GRID_W + 1, n], [GRID_W, BIAS_SLOTS], [1, WIN_C]])
                    row = table[lh, slots, WIN_C - 1 - WIN_C // 2:2 * WIN_C - 1 - WIN_C // 2]
                    src = bass.AP(row.tensor, row.offset, [[0, n], [RPB_C, BIAS_SLOTS], [1, WIN_C]])
                    pool.dma_start(dst, src).then_inc(bias_stored, 16)
                for cq, start in [(q, 0) for q in range(WIN_C // 2)] + \
                        [(q, GRID_W - WIN_C) for q in range(GRID_W - WIN_C // 2 + 1, GRID_W)]:
                    off = start - cq + WIN_C - 1
                    pool.dma_start(windows[par, :, cq, :, start:start + WIN_C], table[:, slots, off:off + WIN_C])\
                        .then_inc(bias_stored, 16)
            for b in blocks:
                if b[:3] == "mix":
                    mix_pool(pool, int(b[3]))

        @block.tensor
        def _(pe):
            pe.wait_ge(const_loaded, 16)
            pe.wait_ge(vec_loaded, 16 * N_VEC)
            for l in range(DEPTH):
                pe.transpose(pair[l][:, 0:P], vrows[:, l, :], ident[:, :]).then_inc(acc_done, 1)
            pe.wait_ge(x_loaded, 16 * (TOK // P))
            for tc in range(TOK // P):
                o = 2 + tc
                pe.wait_ge(acc_free[o % 2], o // 2)
                for k in range(KD):
                    last = pe.transpose(pair[o % 2][:, k * P:(k + 1) * P], x_rows[:, tc, k * P:(k + 1) * P],
                                        ident[:, :])
                last.then_inc(acc_done, 1)
            pe.wait_ge(cs_ready, 2)
            pe.wait_ge(const_set, 2)
            for u in range(2 * PAIR_0):
                mod_product(pe, u)
            for b in blocks:
                if b[:2] == "ff":
                    inst = int(b[2])
                    x_norm_pe(pe, X_NORM[inst // 2, 2 * (inst % 2)])
                    ff_pe(pe, inst)
                else:
                    if b == "mix0":
                        pe.wait_ge(table_loaded, 48)
                        pe.wait_ge(blk_set, 3)
                    mix_pe(pe, int(b[3]))
            for tc in range(SEQ // P):
                o = o_final + tc
                if tc == 0:
                    for e in (0, 1):
                        pe.wait_ge(acc_free[(o_final + e) % 2], (o_final + e) // 2)
                pe.wait_ge(acc_free[o % 2], o // 2)
                for k in range(KD):
                    last = pe.transpose(pair[o % 2][:, k * P:(k + 1) * P], xT[:, k, tc * P:(tc + 1) * P],
                                        ident[:, :])
                last.then_inc(acc_done, 1)

        @block.scalar
        def _(act):
            for n in range(1, START_MOD // MOD_GROUP, 2):
                first_mod_load(act, n)
            act.wait_ge(acc_free[0], 1)
            for j in range(2):
                act.activation(cs[:, :, j], vecs[:, 0, V_C + j * KD:V_C + (j + 1) * KD], ACT.Silu).then_inc(cs_ready, 1)
            act.wait_ge(const_set, 2)
            for o in range(DEPTH, N_START):
                act.wait_ge(acc_free[o % 2], o // 2 + 1)
            for k in range(KD):
                norm_square(act, X_NORM[0, 0], Nth(k, 0, k))
            for t in range(2):
                split_hi(act, Nth(t, 1, 0), WIDTHS[t], None)
            for b in blocks:
                if b[:2] == "ff":
                    inst = int(b[2])
                    x_norm_act(act, X_NORM[inst // 2, 2 * (inst % 2)])
                    ff_act(act, inst)
                else:
                    mix_act(act, int(b[3]))

        @block.vector
        def _(dve):
            for l in range(DEPTH):
                dve.wait_ge(acc_done, l + 1)
                dve.tensor_copy(vecs[:, l, :], pair[l][:, 0:P]).then_inc(acc_free[l], 1)
            for tc in range(TOK // P):
                o = 2 + tc
                dve.wait_ge(acc_done, o + 1)
                dve.tensor_copy(xT[:, :, tc * P:(tc + 1) * P], pair[o % 2][:, :].rearrange("p (k t) -> p k t", k=KD))\
                   .then_inc(acc_free[o % 2], 1)
            dve.wait_ge(acc_free[0], 1)
            dve.wait_ge(acc_free[1], 1)
            dve.tensor_scalar(vecs_half[:, :, :], vecs[:, :, :], 0.5, None, ALU.mult).then_inc(vec_half_ready, 1)
            dve.wait_ge(vec_half_ready, 1)
            for col, scale in ((V_GQ, MLA_SCALE), (V_GNQ, NA_SCALE)):
                gains = vecs[:, :, col:col + 1].rearrange("p l a -> p (l a)")
                dve.tensor_scalar(gains, gains, scale, None, ALU.mult).then_inc(gain_scaled, 1)
            norm_clear(dve, X_NORM[0, 0])
            for k in range(KD):
                norm_add(dve, X_NORM[0, 0], Nth(k, 0, k))
            for u in range(2 * PAIR_0):
                mod_read(dve, u)
            for t in range(2):
                split_lo(dve, Nth(t, 1, 0), WIDTHS[t])
            for b in blocks:
                if b[:2] == "ff":
                    inst = int(b[2])
                    mod_vectors(dve, inst // 2, 2 * (inst % 2))
                    x_norm_dve(dve, X_NORM[inst // 2, 2 * (inst % 2)])
                    ff_dve(dve, inst)
                else:
                    if b == "mix0":
                        dve.wait_ge(table_loaded, 48)
                        dve.wait_ge(bias_filled, 16 * 2 * DEPTH * NA_HEADS)
                    mix_dve(dve, int(b[3]))
            for tc in range(SEQ // P):
                o = o_final + tc
                dve.wait_ge(acc_done, o + 1)
                if tc >= 2:
                    dve.wait_ge(out_stored[tc % 2], 16 * (tc // 2))
                dve.tensor_copy(out_rows[:, tc % 2, :], pair[o % 2][:, :]).then_inc(out_staged, 1)
                dve.wait_ge(out_staged, tc + 1)
                dve.sem_inc(acc_free[o % 2], 1)


_INS = ["x", "c", "ctx", "c_ctx", "w_mod", "b_mod", "w_ffn_gate", "w_ffn_up", "w_ffn_down", "w_in", "g_cq", "w_q_up",
        "g_ckv", "w_kv_up", "g_mla_q", "g_mla_k", "g_na_q", "g_na_k", "na_rpb", "w_pool", "pool_scale", "w_out"]


def constants():
    ident = np.eye(P, dtype=np.float32)
    a = ROPE // 2
    perm = np.zeros((QK, QK), np.float32)
    cos, sin = np.ones((QK, SEQ), np.float32), np.zeros((QK, SEQ), np.float32)
    t = np.arange(SEQ)
    inv_freq = (10000.0 ** (-np.arange(0, a, 2, dtype=np.float32) / np.float32(a))).astype(np.float32)
    for axis, pos in enumerate((t // GRID_W, t % GRID_W)):
        ang = pos.astype(np.float32)[None, :] * inv_freq[:, None]
        r = NOPE + axis * a
        h = a // 2
        cos[r:r + h], cos[r + h:r + a] = np.cos(ang), np.cos(ang)
        sin[r:r + h], sin[r + h:r + a] = -np.sin(ang), np.sin(ang)
        for i in range(h):
            perm[r + h + i, r + i] = 1.0
            perm[r + i, r + h + i] = 1.0
    inv = np.zeros((P, 2, POOLW), np.float32)
    for g in range(POOL_G):
        w = 2 << g
        for start, n in ((PAD, CTX), (2 * PAD + CTX, SEQ)):
            t = np.arange(n)
            cnt = np.clip(t + w // 2, 0, n) - np.clip(t - w // 2, 0, n)
            inv[(g % 2) * 64:(g % 2) * 64 + 64, g // 2, start:start + n] = (np.float32(1) / cnt.astype(np.float32))
    return dict(k_ident=ident, k_perm=perm, k_cos=cos, k_sin=sin, k_invcnt=inv)



def kernel(**inputs):
    import concourse.bacc as bacc
    from concourse.bass_utils import run_bass_kernel_spmd

    nc = bacc.Bacc("TRN2", target_bir_lowering=False, num_devices=1, dynamic_dma_scratch_size=8192)
    arrays, args = {}, []
    for name, value in [(n, inputs[n]) for n in _INS] + list(constants().items()):
        a = np.ascontiguousarray(value)
        arrays[f"in_{name}"] = a
        args.append(nc.dram_tensor(f"in_{name}", a.shape, mybir.dt.from_np(a.dtype), kind="ExternalInput").ap())
    args.append(nc.dram_tensor("out", (1, SEQ, D_MODEL), F32, kind="ExternalOutput").ap())
    args.append(nc.dram_tensor("na_bias", (DEPTH, NA_HEADS, P, BIAS_SLOTS * GRID_W), F32, kind="Internal").ap())
    program(nc, *args)
    return run_bass_kernel_spmd(nc, [arrays], core_ids=[0]).results[0]["out"]
```
